# Optimizing a Trainium2 kernel written in Bass

```python
import jax
import jax.numpy as jnp
from jax import lax
import numpy as np

D_MODEL = 2048
BATCH = 1
SEQ = 512
DEPTH = 1

D_MIX = D_MODEL
W_POOL = D_MIX // 4
W_CONV = D_MIX // 4
W_DSA = D_MIX // 4
W_NSA = D_MIX - W_POOL - W_CONV - W_DSA
HEAD_DIM = 128
POOL_WINDOWS = (2, 4, 8, 16)
N_POOL_GROUPS = len(POOL_WINDOWS)
POOL_GROUP = W_POOL // N_POOL_GROUPS
CONV_WIDTH = 31
DSA_HEADS = W_DSA // HEAD_DIM
IDX_HEADS = 8
IDX_DIM = 64
DSA_TOPK_MAX = 256
NSA_HEADS = W_NSA // HEAD_DIM
NSA_CMP_BLOCK = 32
NSA_CMP_STRIDE = 16
NSA_SEL_BLOCK = 64
NSA_SEL_TOPK = 16
NSA_WINDOW = 512
Q_BLOCK = 128
D_FF = ((8 * D_MODEL + 3 * 256 - 1) // (3 * 256)) * 256
DN_ALPHA = (2 * DEPTH) ** 0.25
DN_BETA = (8 * DEPTH) ** -0.25
ATTN_SCALE = HEAD_DIM ** -0.5
IDX_SCALE = (IDX_HEADS * IDX_DIM) ** -0.5

IN_SIZES = (
    W_POOL,
    W_CONV, W_CONV,
    W_DSA, HEAD_DIM, HEAD_DIM,
    IDX_HEADS * IDX_DIM, IDX_DIM, IDX_HEADS,
    W_NSA,
    HEAD_DIM, HEAD_DIM,
    HEAD_DIM, HEAD_DIM,
    HEAD_DIM, HEAD_DIM,
    NSA_HEADS * 3,
)
IN_OFFSETS = tuple(int(v) for v in np.cumsum(IN_SIZES)[:-1])
D_IN = int(sum(IN_SIZES))

kernel_name = 'hybrid_pool_conv_dsa_nsa_deepnorm'

def _alibi_slopes():
    n = DSA_HEADS + NSA_HEADS
    s = np.power(2.0, -8.0 * np.arange(1, n + 1) / n).astype(np.float32)
    return jnp.asarray(s[0::2]), jnp.asarray(s[1::2])

def _layernorm(x, g, b, eps=1e-5):
    xf = x.astype(jnp.float32)
    mu = jnp.mean(xf, axis=-1, keepdims=True)
    var = jnp.mean(jnp.square(xf - mu), axis=-1, keepdims=True)
    y = (xf - mu) * lax.rsqrt(var + eps) * g.astype(jnp.float32) + b.astype(jnp.float32)
    return y.astype(x.dtype)

def _masked_softmax(s, mask):
    s = jnp.where(mask, s, -jnp.inf)
    m = jnp.max(s, axis=-1, keepdims=True)
    m = jnp.where(jnp.isfinite(m), m, 0.0)
    e = jnp.where(mask, jnp.exp(s - m), 0.0)
    return e / jnp.maximum(jnp.sum(e, axis=-1, keepdims=True), 1e-30)

def _sweep_blocks(fn, n_tokens):
    n_blocks = n_tokens // Q_BLOCK
    out = lax.map(fn, jnp.arange(n_blocks) * Q_BLOCK)
    out = jnp.moveaxis(out, 0, 1)
    return out.reshape((out.shape[0], n_blocks * Q_BLOCK) + out.shape[3:])

def _pool_mixer(u, w, scale):
    B, S, _ = u.shape
    ug = u.astype(jnp.float32).reshape(B, S, N_POOL_GROUPS, POOL_GROUP)
    cs = jnp.cumsum(ug, axis=1)
    pos = jnp.arange(S)
    outs = []
    for gi, win in enumerate(POOL_WINDOWS):
        c = cs[:, :, gi]
        prev = jnp.pad(c, ((0, 0), (win, 0), (0, 0)))[:, :S]
        cnt = jnp.minimum(pos + 1, win).astype(jnp.float32)[None, :, None]
        outs.append((c - prev) / cnt - ug[:, :, gi])
    d = jnp.stack(outs, axis=2)
    y = jnp.einsum('bsgc,gcd->bsgd', d, w.astype(jnp.float32)).reshape(B, S, W_POOL)
    return (y * scale.astype(jnp.float32)).astype(u.dtype)

def _conv_module(a, gate, conv_w, conv_b, ln_g, ln_b, pw_w, pw_b):
    h = a * jax.nn.sigmoid(gate)
    hp = jnp.pad(h, ((0, 0), (CONV_WIDTH - 1, 0), (0, 0)))
    h = lax.conv_general_dilated(hp, conv_w[:, None, :], window_strides=(1,), padding='VALID',
                                 dimension_numbers=('NWC', 'WIO', 'NWC'),
                                 feature_group_count=W_CONV) + conv_b
    h = jax.nn.silu(_layernorm(h, ln_g, ln_b))
    return h @ pw_w + pw_b

def _dsa_attention(q, k, v, iq, ik, iw, slopes):
    B, S, _ = q.shape
    q = q.reshape(B, S, DSA_HEADS, HEAD_DIM)
    iq = iq.reshape(B, S, IDX_HEADS, IDX_DIM)
    iw = iw.astype(jnp.float32) * IDX_SCALE
    topk = min(DSA_TOPK_MAX, S // 4)
    s_pos = jnp.arange(S)
    b_ix = jnp.arange(B)[:, None, None]

    def block(t0):
        t_pos = t0 + jnp.arange(Q_BLOCK)
        qb = lax.dynamic_slice_in_dim(q, t0, Q_BLOCK, axis=1)
        iqb = lax.dynamic_slice_in_dim(iq, t0, Q_BLOCK, axis=1)
        iwb = lax.dynamic_slice_in_dim(iw, t0, Q_BLOCK, axis=1)
        logits = jnp.einsum('bthd,bsd->bths', iqb, ik).astype(jnp.float32)
        score = jnp.einsum('bths,bth->bts', jax.nn.relu(logits), iwb)
        score = jnp.where(s_pos[None, None, :] <= t_pos[None, :, None], score, -jnp.inf)
        _, idx = lax.top_k(score, topk)
        kg = k[b_ix, idx]
        vg = v[b_ix, idx]
        dist = (t_pos[None, :, None] - idx).astype(jnp.float32)
        a = jnp.einsum('bthd,btjd->bhtj', qb, kg).astype(jnp.float32) * ATTN_SCALE
        a = a - slopes[None, :, None, None] * dist[:, None]
        p = _masked_softmax(a, (dist >= 0)[:, None])
        return jnp.einsum('bhtj,btjd->bthd', p.astype(vg.dtype), vg)

    return _sweep_blocks(block, S).reshape(B, S, W_DSA)

def _compress_blocks(raw, blk_idx, pos, w1, w2):
    B = raw.shape[0]
    blocks = raw[:, blk_idx] + pos
    h = jax.nn.gelu(blocks.reshape(B, blk_idx.shape[0], -1) @ w1)
    return h @ w2

def _nsa_attention(q, ck, cv, sk, sv, wk, wv, g, pos_k, pos_v, k_w1, k_w2, v_w1, v_w2, slopes):
    B, S, _ = q.shape
    q = q.reshape(B, S, NSA_HEADS, HEAD_DIM)
    t_all = jnp.arange(S)
    n_cmp = (S - NSA_CMP_BLOCK) // NSA_CMP_STRIDE + 1
    starts = np.arange(n_cmp) * NSA_CMP_STRIDE
    blk_idx = starts[:, None] + np.arange(NSA_CMP_BLOCK)[None, :]
    ends = blk_idx[:, -1]
    k_cmp = _compress_blocks(ck, blk_idx, pos_k, k_w1, k_w2)
    v_cmp = _compress_blocks(cv, blk_idx, pos_v, v_w1, v_w2)
    cd = (t_all[:, None] - ends[None, :]).astype(jnp.float32)
    a = jnp.einsum('bthd,bcd->bhtc', q, k_cmp).astype(jnp.float32) * ATTN_SCALE
    a = a - slopes[:, None, None] * cd
    p_cmp = _masked_softmax(a, cd >= 0)
    o_cmp = jnp.einsum('bhtc,bcd->bthd', p_cmp.astype(v_cmp.dtype), v_cmp)
    n_sel = S // NSA_SEL_BLOCK
    sel_start = np.arange(n_sel) * NSA_SEL_BLOCK
    overlap = ((starts[:, None] < sel_start[None, :] + NSA_SEL_BLOCK)
               & (ends[:, None] >= sel_start[None, :])).astype(np.float32)
    imp = jnp.einsum('bhtc,cn->btn', p_cmp, overlap)
    t_blk = t_all // NSA_SEL_BLOCK
    j = jnp.arange(n_sel)
    forced = (j[None, :] == 0) | (j[None, :] == t_blk[:, None]) | (j[None, :] == t_blk[:, None] - 1)
    imp = jnp.where(forced[None], jnp.inf, imp)
    imp = jnp.where((j[None, :] <= t_blk[:, None])[None], imp, -jnp.inf)
    n_top = min(NSA_SEL_TOPK, n_sel)
    _, sel_idx = lax.top_k(imp, n_top)
    ks_b = sk.reshape(B, n_sel, NSA_SEL_BLOCK, HEAD_DIM)
    vs_b = sv.reshape(B, n_sel, NSA_SEL_BLOCK, HEAD_DIM)
    wk_p = jnp.pad(wk, ((0, 0), (NSA_WINDOW, 0), (0, 0)))
    wv_p = jnp.pad(wv, ((0, 0), (NSA_WINDOW, 0), (0, 0)))
    b_ix = jnp.arange(B)[:, None, None]
    in_blk = jnp.arange(NSA_SEL_BLOCK)
    win_off = jnp.arange(Q_BLOCK + NSA_WINDOW) - NSA_WINDOW

    def block(t0):
        t_pos = t0 + jnp.arange(Q_BLOCK)
        qb = lax.dynamic_slice_in_dim(q, t0, Q_BLOCK, axis=1)
        idx = lax.dynamic_slice_in_dim(sel_idx, t0, Q_BLOCK, axis=1)
        kg = ks_b[b_ix, idx].reshape(B, Q_BLOCK, n_top * NSA_SEL_BLOCK, HEAD_DIM)
        vg = vs_b[b_ix, idx].reshape(B, Q_BLOCK, n_top * NSA_SEL_BLOCK, HEAD_DIM)
        kpos = (idx[..., None] * NSA_SEL_BLOCK + in_blk).reshape(B, Q_BLOCK, -1)
        sd = (t_pos[None, :, None] - kpos).astype(jnp.float32)
        a = jnp.einsum('bthd,btjd->bhtj', qb, kg).astype(jnp.float32) * ATTN_SCALE
        a = a - slopes[None, :, None, None] * sd[:, None]
        o_slc = jnp.einsum('bhtj,btjd->bthd', _masked_softmax(a, (sd >= 0)[:, None]).astype(vg.dtype), vg)
        kw_b = lax.dynamic_slice_in_dim(wk_p, t0, Q_BLOCK + NSA_WINDOW, axis=1)
        vw_b = lax.dynamic_slice_in_dim(wv_p, t0, Q_BLOCK + NSA_WINDOW, axis=1)
        wpos = t0 + win_off
        wd = (t_pos[:, None] - wpos[None, :]).astype(jnp.float32)
        wmask = (wd >= 0) & (wd < NSA_WINDOW) & (wpos[None, :] >= 0)
        a = jnp.einsum('bthd,bkd->bhtk', qb, kw_b).astype(jnp.float32) * ATTN_SCALE
        a = a - slopes[:, None, None] * wd
        o_win = jnp.einsum('bhtk,bkd->bthd', _masked_softmax(a, wmask).astype(vw_b.dtype), vw_b)
        return jnp.stack([o_slc, o_win], axis=2)

    o_sw = _sweep_blocks(block, S)
    gates = jax.nn.sigmoid(g.reshape(B, S, NSA_HEADS, 3))
    o = gates[..., 0:1] * o_cmp + gates[..., 1:2] * o_sw[:, :, 0] + gates[..., 2:3] * o_sw[:, :, 1]
    return o.reshape(B, S, W_NSA)

def setup_inputs(seed: int = 0) -> dict:
    key = jax.random.key(seed)
    ks = jax.random.split(key, 24)
    L = DEPTH

    def nrm(k, shape, scale):
        return jax.random.normal(k, shape, jnp.float32) * scale

    return {
        'x': nrm(ks[0], (BATCH, SEQ, D_MODEL), 1.0),
        'w_in': nrm(ks[1], (L, D_MODEL, D_IN), D_MODEL ** -0.5),
        'w_out': nrm(ks[2], (L, D_MIX, D_MODEL), D_MIX ** -0.5 * DN_BETA),
        'pool_w': nrm(ks[3], (L, N_POOL_GROUPS, POOL_GROUP, POOL_GROUP), POOL_GROUP ** -0.5),
        'pool_scale': 1.0 + nrm(ks[4], (L, W_POOL), 0.1),
        'conv_w': nrm(ks[5], (L, CONV_WIDTH, W_CONV), CONV_WIDTH ** -0.5),
        'conv_b': nrm(ks[6], (L, W_CONV), 0.02),
        'conv_ln_g': 1.0 + nrm(ks[7], (L, W_CONV), 0.05),
        'conv_ln_b': nrm(ks[8], (L, W_CONV), 0.02),
        'conv_pw_w': nrm(ks[9], (L, W_CONV, W_CONV), W_CONV ** -0.5),
        'conv_pw_b': nrm(ks[10], (L, W_CONV), 0.02),
        'cmp_pos_k': nrm(ks[11], (L, NSA_CMP_BLOCK, HEAD_DIM), 0.1),
        'cmp_pos_v': nrm(ks[12], (L, NSA_CMP_BLOCK, HEAD_DIM), 0.1),
        'cmp_k_w1': nrm(ks[13], (L, NSA_CMP_BLOCK * HEAD_DIM, HEAD_DIM), (NSA_CMP_BLOCK * HEAD_DIM) ** -0.5),
        'cmp_k_w2': nrm(ks[14], (L, HEAD_DIM, HEAD_DIM), HEAD_DIM ** -0.5),
        'cmp_v_w1': nrm(ks[15], (L, NSA_CMP_BLOCK * HEAD_DIM, HEAD_DIM), (NSA_CMP_BLOCK * HEAD_DIM) ** -0.5),
        'cmp_v_w2': nrm(ks[16], (L, HEAD_DIM, HEAD_DIM), HEAD_DIM ** -0.5),
        'ln1_g': 1.0 + nrm(ks[17], (L, D_MODEL), 0.05),
        'ln1_b': nrm(ks[18], (L, D_MODEL), 0.02),
        'ln2_g': 1.0 + nrm(ks[19], (L, D_MODEL), 0.05),
        'ln2_b': nrm(ks[20], (L, D_MODEL), 0.02),
        'w_gate_up': nrm(ks[21], (L, D_MODEL, 2 * D_FF), D_MODEL ** -0.5),
        'w_down': nrm(ks[22], (L, D_FF, D_MODEL), D_FF ** -0.5 * DN_BETA),
    }

def reference(x, w_in, w_out, pool_w, pool_scale, conv_w, conv_b, conv_ln_g, conv_ln_b,
              conv_pw_w, conv_pw_b, cmp_pos_k, cmp_pos_v, cmp_k_w1, cmp_k_w2, cmp_v_w1, cmp_v_w2,
              ln1_g, ln1_b, ln2_g, ln2_b, w_gate_up, w_down):
    slopes_dsa, slopes_nsa = _alibi_slopes()
    for l in range(DEPTH):
        (u_pool, c_a, c_g, d_q, d_k, d_v, i_q, i_k, i_w,
         n_q, n_ck, n_cv, n_sk, n_sv, n_wk, n_wv, n_g) = jnp.split(x @ w_in[l], IN_OFFSETS, axis=-1)
        y_pool = _pool_mixer(u_pool, pool_w[l], pool_scale[l])
        y_conv = _conv_module(c_a, c_g, conv_w[l], conv_b[l], conv_ln_g[l], conv_ln_b[l],
                              conv_pw_w[l], conv_pw_b[l])
        y_dsa = _dsa_attention(d_q, d_k, d_v, i_q, i_k, i_w, slopes_dsa)
        y_nsa = _nsa_attention(n_q, n_ck, n_cv, n_sk, n_sv, n_wk, n_wv, n_g,
                               cmp_pos_k[l], cmp_pos_v[l], cmp_k_w1[l], cmp_k_w2[l],
                               cmp_v_w1[l], cmp_v_w2[l], slopes_nsa)
        mix = jnp.concatenate([y_pool, y_conv, y_dsa, y_nsa], axis=-1)
        x = _layernorm(DN_ALPHA * x + mix @ w_out[l], ln1_g[l], ln1_b[l])
        gate, up = jnp.split(x @ w_gate_up[l], 2, axis=-1)
        x = _layernorm(DN_ALPHA * x + (jax.nn.silu(gate) * up) @ w_down[l], ln2_g[l], ln2_b[l])
    return x


_drawn_inputs = setup_inputs


def setup_inputs(seed=0):
    import zlib

    import numpy as np

    out = dict(_drawn_inputs(seed))
    spreads = {}
    factors = {'conv_b': 8.0,
     'conv_ln_g': 6.256,
     'conv_ln_b': 24.303,
     'conv_pw_b': 8.0,
     'cmp_pos_k': 8.0,
     'cmp_pos_v': 7.445,
     'cmp_k_w1': 4.116,
     'cmp_k_w2': 4.119,
     'ln1_b': 2.731,
     'ln2_b': 2.875,
     'pool_scale': 3.813}
    for name, (base, spread) in spreads.items():
        noise = np.random.default_rng([zlib.crc32(name.encode()), seed]).standard_normal(out[name].shape)
        drawn = base * np.exp(spread * noise) if base else spread * noise
        out[name] = jnp.asarray(drawn.astype(out[name].dtype))
    for name, factor in factors.items():
        out[name] = (out[name] * factor).astype(out[name].dtype)
    return out
```

```python
from contextlib import ExitStack

import numpy as np

import concourse.bass as bass
from concourse import mybir

F32 = mybir.dt.float32
F32R = mybir.dt.float32r
ALU = mybir.AluOpType
ACT = mybir.ActivationFunctionType
AX = mybir.AxisListType

P = 128
SEQ = 512
D_MODEL = 2048
KT = D_MODEL // P
TT = SEQ // P
D_FF = 5632
HEADS = 4
IDX_HEADS, IDX_DIM = 8, 64
TOPK = min(256, SEQ // 4)
CONV_WIDTH = 31
CMP_BLOCK, CMP_STRIDE = 32, 16
N_CMP = (SEQ - CMP_BLOCK) // CMP_STRIDE + 1
ALPHA = 2.0 ** 0.25
LN_EPS = 1e-5
ATTN_SCALE = float(P) ** -0.5
IDX_SCALE = float(IDX_HEADS * IDX_DIM) ** -0.5
SLOPES_DSA = [2.0 ** -(2 * h + 1) for h in range(HEADS)]
SLOPES_NSA = [2.0 ** -(2 * h + 2) for h in range(HEADS)]
MASKED = -1e30
PICKED = -3e38

SLAB = 2048
C_POOL, C_A, C_G, C_DQ, C_IQ, C_IK, C_NQ, C_NG = 0, 512, 1024, 1536, 2304, 2816, 2888, 4168
W_IKW, W_NG = IDX_DIM + IDX_HEADS, 3 * HEADS

N_IDX, N_IKWG, N_CONV, N_POOL, N_QKV = 0, 4, 5, 13, 17
N_IN = 33
N_OUT = 16
FF_CHUNKS = D_FF // P
FF_GROUPS = FF_CHUNKS // 4

S_IQ, S_IKWG, S_CONV, S_SPARE, S_POOL, S_DQ, S_DK, S_DV, S_NQ = 0, 4, 5, 9, 10, 14, 18, 19, 20
S_CK, S_CV, S_SK, S_SV, S_WK, S_WV = 24, 25, 26, 27, 28, 29
N_SLOTS = 30
CONV_OUT = [S_SPARE, S_CONV, S_CONV + 1, S_CONV + 2]
VEC_ROWS = CONV_WIDTH + 5
V_CB, V_LG, V_LB, V_PB, V_PS = range(CONV_WIDTH, VEC_ROWS)

UNITS = [(S_DQ + h, S_DK, S_DV, SLOPES_DSA[h]) for h in range(HEADS)]
for _h in range(HEADS):
    UNITS += [(S_NQ + _h, S_SK, S_SV, SLOPES_NSA[_h]), (S_NQ + _h, S_WK, S_WV, SLOPES_NSA[_h])]
N_UNITS = len(UNITS)
N_TILES = N_UNITS * TT
SLAB_OF = {S_POOL + g: N_POOL + g for g in range(4)}
SLAB_OF.update({S_DQ + s: N_QKV + s for s in range(16)})
PW_BANKS = [2, 3, 6, 7]
X1_BANKS = [0, 1, 2, 3, 6, 7]
SEL_OFF = [None, 0, 2 * P, 5 * P]
MIX_ORDER = [(4 + c, CONV_OUT[c]) for c in range(4)] + [(c, S_POOL + c) for c in range(4)] + \
            [(8 + c, S_DQ + c) for c in range(4)] + [(12 + c, S_NQ + c) for c in range(4)]


def build(nc, x, w_in, w_out, pool_w, pool_scale, conv_w, conv_b, conv_ln_g, conv_ln_b, conv_pw_w,
          conv_pw_b, cmp_pos_k, cmp_pos_v, cmp_k_w1, cmp_k_w2, cmp_v_w1, cmp_v_w2, ln1_g, ln1_b,
          ln2_g, ln2_b, w_gate_up, w_down, out):
    with ExitStack() as ctx:
        def sb(name, shape, dt=F32, where=ctx):
            return where.enter_context(nc.sbuf_tensor(name, shape, dt))

        def sem(name):
            return ctx.enter_context(nc.semaphore(name))

        psum = ctx.enter_context(nc.psum_tensor("psum", [P, 8, SEQ], F32))

        act_hi = sb("act_hi", [P, KT, SEQ], F32R)
        act_lo = sb("act_lo", [P, KT, SEQ], F32R)
        w_hi = sb("w_hi", [P, 2, SLAB], F32R)
        w_lo = sb("w_lo", [P, 2, SLAB], F32R)
        raw = sb("raw", [P, 2, SLAB])
        stats = sb("stats", [P, TT, 4, 6])
        moments = sb("moments", [P, TT, 2])
        rstd = sb("rstd", [P, TT])
        shift = sb("shift", [P, TT])
        std = sb("std", [P, TT])
        ident = sb("ident", [P, P])
        eps = sb("eps", [P, 1])

        mixing = ExitStack()
        with mixing:
            def sbm(name, shape):
                return sb(name, shape, F32, mixing)

            proj = sbm("proj", [P, N_SLOTS, SEQ])
            dist = sbm("dist", [P, SEQ])
            sel = sbm("sel", [P, 9 * P])
            pt = sbm("pt", [P, 2, 13 * P])
            blk = sbm("blk", [P, 2, CMP_BLOCK * CMP_BLOCK])
            cmp_p = sbm("cmp_p", [P, 16 * N_CMP])
            vecs = sbm("vecs", [P, 4, VEC_ROWS])
            pos = sbm("pos", [P, 2 * CMP_BLOCK])
            iwg = sbm("iwg", [P, TT, W_IKW + W_NG])
            cmp_dist = sbm("cmp_dist", [P, TT * N_CMP])
            cmp_kT = sbm("cmp_kT", [P, N_CMP])
            cmp_h = sbm("cmp_h", [P, 2, N_CMP])
            cmp_v = sbm("cmp_v", [N_CMP, P])
            w2 = sbm("w2", [P, 2, P])
            inv_count = sbm("inv_count", [P, 16])
            top8 = sbm("top8", [P, 8])
            row_max = sbm("row_max", [P, 4])
            neg_max = sbm("neg_max", [P, 4])
            row_sum = sbm("row_sum", [P, 4])
            row_inv = sbm("row_inv", [P, 4])
            cmp_m = sbm("cmp_m", [P, 16])
            cmp_r = sbm("cmp_r", [P, 16])
        feed = ExitStack()
        feed_ctx = ctx.enter_context(feed)
        acc = sb("acc", [P, TT, D_MODEL], F32, feed)
        ln_g = sb("ln_g", [P, D_MODEL], F32, feed)
        ln_b = sb("ln_b", [P, D_MODEL], F32, feed)
        h_hi = sb("h_hi", [P, 4, SEQ], F32R, feed)
        h_lo = sb("h_lo", [P, 4, SEQ], F32R, feed)
        silu_g = sb("silu_g", [P, 2, SEQ], F32, feed)
        hid = sb("hid", [P, 2, SEQ], F32, feed)

        x_nat = proj[:, 0:16, :].rearrange("p (i k) s -> p i (k s)", i=TT)
        vec_nat = sel[0:VEC_ROWS, 0:SEQ]
        pos_nat = sel[0:2 * CMP_BLOCK, SEQ:SEQ + P]
        later = cmp_p[:, 0:P]
        ones = cmp_p[:, P:2 * P]
        ik_high = blk[64:128, 0, 0:SEQ]
        relu_ring = pt[:, :, :].rearrange("p a b -> p (a b)")[:, 0:6 * SEQ].rearrange("p (r s) -> p r s", r=6)
        squares = relu_ring
        rstd_conv = proj[:, S_CONV + 3, :]
        tmp_a, tmp_b = blk[:, 0, 0:SEQ], blk[:, 0, SEQ:2 * SEQ]
        cmp_pT = blk[0:N_CMP, :, :].rearrange("c a b -> c (a b)").rearrange("c (h s) -> c h s", h=HEADS)
        t_ring = proj[:, S_IQ:S_IQ + 4, :]

        raw_loaded = [sem(f"raw_loaded{i}") for i in range(2)]
        aux_used = sem("aux_used")
        split_begun = sem("split_begun")
        hi_done = sem("hi_done")
        split_done = sem("split_done")
        slab_done = sem("slab_done")
        x_loaded = [sem(f"x_loaded{i}") for i in range(TT)]
        small_loaded = sem("small_loaded")
        const_ready = sem("const_ready")
        ident_ready = sem("ident_ready")
        xt_done = sem("xt_done")
        xt_hi = sem("xt_hi")
        xt_lo = sem("xt_lo")
        bank_free = [sem(f"bank_free{i}") for i in range(2)]
        vec_t = sem("vec_t")
        vec_ready = sem("vec_ready")
        iwg_t = sem("iwg_t")
        iwg_ready = sem("iwg_ready")
        gates_ready = sem("gates_ready")
        ik_dup = sem("ik_dup")
        logit_done = sem("logit_done")
        relu_done = sem("relu_done")
        relu_used = sem("relu_used")
        sig_ready = sem("sig_ready")
        dve = sem("dve")
        conv_out = sem("conv_out")
        mean_done = sem("mean_done")
        centred = sem("centred")
        squared = sem("squared")
        var_done = sem("var_done")
        std_ready = sem("std_ready")
        normed = sem("normed")
        silu_ready = sem("silu_ready")
        pw_done = sem("pw_done")
        pool_in = sem("pool_in")
        pool_done = sem("pool_done")
        v_t = sem("v_t")
        v_nat = sem("v_nat")
        blk_ready = sem("blk_ready")
        cmp1_done = sem("cmp1_done")
        gelu_ready = sem("gelu_ready")
        cmp2_done = sem("cmp2_done")
        cmp_kv = sem("cmp_kv")
        cmp_logit = sem("cmp_logit")
        cmp_shift = sem("cmp_shift")
        cmp_exp = sem("cmp_exp")
        cmp_prob = sem("cmp_prob")
        cmp_t = sem("cmp_t")
        cmp_t_ready = sem("cmp_t_ready")
        qk_done = sem("qk_done")
        scored = sem("scored")
        max_ready = sem("max_ready")
        exp_done = sem("exp_done")
        prob_ready = sem("prob_ready")
        tr_done = sem("tr_done")
        pt_ready = sem("pt_ready")
        pv_done = sem("pv_done")
        mix_ready = sem("mix_ready")
        mix_hi = sem("mix_hi")
        mix_split = sem("mix_split")
        resid_loaded = sem("resid_loaded")
        ln_loaded = sem("ln_loaded")
        tile_done = sem("tile_done")
        tile_added = sem("tile_added")
        var_ready = sem("var_ready")
        std_done = sem("std_done")
        rstd_ready = sem("rstd_ready")
        xn_ready = sem("xn_ready")
        gained = sem("gained")
        x1_ready = [sem(f"x1_ready{i}") for i in range(TT)]
        x1_t = sem("x1_t")
        x1_hi = sem("x1_hi")
        x1_lo = sem("x1_lo")
        scaled = sem("scaled")
        silu_done = sem("silu_done")
        hid_ready = sem("hid_ready")
        hid_hi = sem("hid_hi")
        hid_lo = sem("hid_lo")
        y_ready = [sem(f"y_ready{i}") for i in range(TT)]
        stored = sem("stored")

        win = w_in[0].rearrange("(k p) n -> p k n", p=P)
        wout = w_out[0].rearrange("(k p) n -> p k n", p=P)
        wgu = w_gate_up[0].rearrange("(k p) n -> p k n", p=P)
        wdown = w_down[0].rearrange("(k p) n -> p k n", p=P)
        x_dram = x[0].rearrange("(i p) d -> p i d", p=P)
        out_dram = out[0].rearrange("(i p) d -> p i d", p=P)

        N_AUX = 6
        FF0 = N_IN + N_OUT
        TILES0 = 8

        def copied(eng, n):
            eng.wait_ge(bank_free[n % 2], n // 2 + 1)

        def tile_ready(eng, group, slab, i):
            if i < TT - 1:
                eng.wait_ge(tile_done, group * (TT - 1) + (i + 1))
            else:
                eng.wait_ge(slab_done, slab + 1)

        def aux_slot(a):
            return (N_IN + a) % 2

        block = ctx.enter_context(nc.Block())

        @block.sync
        def _(sp):
            def load(slot, src, shape_k):
                dst = raw[:, slot, 0:shape_k * (SLAB // shape_k)].rearrange("p (k n) -> p k n", k=shape_k)
                nc.sync.dma_start(dst, src).then_inc(raw_loaded[slot], 16)

            def x_tile(i):
                nc.sync.dma_start(x_nat[:, i, :], x_dram[:, i, :]).then_inc(x_loaded[i], 16)

            x_tile(0)
            load(0, win[:, :, C_IQ:C_IQ + P], KT)
            x_tile(1)
            x_tile(2)
            x_tile(3)
            load(1, win[:, :, C_IQ + P:C_IQ + 2 * P], KT)
            rows = ((conv_w[0], 0, CONV_WIDTH), (conv_b, V_CB, 1), (conv_ln_g, V_LG, 1),
                    (conv_ln_b, V_LB, 1), (conv_pw_b, V_PB, 1), (pool_scale, V_PS, 1))
            for src, at, n in rows:
                nc.sync.dma_start(sel[at:at + n, 0:SEQ], src).then_inc(small_loaded, 16)
            nc.sync.dma_start(sel[0:CMP_BLOCK, SEQ:SEQ + P], cmp_pos_k[0]).then_inc(small_loaded, 16)
            nc.sync.dma_start(sel[CMP_BLOCK:2 * CMP_BLOCK, SEQ:SEQ + P], cmp_pos_v[0]).then_inc(small_loaded, 16)
            nc.sync.dma_start(w2[:, 0, :], cmp_k_w2[0]).then_inc(small_loaded, 16)
            nc.sync.dma_start(w2[:, 1, :], cmp_v_w2[0]).then_inc(small_loaded, 16)

            for n in (2, 3):
                sp.wait_ge(split_done, n - 1)
                load(n % 2, win[:, :, C_IQ + n * P:C_IQ + (n + 1) * P], KT)
            sp.wait_ge(split_done, N_IKWG - 1)
            ikwg = raw[:, 0, 0:KT * (W_IKW + W_NG)].rearrange("p (k n) -> p k n", k=KT)
            nc.sync.dma_start(ikwg[:, :, 0:W_IKW], win[:, :, C_IK:C_IK + W_IKW]).then_inc(raw_loaded[0], 16)
            nc.sync.dma_start(ikwg[:, :, W_IKW:], win[:, :, C_NG:C_NG + W_NG]).then_inc(raw_loaded[0], 16)

            with sp.Fori(0, 4) as c:
                sp.wait_ge(split_done, 2 * c + (N_CONV - 1))
                load(1, win[:, :, bass.ds(c * P + C_G, P)], KT)
                sp.wait_ge(split_done, 2 * c + N_CONV)
                load(0, win[:, :, bass.ds(c * P + C_A, P)], KT)

            def pairs(count, first, column):
                with sp.Fori(0, count) as c:
                    sp.wait_ge(split_done, 2 * c + (first - 1))
                    load(1, win[:, :, bass.ds(c * (2 * P) + column, P)], KT)
                    sp.wait_ge(split_done, 2 * c + first)
                    load(0, win[:, :, bass.ds(c * (2 * P) + (column + P), P)], KT)

            pairs(2, N_POOL, C_POOL)
            pairs(3, N_QKV, C_DQ)
            pairs(5, N_QKV + 6, C_NQ)

            for a in range(N_AUX):
                if a < 2:
                    sp.wait_ge(split_done, N_IN - 1 + a)
                else:
                    sp.wait_ge(aux_used, a - 1)
                slot = (N_IN + a) % 2
                if a < 4:
                    w1 = (cmp_k_w1, cmp_v_w1)[a // 2][0].rearrange("(l d) h -> d l h", d=P)
                    load(slot, w1[:, 16 * (a % 2):16 * (a % 2) + 16, :], 16)
                elif a == 4:
                    load(slot, conv_pw_w[0].rearrange("(k p) n -> p k n", p=P), 4)
                else:
                    nc.sync.dma_start(raw[:, slot, 0:4 * P].rearrange("p (g d) -> p g d", g=4),
                                      pool_w[0].rearrange("g c d -> c g d")).then_inc(raw_loaded[slot], 16)

            for m in range(2):
                sp.wait_ge((pw_done, pool_done)[m], 4)
                load((m + 1) % 2, wout[:, 4 * m:4 * m + 4, 0:SEQ], 4)
            for m in range(2, 4):
                sp.wait_ge(split_done, N_IN + m - 1)
                load((m + 1) % 2, wout[:, 4 * m:4 * m + 4, 0:SEQ], 4)
            sp.wait_ge(mix_split, 16)
            nc.sync.dma_start(acc[:, :, :], x_dram).then_inc(resid_loaded, 16)
            nc.sync.dma_start(ln_g[:, :], ln1_g.to_broadcast([P, D_MODEL])).then_inc(ln_loaded, 16)
            nc.sync.dma_start(ln_b[:, :], ln1_b.to_broadcast([P, D_MODEL])).then_inc(ln_loaded, 16)
            with sp.Fori(1, 4) as n:
                for kq in range(4):
                    sp.wait_ge(split_done, 4 * n + (N_IN + kq - 1))
                    load((kq + 1) % 2, wout[:, 4 * kq:4 * kq + 4, bass.ds(n * SEQ, SEQ)], 4)

            def gate_up(first, chunk):
                for u in range(2):
                    sp.wait_ge(split_done, first + (u - 1))
                    load((u + 1) % 2, wgu[:, :, bass.ds(chunk * P + u * D_FF, P)], KT)

            def down(first, group):
                for n in range(4):
                    sp.wait_ge(split_done, first + (n - 1))
                    load((n + 1) % 2, wdown[:, bass.ds(group * 4, 4), n * SEQ:(n + 1) * SEQ], 4)

            gate_up(FF0, 0)
            gate_up(FF0 + 2, 1)
            for i in range(TT):
                sp.wait_ge(x1_ready[i], 1)
            nc.sync.dma_start(ln_g[:, :], ln2_g.to_broadcast([P, D_MODEL])).then_inc(ln_loaded, 16)
            nc.sync.dma_start(ln_b[:, :], ln2_b.to_broadcast([P, D_MODEL])).then_inc(ln_loaded, 16)
            with sp.Fori(0, FF_GROUPS - 1) as g:
                gate_up(g * 12 + (FF0 + 4), g * 4 + 2)
                gate_up(g * 12 + (FF0 + 6), g * 4 + 3)
                gate_up(g * 12 + (FF0 + 8), g * 4 + 4)
                down(g * 12 + (FF0 + 10), g)
                gate_up(g * 12 + (FF0 + 14), g * 4 + 5)
            last = FF0 + 12 * (FF_GROUPS - 1)
            gate_up(last + 4, FF_CHUNKS - 2)
            gate_up(last + 6, FF_CHUNKS - 1)
            down(last + 8, FF_GROUPS - 1)

            for i in range(TT):
                sp.wait_ge(y_ready[i], 1)
                nc.sync.dma_start(out_dram[:, i, :], acc[:, i, :]).then_inc(stored, 16)
            sp.wait_ge(stored, 16 * TT)

        @block.gpsimd
        def _(pool):
            nc.gpsimd.memset(ident[:, :], 0.0).then_inc(const_ready, 1)
            pool.wait_ge(const_ready, 1)
            nc.gpsimd.affine_select(out=ident[:, :], in_=ident[:, :], compare_op=ALU.not_equal, fill=1.0,
                                    base=0, pattern=[[-1, P]], channel_multiplier=1).then_inc(ident_ready, 1)

            def split(slot, loads, n, words=SLAB):
                pool.wait_ge(raw_loaded[slot], loads)
                if not (isinstance(n, int) and n < 2):
                    pool.wait_ge(slab_done, n - 1)
                nc.gpsimd.sem_inc(split_begun, 1)
                nc.gpsimd.tensor_scalar(w_hi[:, slot, 0:words], raw[:, slot, 0:words], 0.0, None,
                                        ALU.bypass).then_inc(hi_done, 1)
                pool.wait_ge(hi_done, n + 1)
                nc.gpsimd.tensor_tensor(w_lo[:, slot, 0:words], raw[:, slot, 0:words],
                                        w_hi[:, slot, 0:words].bitcast(F32), ALU.subtract).then_inc(split_done, 1)

            split(0, 16, 0)
            nc.gpsimd.iota(dist[:, :], pattern=[[1, SEQ]], base=-(SEQ - P), channel_multiplier=-1,
                           allow_small_or_imprecise_dtypes=True).then_inc(const_ready, 1)
            pool.wait_ge(const_ready, 2)
            nc.gpsimd.affine_select(out=dist[:, :], in_=dist[:, :], compare_op=ALU.is_ge, fill=MASKED,
                                    base=SEQ - P, pattern=[[-1, SEQ]], channel_multiplier=1).then_inc(const_ready, 1)
            nc.gpsimd.iota(cmp_dist[:, :], pattern=[[-P, TT], [CMP_STRIDE, N_CMP]], base=CMP_BLOCK - 1,
                           channel_multiplier=-1, allow_small_or_imprecise_dtypes=True).then_inc(const_ready, 1)
            pool.wait_ge(const_ready, 4)
            nc.gpsimd.affine_select(out=cmp_dist[:, :], in_=cmp_dist[:, :], compare_op=ALU.is_ge, fill=MASKED,
                                    base=-(CMP_BLOCK - 1), pattern=[[P, TT], [-CMP_STRIDE, N_CMP]],
                                    channel_multiplier=1).then_inc(const_ready, 1)
            nc.gpsimd.memset(later[:, :], 0.0).then_inc(const_ready, 1)
            nc.gpsimd.memset(ones[:, :], 1.0 / SEQ).then_inc(const_ready, 1)
            nc.gpsimd.memset(eps[:, :], LN_EPS).then_inc(const_ready, 1)
            nc.gpsimd.iota(inv_count[:, :], pattern=[[1, 16]], base=1, channel_multiplier=0,
                           allow_small_or_imprecise_dtypes=True).then_inc(const_ready, 1)
            pool.wait_ge(const_ready, 6)
            nc.gpsimd.affine_select(out=later[:, :], in_=later[:, :], compare_op=ALU.is_ge, fill=MASKED,
                                    base=0, pattern=[[-1, P]], channel_multiplier=1).then_inc(const_ready, 1)

            split(1, 16, 1)
            split(0, 32, 2)
            split(1, 32, 3)
            split(0, 64, N_IKWG, KT * (W_IKW + W_NG))
            with pool.Fori(0, (N_IN - N_CONV) // 2) as c:
                split(1, c * 16 + 48, 2 * c + N_CONV)
                split(0, c * 16 + 80, 2 * c + (N_CONV + 1))

            def split_mix(first, end):
                for m in range(first, end):
                    chunk, slot = MIX_ORDER[m]
                    pool.wait_ge(mix_ready, m + 1)
                    nc.gpsimd.tensor_scalar(act_hi[:, chunk, :], proj[:, slot, :], 0.0, None,
                                            ALU.bypass).then_inc(mix_hi, 1)
                    pool.wait_ge(mix_hi, m + 1)
                    nc.gpsimd.tensor_tensor(act_lo[:, chunk, :], proj[:, slot, :],
                                            act_hi[:, chunk, :].bitcast(F32), ALU.subtract).then_inc(mix_split, 1)

            odd = 16 * (N_IN // 2 + N_AUX // 2)
            even = 16 * (N_IN // 2 + 2 + N_AUX // 2)
            pool.wait_ge(slab_done, N_IN)
            split_mix(0, 8)
            split(1, odd + 16, N_IN)
            split(0, even + 16, N_IN + 1)
            split_mix(8, 16)

            def split_pairs(first, end):
                with pool.Fori(first, end) as c:
                    split(1, c * 16 + (odd + 16), 2 * c + N_IN)
                    split(0, c * 16 + (even + 16), 2 * c + (N_IN + 1))

            def add_bias(i, half, done):
                pool.wait_ge(gained, TT * half + i + 1)
                nc.gpsimd.tensor_tensor(acc[:, i, :], acc[:, i, :], ln_b[:, :], ALU.add).then_inc(done[i], 1)

            ff_pair = N_OUT // 2
            split_pairs(1, ff_pair)
            split(1, odd + 16 * (ff_pair + 1), FF0)
            add_bias(0, 0, x1_ready)
            split(0, even + 16 * (ff_pair + 1), FF0 + 1)
            add_bias(2, 0, x1_ready)
            split_pairs(ff_pair + 1, (N_OUT + 12 * FF_GROUPS) // 2)
            add_bias(0, 1, y_ready)
            add_bias(2, 1, y_ready)

        @block.tensor
        def _(pe):
            def passes(out_ap, stat_hi, stat_lo, mov_hi, mov_lo, first, last):
                nc.tensor.matmul(out_ap, stat_hi, mov_hi, start=first, stop=False)
                nc.tensor.matmul(out_ap, stat_hi, mov_lo, start=False, stop=False)
                return nc.tensor.matmul(out_ap, stat_lo, mov_hi, start=False, stop=last)

            pe.wait_ge(ident_ready, 1)
            for i in range(TT):
                pe.wait_ge(x_loaded[i], 16)
                for q in range(4):
                    g = 4 * i + q
                    if g >= 6:
                        pe.wait_ge(xt_lo, g - 5)
                    for k in range(4):
                        mm = nc.tensor.transpose(psum[:, 2 + g % 6, k * P:(k + 1) * P],
                                                 x_nat[:, i, (4 * q + k) * P:(4 * q + k + 1) * P], ident[:, :])
                    mm.then_inc(xt_done, 1)
            pe.wait_ge(xt_lo, 4 * TT)

            def feature_slab(bank, slot, ready, m=P):
                pe.wait_ge(split_done, ready)
                for k in range(KT):
                    cols = slice(k * m, (k + 1) * m)
                    mm = passes(psum[0:m, bank, :], w_hi[:, slot, cols], w_lo[:, slot, cols],
                                act_hi[:, k, :], act_lo[:, k, :], k == 0, k == KT - 1)
                return mm

            def proj_slab(n, m=P, free=None):
                parity = n % 2 if isinstance(n, int) else None
                if free is not None:
                    pe.wait_ge(bank_free[parity], free)
                feature_slab(parity, parity, n + 1, m).then_inc(slab_done, 1)

            def proj_pairs(first, count):
                with pe.Fori(0, count) as c:
                    for b in (1, 0):
                        pe.wait_ge(bank_free[b], c + ((first - 1) // 2 + (1 - b)))
                        feature_slab(b, b, 2 * c + (first + 2 - b)).then_inc(slab_done, 1)

            proj_slab(0)
            proj_slab(1)
            proj_slab(2, free=1)
            proj_slab(3, free=1)
            proj_slab(N_IKWG, m=W_IKW + W_NG, free=2)

            pe.wait_ge(small_loaded, 16 * 10)
            for c in range(4):
                nc.tensor.transpose(psum[:, 7, c * VEC_ROWS:(c + 1) * VEC_ROWS],
                                    sel[0:VEC_ROWS, c * P:(c + 1) * P], ident[0:VEC_ROWS, 0:VEC_ROWS])
            nc.tensor.transpose(psum[:, 7, 4 * VEC_ROWS:4 * VEC_ROWS + 2 * CMP_BLOCK], pos_nat,
                                ident[0:2 * CMP_BLOCK, 0:2 * CMP_BLOCK]).then_inc(vec_t, 1)

            proj_pairs(N_CONV, 2)

            width = W_IKW + W_NG
            copied(pe, N_IKWG)
            for i in range(TT):
                mm = nc.tensor.transpose(psum[:, 6, i * width:(i + 1) * width],
                                         proj[0:width, S_IKWG, i * P:(i + 1) * P], ident[0:width, 0:width])
            mm.then_inc(iwg_t, 1)
            pe.wait_ge(ik_dup, 16)
            for e in range(3 * IDX_HEADS):
                i, h = e // IDX_HEADS + 1, e % IDX_HEADS
                if e >= 4:
                    pe.wait_ge(relu_done, e - 3)
                half = slice(64 * (h % 2), 64 * (h % 2) + 64)
                keys = proj[0:64, S_IKWG, 0:(i + 1) * P] if h % 2 == 0 else ik_high[:, 0:(i + 1) * P]
                nc.tensor.matmul(psum[:, 2 + e % 4, 0:(i + 1) * P], proj[half, S_IQ + h // 2, i * P:(i + 1) * P],
                                 keys, start=True, stop=True).then_inc(logit_done, 1)

            proj_pairs(N_CONV + 4, 10)
            for c in range(4):
                pe.wait_ge(conv_out, c + 1)
                mm = nc.tensor.matmul(psum[:, 2, :], ones[:, :], proj[:, CONV_OUT[c], :], start=c == 0, stop=c == 3)
            mm.then_inc(mean_done, 1)
            proj_pairs(N_CONV + 24, 1)
            for c in range(4):
                pe.wait_ge(squared, c + 1)
                mm = nc.tensor.matmul(psum[:, 3, :], ones[:, :], squares[:, c, :], start=c == 0, stop=c == 3)
            mm.then_inc(var_done, 1)
            proj_pairs(N_CONV + 26, 1)

            for v, slot in enumerate((S_DV, S_SV, S_WV)):
                copied(pe, SLAB_OF[slot])
                for j in range(TT):
                    mm = nc.tensor.transpose(psum[:, 4 + v, j * P:(j + 1) * P], proj[:, slot, j * P:(j + 1) * P],
                                             ident[:, :])
                mm.then_inc(v_t, 1)

            def aux_wait(a):
                slot = aux_slot(a)
                pe.wait_ge(raw_loaded[slot], 16 * (N_IN // 2 + (2 if slot == 0 else 0) + a // 2 + 1))
                return slot

            copied(pe, N_IN - 1)
            copied(pe, N_IN - 2)
            for a in range(4):
                slot, kv = aux_wait(a), a // 2
                pe.wait_ge(blk_ready, 2 * kv + 2)
                for l in range(16):
                    row = 16 * (a % 2) + l
                    mm = nc.tensor.matmul(psum[:, kv, 0:N_CMP], raw[:, slot, l * P:(l + 1) * P],
                                          blk[:, kv, row * CMP_BLOCK:row * CMP_BLOCK + N_CMP],
                                          start=row == 0, stop=row == CMP_BLOCK - 1)
                mm.then_inc(aux_used, 1)
            slot = aux_wait(4)
            pe.wait_ge(silu_ready, 4)
            pe.wait_ge(v_nat, 3)
            for m in range(4):
                for c in range(4):
                    mm = nc.tensor.matmul(psum[:, PW_BANKS[m], :],
                                          raw[:, slot, c * SEQ + m * P:c * SEQ + (m + 1) * P],
                                          proj[:, CONV_OUT[c], :], start=c == 0, stop=c == 3)
                mm.then_inc(pw_done, 1)
            slot = aux_wait(5)
            for g in range(4):
                pe.wait_ge(pool_in, g + 1)
                if g >= 2:
                    pe.wait_ge(mix_ready, 4 + g - 1)
                mm = nc.tensor.matmul(psum[:, 4 + g % 2, :], raw[:, slot, g * P:(g + 1) * P],
                                      proj[:, S_POOL + g, :], start=True, stop=True)
                mm.then_inc(pool_done, 1)
            pe.wait_ge(gelu_ready, 2)
            nc.tensor.matmul(psum[:, 0, 64:64 + N_CMP], w2[:, 0, :], cmp_h[:, 0, :], start=True, stop=True)
            nc.tensor.matmul(psum[0:N_CMP, 1, P:2 * P], cmp_h[:, 1, :], w2[:, 1, :],
                             start=True, stop=True).then_inc(cmp2_done, 1)
            pe.wait_ge(cmp_kv, 2)
            for e in range(HEADS * TT):
                h, i = e // TT, e % TT
                mm = nc.tensor.matmul(psum[:, 0, e * N_CMP:(e + 1) * N_CMP],
                                      proj[:, S_NQ + h, i * P:(i + 1) * P], cmp_kT[:, :], start=True, stop=True)
            mm.then_inc(cmp_logit, 1)

            def scores(g):
                q, k, _, _ = UNITS[g // TT]
                i = g % TT
                if g < 2:
                    pe.wait_ge(mix_ready, 4)
                else:
                    pe.wait_ge(scored, g - 1)
                nc.tensor.matmul(psum[:, 2 + g % 2, 0:(i + 1) * P], proj[:, q, i * P:(i + 1) * P],
                                 proj[:, k, 0:(i + 1) * P], start=True, stop=True).then_inc(qk_done, 1)

            def turn(g):
                i = g % TT
                pe.wait_ge(prob_ready, g + 1)
                if g < 2:
                    pe.wait_ge(mix_ready, 8)
                else:
                    pe.wait_ge(pt_ready, g - 1)
                for j in range(i + 1):
                    mm = nc.tensor.transpose(psum[:, 4 + g % 2, j * P:(j + 1) * P],
                                             t_ring[:, g % 4, j * P:(j + 1) * P], ident[:, :])
                mm.then_inc(tr_done, 1)

            def weigh(u):
                v = UNITS[u][2]
                o = u if u < HEADS else HEADS + (u - HEADS) // 2
                opens = u < HEADS or (u - HEADS) % 2 == 0
                closes = u < HEADS or (u - HEADS) % 2 == 1
                pe.wait_ge(pt_ready, TT * (u + 1))
                if opens and o >= 2:
                    pe.wait_ge(mix_ready, 7 + o)
                for j in range(TT):
                    mm = nc.tensor.matmul(psum[:, 6 + o % 2, j * P:SEQ], proj[:, v, j * P:(j + 1) * P],
                                          pt[:, u % 2, 4 * j * P:4 * j * P + (TT - j) * P],
                                          start=opens and j == 0, stop=u < HEADS and j == TT - 1)
                if u >= HEADS and closes:
                    pe.wait_ge(cmp_t_ready, HEADS)
                    mm = nc.tensor.matmul(psum[:, 6 + o % 2, :], cmp_v[:, :], cmp_pT[:, o - HEADS, :],
                                          start=False, stop=True)
                mm.then_inc(pv_done, 1)

            for g in range(N_TILES + 5):
                if g < N_TILES:
                    scores(g)
                if 3 <= g < N_TILES + 3:
                    turn(g - 3)
                if g >= 5 and (g - 5) % TT == TT - 1:
                    weigh((g - 5) // TT)
                if g == HEADS * TT:
                    pe.wait_ge(cmp_prob, 1)
                    for h in range(HEADS):
                        if h >= 2:
                            pe.wait_ge(cmp_t_ready, h - 1)
                        for i in range(TT):
                            e = h * TT + i
                            mm = nc.tensor.matmul(psum[0:N_CMP, h % 2, i * P:(i + 1) * P],
                                                  cmp_p[:, e * N_CMP:(e + 1) * N_CMP], ident[:, :],
                                                  start=True, stop=True)
                        mm.then_inc(cmp_t, 1)

            pe.wait_ge(mix_split, 16)
            nc.tensor.sem_inc(tile_added, TILES0)

            def token_slabs(bank0, slots, first, hi, lo, tiles, added):
                for s, slot in enumerate(slots):
                    pe.wait_ge(split_done, first + (s + 1))
                    for i in range(TT):
                        if s == 0:
                            pe.wait_ge(tile_added, added + (i + 1))
                        for k in range(4):
                            t = tiles * s + k
                            toks, cols = slice(i * P, (i + 1) * P), slice(k * SEQ, (k + 1) * SEQ)
                            out_ap = psum[:, bank0 + i, :]
                            first_mm = s == 0 and k == 0
                            last_mm = s == len(slots) - 1 and k == 3
                            nc.tensor.matmul(out_ap, hi[:, t, toks], w_hi[:, slot, cols], start=first_mm, stop=False)
                            nc.tensor.matmul(out_ap, lo[:, t, toks], w_hi[:, slot, cols], start=False, stop=False)
                            mm = nc.tensor.matmul(out_ap, hi[:, t, toks], w_lo[:, slot, cols],
                                                  start=False, stop=last_mm)
                        if i == TT - 1:
                            mm.then_inc(slab_done, 1)
                        elif s == len(slots) - 1:
                            mm.then_inc(tile_done, 1)

            with pe.Fori(0, 2) as c:
                for half in range(2):
                    token_slabs(4 * half, (1, 0, 1, 0), 8 * c + (N_IN + 4 * half), act_hi, act_lo, 4,
                                8 * c + 4 * half)

            def turn_x1(i):
                pe.wait_ge(x1_ready[i], 1)
                for q in range(4):
                    e = 4 * i + q
                    if e >= 6:
                        pe.wait_ge(x1_lo, e - 5)
                    for k in range(4):
                        mm = nc.tensor.transpose(psum[:, X1_BANKS[e % 6], k * P:(k + 1) * P],
                                                 acc[:, i, (4 * q + k) * P:(4 * q + k + 1) * P], ident[:, :])
                    mm.then_inc(x1_t, 1)

            def hidden(j, first, free=None):
                if free is not None:
                    pe.wait_ge(hid_ready, free)
                for u in range(2):
                    feature_slab(4 + 2 * (j % 2) + u, (u + 1) % 2, first + (u + 1)).then_inc(slab_done, 1)

            def down(first, group):
                pe.wait_ge(hid_lo, group * 4 + 4)
                for n in range(4):
                    token_slabs(0, ((n + 1) % 2,), first + n, h_hi, h_lo, 0,
                                group * 16 + (4 * n + TILES0 + 4 * 4 - 4))

            half_toks = SEQ // 2
            for half in range(2):
                turn_x1(2 * half)
                turn_x1(2 * half + 1)
                pe.wait_ge(x1_lo, 8 * half + 8)
                toks = slice(half * half_toks, (half + 1) * half_toks)
                for u in range(2):
                    pe.wait_ge(split_done, FF0 + 1 + u)
                    for k in range(KT):
                        cols = slice(k * P, (k + 1) * P)
                        mm = passes(psum[:, 4 + u, toks], w_hi[:, (u + 1) % 2, cols], w_lo[:, (u + 1) % 2, cols],
                                    act_hi[:, k, toks], act_lo[:, k, toks], k == 0, k == KT - 1)
                    if half == 1:
                        mm.then_inc(slab_done, 1)
            hidden(1, FF0 + 2)
            with pe.Fori(0, FF_GROUPS - 1) as g:
                hidden(2, g * 12 + (FF0 + 4), g * 4 + 1)
                hidden(3, g * 12 + (FF0 + 6), g * 4 + 2)
                hidden(4, g * 12 + (FF0 + 8), g * 4 + 3)
                down(g * 12 + (FF0 + 10), g)
                hidden(5, g * 12 + (FF0 + 14), g * 4 + 4)
            last = FF_GROUPS - 1
            hidden(2, 12 * last + FF0 + 4, 4 * last + 1)
            hidden(3, 12 * last + FF0 + 6, 4 * last + 2)
            down(12 * last + FF0 + 8, last)

        @block.scalar
        def _(act):
            for i in range(TT):
                for q in range(4):
                    g = 4 * i + q
                    act.wait_ge(xt_done, g + 1)
                    nc.scalar.copy(act_hi[:, 4 * q:4 * q + 4, i * P:(i + 1) * P],
                                   psum[:, 2 + g % 6, :].rearrange("p (k s) -> p k s", k=4)).then_inc(xt_hi, 1)

            def copy_out(n, slot, scale=1.0, rows=P):
                act.wait_ge(slab_done, n + 1)
                nc.scalar.activation(proj[0:rows, slot, :], psum[0:rows, n % 2, :], ACT.Copy,
                                     scale=scale).then_inc(bank_free[n % 2], 1)

            def conv_gate(c):
                n = N_CONV + 2 * c
                act.wait_ge(slab_done, n + 1)
                nc.scalar.activation(proj[:, S_CONV + c, :], psum[:, n % 2, :], ACT.Sigmoid)\
                    .then_inc(bank_free[n % 2], 1)

            for n in range(4):
                copy_out(n, S_IQ + n)
            copy_out(N_IKWG, S_IKWG, rows=W_IKW + W_NG)
            copied(act, N_IKWG)
            nc.scalar.dma_start(ik_high, proj[0:64, S_IKWG, :]).then_inc(ik_dup, 16)
            conv_gate(0)
            conv_gate(1)
            act.wait_ge(iwg_ready, 2)
            nc.scalar.activation(iwg[:, :, W_IKW:], iwg[:, :, W_IKW:], ACT.Sigmoid).then_inc(gates_ready, 1)
            for e in range(3 * IDX_HEADS):
                w = (e // IDX_HEADS + 2) * P
                act.wait_ge(logit_done, e + 1)
                if e >= 6:
                    act.wait_ge(relu_used, e - 5)
                nc.scalar.activation(relu_ring[:, e % 6, 0:w], psum[:, 2 + e % 4, 0:w], ACT.Relu)\
                    .then_inc(relu_done, 1)
            conv_gate(2)
            conv_gate(3)
            for g in range(4):
                copy_out(N_POOL + g, S_POOL + g)
            for s in range(12):
                scale = 1.0
                if s < 4:
                    scale = ATTN_SCALE / SLOPES_DSA[s]
                elif 6 <= s < 10:
                    scale = ATTN_SCALE / SLOPES_NSA[s - 6]
                copy_out(N_QKV + s, S_DQ + s, scale)
            for c in range(4):
                act.wait_ge(centred, c + 1)
                nc.scalar.activation(squares[:, c, :], proj[:, CONV_OUT[c], :], ACT.Square).then_inc(squared, 1)
            copy_out(N_QKV + 12, S_SK)
            copy_out(N_QKV + 13, S_SV)
            act.wait_ge(var_done, 1)
            act.wait_ge(conv_out, 4)
            nc.scalar.activation(rstd_conv, psum[:, 3, :], ACT.Sqrt, bias=eps[:, :]).then_inc(std_ready, 1)
            for s in range(14, 16):
                copy_out(N_QKV + s, S_DQ + s)
            for c in range(4):
                act.wait_ge(normed, c + 1)
                nc.scalar.activation(proj[:, CONV_OUT[c], :], proj[:, CONV_OUT[c], :], ACT.Silu,
                                     bias=vecs[:, c, V_LB:V_LB + 1],
                                     scale=vecs[:, c, V_LG:V_LG + 1]).then_inc(silu_ready, 1)
            for v, slot in enumerate((S_DV, S_SV, S_WV)):
                act.wait_ge(v_t, v + 1)
                nc.scalar.copy(proj[:, slot, :], psum[:, 4 + v, :]).then_inc(v_nat, 1)
            for kv in range(2):
                act.wait_ge(aux_used, 2 * kv + 2)
                nc.scalar.activation(cmp_h[:, kv, :], psum[:, kv, 0:N_CMP], ACT.Gelu_apprx_tanh)\
                    .then_inc(gelu_ready, 1)
            act.wait_ge(pw_done, 4)
            for m in range(4):
                nc.scalar.activation(proj[:, CONV_OUT[m], :], psum[:, PW_BANKS[m], :], ACT.Identity,
                                     bias=vecs[:, m, V_PB:V_PB + 1]).then_inc(mix_ready, 1)
            for g in range(4):
                act.wait_ge(pool_done, g + 1)
                nc.scalar.activation(proj[:, S_POOL + g, :], psum[:, 4 + g % 2, :], ACT.Copy,
                                     scale=vecs[:, g, V_PS:V_PS + 1]).then_inc(mix_ready, 1)

            act.wait_ge(cmp_shift, 1)
            for h in range(HEADS):
                cols = slice(h * TT * N_CMP, (h + 1) * TT * N_CMP)
                nc.scalar.activation(cmp_p[:, cols], cmp_p[:, cols], ACT.Exp, scale=SLOPES_NSA[h])\
                    .then_inc(cmp_exp, 1)

            def exponentials(g):
                u, w = g // TT, (g % TT + 1) * P
                act.wait_ge(max_ready, g + 1)
                nc.scalar.activation(t_ring[:, g % 4, 0:w], t_ring[:, g % 4, 0:w], ACT.Exp,
                                     bias=neg_max[:, g % 4:g % 4 + 1], scale=UNITS[u][3],
                                     accum_out=row_sum[:, g % 4:g % 4 + 1]).then_inc(exp_done, 1)

            def turned(g):
                u, i = g // TT, g % TT
                act.wait_ge(tr_done, g + 1)
                if i == 0 and u >= 2:
                    act.wait_ge(pv_done, u - 1)
                dst = pt[:, u % 2, :].rearrange("p (b s) -> p b s", s=P)[:, i:i + 3 * i + 1:3, :]
                nc.scalar.copy(dst, psum[:, 4 + g % 2, 0:(i + 1) * P].rearrange("p (b s) -> p b s", s=P))\
                    .then_inc(pt_ready, 1)

            def head_out(u):
                if u < HEADS or (u - HEADS) % 2 == 1:
                    o = u if u < HEADS else HEADS + (u - HEADS) // 2
                    act.wait_ge(pv_done, u + 1)
                    nc.scalar.copy(proj[:, UNITS[u][0], :], psum[:, 6 + o % 2, :]).then_inc(mix_ready, 1)

            for g in range(N_TILES + 6):
                if g < N_TILES:
                    exponentials(g)
                if 3 <= g < N_TILES + 3:
                    turned(g - 3)
                if g >= 6 and (g - 6) % TT == TT - 1:
                    head_out((g - 6) // TT)

            def deviation(i, half):
                act.wait_ge(var_ready, TT * half + i + 1)
                nc.scalar.activation(std[:, i:i + 1], moments[:, i, 1:2], ACT.Sqrt, bias=eps[:, :])\
                    .then_inc(std_done, 1)

            def normal(i, half):
                act.wait_ge(rstd_ready, TT * half + i + 1)
                nc.scalar.activation(acc[:, i, :], acc[:, i, :], ACT.Identity, bias=shift[:, i:i + 1],
                                     scale=rstd[:, i:i + 1]).then_inc(xn_ready, 1)

            def normalise_tiles(half):
                deviation(0, half)
                for i in range(1, TT):
                    deviation(i, half)
                    normal(i - 1, half)
                normal(TT - 1, half)

            normalise_tiles(0)
            for i in range(TT):
                for q in range(4):
                    e = 4 * i + q
                    act.wait_ge(x1_t, e + 1)
                    nc.scalar.copy(act_hi[:, 4 * q:4 * q + 4, i * P:(i + 1) * P],
                                   psum[:, X1_BANKS[e % 6], :].rearrange("p (k s) -> p k s", k=4)).then_inc(x1_hi, 1)
            for i in range(TT):
                nc.scalar.mul(acc[:, i, :], acc[:, i, :], ALPHA).then_inc(scaled, 1)

            def gate(j, q, slab):
                act.wait_ge(slab_done, slab + 1)
                if not isinstance(q, int) or q >= 2:
                    act.wait_ge(hid_ready, q - 1)
                nc.scalar.activation(silu_g[:, j % 2, :], psum[:, 4 + 2 * (j % 2), :], ACT.Silu).then_inc(silu_done, 1)

            def hidden_hi(j, q):
                act.wait_ge(hid_ready, q + 1)
                nc.scalar.copy(h_hi[:, j % 4, :], hid[:, j % 2, :]).then_inc(hid_hi, 1)

            gate(0, 0, FF0)
            hidden_hi(0, 0)
            gate(1, 1, FF0 + 2)
            hidden_hi(1, 1)
            with act.Fori(0, FF_GROUPS - 1) as g:
                for j in (2, 3):
                    gate(j, g * 4 + j, g * 12 + (FF0 + 2 * j))
                    hidden_hi(j, g * 4 + j)
                gate(4, g * 4 + 4, g * 12 + (FF0 + 8))
                act.wait_ge(slab_done, g * 12 + (FF0 + 14))
                hidden_hi(4, g * 4 + 4)
                gate(5, g * 4 + 5, g * 12 + (FF0 + 14))
                hidden_hi(5, g * 4 + 5)
            last = FF_GROUPS - 1
            for j in (2, 3):
                gate(j, 4 * last + j, 12 * last + FF0 + 2 * j)
                hidden_hi(j, 4 * last + j)
            normalise_tiles(1)

        @block.vector
        def _(ve):
            chain = [0]

            def link(ins):
                chain[0] += 1
                ins.then_inc(dve, 1)
                ve.wait_ge(dve, chain[0])

            ve.wait_ge(const_ready, 10)
            link(nc.vector.reciprocal(inv_count[:, :], inv_count[:, :]))
            for i in range(TT):
                for q in range(4):
                    g = 4 * i + q
                    here = (slice(None), slice(4 * q, 4 * q + 4), slice(i * P, (i + 1) * P))
                    ve.wait_ge(xt_hi, g + 1)
                    nc.vector.tensor_tensor(act_lo[here], psum[:, 2 + g % 6, :].rearrange("p (k s) -> p k s", k=4),
                                            act_hi[here].bitcast(F32), ALU.subtract).then_inc(xt_lo, 1)
            ve.wait_ge(vec_t, 1)
            nc.vector.tensor_copy(vecs[:, :, :].rearrange("p c v -> p (c v)"), psum[:, 7, 0:4 * VEC_ROWS])\
                .then_inc(vec_ready, 1)
            nc.vector.tensor_copy(pos[:, :], psum[:, 7, 4 * VEC_ROWS:4 * VEC_ROWS + 2 * CMP_BLOCK])\
                .then_inc(vec_ready, 1)

            def conv_value(c):
                n = N_CONV + 2 * c + 1
                copied(ve, n - 1)
                ve.wait_ge(slab_done, n + 1)
                nc.vector.tensor_tensor(proj[:, S_CONV + c, :], psum[:, n % 2, :], proj[:, S_CONV + c, :],
                                        ALU.mult).then_inc(bank_free[n % 2], 1)

            conv_value(0)
            conv_value(1)
            ve.wait_ge(iwg_t, 1)
            nc.vector.tensor_copy(iwg[:, :, :].rearrange("p i w -> p (i w)"), psum[:, 6, 0:TT * (W_IKW + W_NG)])\
                .then_inc(iwg_ready, 1)
            ve.wait_ge(iwg_ready, 1)
            nc.vector.tensor_scalar(iwg[:, :, IDX_DIM:W_IKW], iwg[:, :, IDX_DIM:W_IKW], IDX_SCALE, None, ALU.mult)\
                .then_inc(iwg_ready, 1)
            ve.wait_ge(iwg_ready, 2)
            for e in range(3 * IDX_HEADS):
                i, h = e // IDX_HEADS + 1, e % IDX_HEADS
                w = (i + 1) * P
                score = sel[:, SEL_OFF[i]:SEL_OFF[i] + w]
                weight = iwg[:, i, IDX_DIM + h:IDX_DIM + h + 1]
                ve.wait_ge(relu_done, e + 1)
                if h > 0:
                    ve.wait_ge(relu_used, e)
                    nc.vector.scalar_tensor_tensor(out=score, in0=relu_ring[:, e % 6, 0:w], scalar=weight,
                                                   in1=score, op0=ALU.mult, op1=ALU.add).then_inc(relu_used, 1)
                else:
                    nc.vector.tensor_scalar(score, relu_ring[:, e % 6, 0:w], weight, None, ALU.mult)\
                        .then_inc(relu_used, 1)
            conv_value(2)
            conv_value(3)
            ve.wait_ge(relu_used, 3 * IDX_HEADS)
            for i in range(1, TT):
                w = (i + 1) * P
                score = sel[:, SEL_OFF[i]:SEL_OFF[i] + w]
                diagonal = sel[:, SEL_OFF[i] + i * P:SEL_OFF[i] + w]
                link(nc.vector.tensor_tensor(diagonal, diagonal, later[:, :], ALU.add))
                for _ in range(TOPK // 8):
                    link(nc.vector.max(out=top8[:, :], in_=score))
                    link(nc.vector.match_replace(out=score, in_to_replace=top8[:, :], in_values=score,
                                                 imm_value=PICKED))
                link(nc.vector.tensor_scalar(score, score, 0.5 * PICKED, MASKED, ALU.is_gt, ALU.mult))
                link(nc.vector.tensor_tensor(score, score, dist[:, SEQ - w:SEQ], ALU.add))

            for c in range(4):
                h_in, y = proj[:, S_CONV + c, :], proj[:, CONV_OUT[c], :]
                copied(ve, N_CONV + 2 * c + 1)
                if c > 0:
                    ve.wait_ge(conv_out, c)
                tap = CONV_WIDTH - 1
                link(nc.vector.tensor_scalar(y, h_in, vecs[:, c, tap:tap + 1], vecs[:, c, V_CB:V_CB + 1],
                                             ALU.mult, ALU.add))
                for tap in range(CONV_WIDTH - 1):
                    s = CONV_WIDTH - 1 - tap
                    ins = nc.vector.scalar_tensor_tensor(out=y[:, s:], in0=h_in[:, 0:SEQ - s],
                                                         scalar=vecs[:, c, tap:tap + 1], in1=y[:, s:],
                                                         op0=ALU.mult, op1=ALU.add)
                    if tap < CONV_WIDTH - 2:
                        link(ins)
                ins.then_inc(conv_out, 1)

            for g in range(4):
                u = proj[:, S_POOL + g, :]
                copied(ve, N_POOL + g)
                if g > 0:
                    ve.wait_ge(pool_in, g)
                src, bufs = u, [tmp_a, tmp_b]
                for s in range(g + 1):
                    step, dst = 2 ** s, bufs[s % 2]
                    nc.vector.tensor_copy(dst[:, 0:step], src[:, 0:step])
                    link(nc.vector.tensor_tensor(dst[:, step:], src[:, step:], src[:, 0:SEQ - step], ALU.add))
                    src = dst
                win = 2 ** (g + 1)
                head = bufs[(g + 1) % 2][:, 0:win - 1]
                link(nc.vector.tensor_tensor(head, src[:, 0:win - 1], inv_count[:, 0:win - 1], ALU.mult))
                link(nc.vector.tensor_tensor(u[:, 0:win - 1], head, u[:, 0:win - 1], ALU.subtract))
                nc.vector.scalar_tensor_tensor(out=u[:, win - 1:], in0=src[:, win - 1:], scalar=1.0 / win,
                                               in1=u[:, win - 1:], op0=ALU.mult, op1=ALU.subtract)\
                    .then_inc(pool_in, 1)

            ve.wait_ge(mean_done, 1)
            ve.wait_ge(conv_out, 4)
            for c in range(4):
                y = proj[:, CONV_OUT[c], :]
                nc.vector.tensor_tensor(y, y, psum[:, 2, :], ALU.subtract).then_inc(centred, 1)
            ve.wait_ge(std_ready, 1)
            link(nc.vector.reciprocal(rstd_conv, rstd_conv))
            ve.wait_ge(squared, 4)
            ve.wait_ge(centred, 4)
            for c in range(4):
                y = proj[:, CONV_OUT[c], :]
                nc.vector.tensor_tensor(y, y, rstd_conv, ALU.mult).then_inc(normed, 1)

            ve.wait_ge(pool_in, 4)
            ve.wait_ge(vec_ready, 2)
            for kv, slot in enumerate((S_CK, S_CV)):
                copied(ve, SLAB_OF[slot])
                src = proj[:, slot, :].rearrange("p (c b) -> p b c", b=CMP_STRIDE)
                dst = blk[:, kv, :].rearrange("p (l c) -> p l c", c=CMP_BLOCK)
                for a in range(2):
                    rows = slice(CMP_STRIDE * a, CMP_STRIDE * (a + 1))
                    at = pos[:, kv * CMP_BLOCK + CMP_STRIDE * a:kv * CMP_BLOCK + CMP_STRIDE * (a + 1)]
                    nc.vector.tensor_tensor(dst[:, rows, 0:N_CMP], src[:, :, a:a + N_CMP],
                                            at.unsqueeze(2).to_broadcast([P, CMP_STRIDE, N_CMP]),
                                            ALU.add).then_inc(blk_ready, 1)

            ve.wait_ge(cmp2_done, 1)
            nc.vector.tensor_copy(cmp_kT[:, :], psum[:, 0, 64:64 + N_CMP]).then_inc(cmp_kv, 1)
            nc.vector.tensor_copy(cmp_v[:, :], psum[0:N_CMP, 1, P:2 * P]).then_inc(cmp_kv, 1)

            flat = cmp_p[:, :].rearrange("p (h e) -> p h e", h=HEADS)
            rows = cmp_p[:, :].rearrange("p (e c) -> p e c", c=N_CMP)
            ve.wait_ge(cmp_logit, 1)
            link(nc.vector.tensor_tensor(flat, psum[:, 0, 0:16 * N_CMP].rearrange("p (h e) -> p h e", h=HEADS),
                                         cmp_dist[:, :].unsqueeze(1).to_broadcast([P, HEADS, TT * N_CMP]), ALU.add))
            link(nc.vector.tensor_reduce(cmp_m[:, :], rows, AX.X, ALU.max))
            link(nc.vector.tensor_scalar(cmp_m[:, :], cmp_m[:, :], 0.1 * MASKED, None, ALU.max))
            nc.vector.tensor_tensor(rows, rows, cmp_m[:, :].unsqueeze(2).to_broadcast([P, 16, N_CMP]), ALU.subtract)\
                .then_inc(cmp_shift, 1)

            def add_distance(g):
                u, i = g // TT, g % TT
                w = (i + 1) * P
                if u < HEADS and i > 0:
                    d = sel[:, SEL_OFF[i]:SEL_OFF[i] + w]
                else:
                    d = dist[:, SEQ - w:SEQ]
                ve.wait_ge(qk_done, g + 1)
                if g >= 4:
                    ve.wait_ge(tr_done, g - 3)
                nc.vector.tensor_tensor_reduce(out=t_ring[:, g % 4, 0:w], in0=psum[:, 2 + g % 2, 0:w], in1=d,
                                               scale=1.0, scalar=PICKED, op0=ALU.add, op1=ALU.max,
                                               accum_out=row_max[:, g % 4:g % 4 + 1]).then_inc(scored, 1)
                ve.wait_ge(scored, g + 1)
                nc.vector.tensor_scalar(neg_max[:, g % 4:g % 4 + 1], row_max[:, g % 4:g % 4 + 1], 0.1 * MASKED,
                                        -UNITS[u][3], ALU.max, ALU.mult).then_inc(max_ready, 1)

            def normalise(g):
                u, i = g // TT, g % TT
                w = (i + 1) * P
                inv = row_inv[:, g % 4:g % 4 + 1]
                ve.wait_ge(exp_done, g + 1)
                link(nc.vector.tensor_scalar(inv, row_sum[:, g % 4:g % 4 + 1], 1e-30, None, ALU.max))
                link(nc.vector.reciprocal(inv, inv))
                p = t_ring[:, g % 4, 0:w]
                if u < HEADS:
                    nc.vector.tensor_scalar(p, p, inv, None, ALU.mult).then_inc(prob_ready, 1)
                else:
                    col = W_IKW + 3 * ((u - HEADS) // 2) + 1 + (u - HEADS) % 2
                    nc.vector.tensor_scalar(p, p, inv, iwg[:, i, col:col + 1], ALU.mult, ALU.mult)\
                        .then_inc(prob_ready, 1)

            def compressed_probs():
                ve.wait_ge(cmp_exp, HEADS)
                link(nc.vector.tensor_reduce(cmp_r[:, :], rows, AX.X, ALU.add))
                link(nc.vector.tensor_scalar(cmp_r[:, :], cmp_r[:, :], 1e-30, None, ALU.max))
                link(nc.vector.reciprocal(cmp_r[:, :], cmp_r[:, :]))
                gates = iwg[:, :, W_IKW:].rearrange("p i (h b) -> p h i b", b=3)[:, :, :, 0]
                r = cmp_r[:, :].rearrange("p (h i) -> p h i", h=HEADS)
                link(nc.vector.tensor_tensor(r, r, gates, ALU.mult))
                nc.vector.tensor_tensor(rows, rows, cmp_r[:, :].unsqueeze(2).to_broadcast([P, 16, N_CMP]),
                                        ALU.mult).then_inc(cmp_prob, 1)

            ve.wait_ge(gates_ready, 1)
            for g in range(N_TILES + 1):
                if g < N_TILES:
                    add_distance(g)
                if g >= 1:
                    normalise(g - 1)
                if g == 4:
                    compressed_probs()
                if g == HEADS * TT:
                    for h in range(HEADS):
                        ve.wait_ge(cmp_t, h + 1)
                        nc.vector.tensor_copy(cmp_pT[:, h, :], psum[0:N_CMP, h % 2, :]).then_inc(cmp_t_ready, 1)

            def add_out(n, i):
                cols = acc[:, i, n * SEQ:(n + 1) * SEQ]
                tile_ready(ve, n, N_IN + 4 * n + 3, i)
                nc.vector.scalar_tensor_tensor(out=cols, in0=cols, scalar=ALPHA, in1=psum[:, 4 * (n % 2) + i, :],
                                               op0=ALU.mult, op1=ALU.add).then_inc(tile_added, 1)
                ve.wait_ge(tile_added, TILES0 + 4 * n + i + 1)
                link(nc.vector.bn_stats(stats[:, i, n, :], cols))

            def add_down(group, slab, n, i, with_stats=False):
                cols = acc[:, i, n * SEQ:(n + 1) * SEQ]
                tile_ready(ve, group * 4 + (4 + n), slab + n, i)
                nc.vector.tensor_tensor(cols, cols, psum[:, i, :], ALU.add).then_inc(tile_added, 1)
                if with_stats:
                    ve.wait_ge(tile_added, group * 16 + (TILES0 + 16 + 4 * n + i + 1))
                    link(nc.vector.bn_stats(stats[:, i, n, :], cols))

            def moments_of(i):
                nc.vector.bn_aggr(moments[:, i, :], stats[:, i, :, :].rearrange("p n s -> p (n s)"))\
                    .then_inc(var_ready, 1)

            def rstd_of(i, half):
                ve.wait_ge(std_done, TT * half + i + 1)
                link(nc.vector.reciprocal(rstd[:, i:i + 1], std[:, i:i + 1]))
                nc.vector.scalar_tensor_tensor(out=shift[:, i:i + 1], in0=moments[:, i, 0:1], scalar=-1.0,
                                               in1=rstd[:, i:i + 1], op0=ALU.mult, op1=ALU.mult)\
                    .then_inc(rstd_ready, 1)

            def gain(i, half):
                ve.wait_ge(xn_ready, TT * half + i + 1)
                nc.vector.tensor_tensor(acc[:, i, :], acc[:, i, :], ln_g[:, :], ALU.mult).then_inc(gained, 1)

            def bias(i, half, done):
                ve.wait_ge(gained, TT * half + i + 1)
                nc.vector.tensor_tensor(acc[:, i, :], acc[:, i, :], ln_b[:, :], ALU.add).then_inc(done[i], 1)

            def x1_split(i):
                for q in range(4):
                    e = 4 * i + q
                    here = (slice(None), slice(4 * q, 4 * q + 4), slice(i * P, (i + 1) * P))
                    ve.wait_ge(x1_hi, e + 1)
                    nc.vector.tensor_tensor(act_lo[here],
                                            psum[:, X1_BANKS[e % 6], :].rearrange("p (k s) -> p k s", k=4),
                                            act_hi[here].bitcast(F32), ALU.subtract).then_inc(x1_lo, 1)

            ve.wait_ge(resid_loaded, 16)
            for n in range(3):
                for i in range(TT):
                    add_out(n, i)
            ve.wait_ge(ln_loaded, 32)
            for i in range(TT):
                add_out(3, i)
                moments_of(i)
                if i >= 1:
                    rstd_of(i - 1, 0)
                if i >= 2:
                    gain(i - 2, 0)
            rstd_of(3, 0)
            bias(1, 0, x1_ready)
            x1_split(0)
            x1_split(1)
            gain(2, 0)
            gain(3, 0)
            bias(3, 0, x1_ready)
            x1_split(2)
            x1_split(3)

            def hidden(j, q, slab):
                ve.wait_ge(slab_done, slab + 1)
                ve.wait_ge(silu_done, q + 1)
                if not isinstance(q, int) or q >= 2:
                    ve.wait_ge(hid_lo, q - 1)
                nc.vector.tensor_tensor(hid[:, j % 2, :], psum[:, 5 + 2 * (j % 2), :], silu_g[:, j % 2, :],
                                        ALU.mult).then_inc(hid_ready, 1)

            def hidden_lo(j, q):
                ve.wait_ge(hid_hi, q + 1)
                nc.vector.tensor_tensor(h_lo[:, j % 4, :], hid[:, j % 2, :], h_hi[:, j % 4, :].bitcast(F32),
                                        ALU.subtract).then_inc(hid_lo, 1)

            hidden(0, 0, FF0 + 1)
            hidden_lo(0, 0)
            hidden(1, 1, FF0 + 3)
            hidden_lo(1, 1)
            ve.wait_ge(scaled, TT)
            with ve.Fori(0, FF_GROUPS - 1) as g:
                for j in (2, 3):
                    hidden(j, g * 4 + j, g * 12 + (FF0 + 2 * j + 1))
                    hidden_lo(j, g * 4 + j)
                hidden(4, g * 4 + 4, g * 12 + (FF0 + 9))
                for n in range(4):
                    for i in range(TT):
                        add_down(g, g * 12 + (FF0 + 10), n, i)
                hidden_lo(4, g * 4 + 4)
                hidden(5, g * 4 + 5, g * 12 + (FF0 + 15))
                hidden_lo(5, g * 4 + 5)
            last = FF_GROUPS - 1
            for j in (2, 3):
                hidden(j, 4 * last + j, 12 * last + FF0 + 2 * j + 1)
                hidden_lo(j, 4 * last + j)
            slab = 12 * last + FF0 + 8
            for n in range(3):
                for i in range(TT):
                    add_down(last, slab, n, i, with_stats=True)
            ve.wait_ge(ln_loaded, 64)
            for i in range(TT):
                add_down(last, slab, 3, i, with_stats=True)
                moments_of(i)
                if i >= 1:
                    rstd_of(i - 1, 1)
                if i >= 2:
                    gain(i - 2, 1)
            rstd_of(3, 1)
            bias(1, 1, y_ready)
            gain(2, 1)
            gain(3, 1)
            bias(3, 1, y_ready)


_INS = ["x", "w_in", "w_out", "pool_w", "pool_scale", "conv_w", "conv_b", "conv_ln_g", "conv_ln_b",
        "conv_pw_w", "conv_pw_b", "cmp_pos_k", "cmp_pos_v", "cmp_k_w1", "cmp_k_w2", "cmp_v_w1",
        "cmp_v_w2", "ln1_g", "ln1_b", "ln2_g", "ln2_b", "w_gate_up", "w_down"]


def kernel(**inputs):
    import concourse.bacc as bacc
    from concourse.bass_utils import run_bass_kernel_spmd

    nc = bacc.Bacc("TRN2", target_bir_lowering=False, num_devices=1)
    arrays, args = {}, []
    for name in _INS:
        a = np.ascontiguousarray(inputs[name])
        arrays[f"in_{name}"] = a
        args.append(nc.dram_tensor(f"in_{name}", a.shape, mybir.dt.from_np(a.dtype), kind="ExternalInput").ap())
    out = nc.dram_tensor("out", (1, SEQ, D_MODEL), F32, kind="ExternalOutput").ap()
    build(nc, *args, out)
    result = run_bass_kernel_spmd(nc, [arrays], core_ids=[0])
    return result.results[0]["out"]
```

```python
from contextlib import ExitStack

import numpy as np

import concourse.bass as bass
from concourse import mybir

F32 = mybir.dt.float32
F32R = mybir.dt.float32r
ALU = mybir.AluOpType
ACT = mybir.ActivationFunctionType
AX = mybir.AxisListType

P = 128
SEQ = 512
D_MODEL = 2048
KT = D_MODEL // P
TT = SEQ // P
D_FF = 5632
HEADS = 4
IDX_HEADS, IDX_DIM = 8, 64
TOPK = min(256, SEQ // 4)
CONV_WIDTH = 31
CMP_BLOCK, CMP_STRIDE = 32, 16
N_CMP = (SEQ - CMP_BLOCK) // CMP_STRIDE + 1
ALPHA = 2.0 ** 0.25
LN_EPS = 1e-5
ATTN_SCALE = float(P) ** -0.5
IDX_SCALE = float(IDX_HEADS * IDX_DIM) ** -0.5
SLOPES_DSA = [2.0 ** -(2 * h + 1) for h in range(HEADS)]
SLOPES_NSA = [2.0 ** -(2 * h + 2) for h in range(HEADS)]
MASKED = -1e30
PICKED = -3e38

SLAB = 2048
C_POOL, C_A, C_G, C_DQ, C_IQ, C_IK, C_NQ, C_NG = 0, 512, 1024, 1536, 2304, 2816, 2888, 4168
W_IKW, W_NG = IDX_DIM + IDX_HEADS, 3 * HEADS

N_IDX, N_IKWG, N_CONV, N_POOL, N_QKV = 0, 4, 5, 13, 17
N_IN = 33
N_OUT = 16
FF_CHUNKS = D_FF // P
FF_GROUPS = FF_CHUNKS // 4

S_IQ, S_IKWG, S_CONV, S_SPARE, S_POOL, S_DQ, S_DK, S_DV, S_NQ = 0, 4, 5, 9, 10, 14, 18, 19, 20
S_CK, S_CV, S_SK, S_SV, S_WK, S_WV = 24, 25, 26, 27, 28, 29
N_SLOTS = 30
CONV_OUT = [S_SPARE, S_CONV, S_CONV + 1, S_CONV + 2]
VEC_ROWS = CONV_WIDTH + 5
V_CB, V_LG, V_LB, V_PB, V_PS = range(CONV_WIDTH, VEC_ROWS)

UNITS = [(S_DQ + h, S_DK, S_DV, SLOPES_DSA[h]) for h in range(HEADS)]
for _h in range(HEADS):
    UNITS += [(S_NQ + _h, S_SK, S_SV, SLOPES_NSA[_h]), (S_NQ + _h, S_WK, S_WV, SLOPES_NSA[_h])]
N_UNITS = len(UNITS)
N_TILES = N_UNITS * TT
SLAB_OF = {S_POOL + g: N_POOL + g for g in range(4)}
SLAB_OF.update({S_DQ + s: N_QKV + s for s in range(16)})
T_SLOTS = [S_IQ, S_IQ + 1, S_IQ + 2, S_IQ + 3, S_IKWG, S_CONV + 3]
RING = len(T_SLOTS)
TURN_LAG = RING - 1
WEIGH_LAG = TURN_LAG + 2
OUT_LAG = WEIGH_LAG + 1
LO_LAG = OUT_LAG + 1
PW_BANKS = [2, 3, 6, 7]
X1_BANKS = [0, 1, 2, 3, 6, 7]
SEL_OFF = [None, 0, 2 * P, 5 * P]
MIX_ORDER = list(range(4, 8)) + list(range(0, 4)) + list(range(8, 16))


def head_of(u):
    return u if u < HEADS else HEADS + (u - HEADS) // 2


def closes_head(u):
    return u < HEADS or (u - HEADS) % 2 == 1


def build(nc, x, w_in, w_out, pool_w, pool_scale, conv_w, conv_b, conv_ln_g, conv_ln_b, conv_pw_w,
          conv_pw_b, cmp_pos_k, cmp_pos_v, cmp_k_w1, cmp_k_w2, cmp_v_w1, cmp_v_w2, ln1_g, ln1_b,
          ln2_g, ln2_b, w_gate_up, w_down, out):
    with ExitStack() as ctx:
        def sb(name, shape, dt=F32, where=ctx):
            return where.enter_context(nc.sbuf_tensor(name, shape, dt))

        def sem(name):
            return ctx.enter_context(nc.semaphore(name))

        psum = ctx.enter_context(nc.psum_tensor("psum", [P, 8, SEQ], F32))

        act_hi = sb("act_hi", [P, KT, SEQ], F32R)
        act_lo = sb("act_lo", [P, KT, SEQ], F32R)
        w_hi = sb("w_hi", [P, 2, SLAB], F32R)
        w_lo = sb("w_lo", [P, 2, SLAB], F32R)
        raw = sb("raw", [P, 2, SLAB])
        stats = sb("stats", [P, TT, 4, 6])
        moments = sb("moments", [P, TT, 2])
        rstd = sb("rstd", [P, TT])
        shift = sb("shift", [P, TT])
        std = sb("std", [P, TT])
        ident = sb("ident", [P, P])
        eps = sb("eps", [P, 1])

        mixing = ExitStack()
        with mixing:
            def sbm(name, shape):
                return sb(name, shape, F32, mixing)

            proj = sbm("proj", [P, N_SLOTS, SEQ])
            dist = sbm("dist", [P, SEQ])
            sel = sbm("sel", [P, 9 * P])
            pt = sbm("pt", [P, 2, 13 * P])
            blk = sbm("blk", [P, 2, CMP_BLOCK * CMP_BLOCK])
            cmp_p = sbm("cmp_p", [P, 16 * N_CMP])
            vecs = sbm("vecs", [P, 4, VEC_ROWS])
            pos = sbm("pos", [P, 2 * CMP_BLOCK])
            iwg = sbm("iwg", [P, TT, W_IKW + W_NG])
            cmp_dist = sbm("cmp_dist", [P, TT * N_CMP])
            cmp_kT = sbm("cmp_kT", [P, N_CMP])
            cmp_h = sbm("cmp_h", [P, 2, N_CMP])
            cmp_v = sbm("cmp_v", [N_CMP, P])
            w2 = sbm("w2", [P, 2, P])
            inv_count = sbm("inv_count", [P, 16])
            top8 = sbm("top8", [P, 8])
            row_max = sbm("row_max", [P, RING])
            neg_max = sbm("neg_max", [P, RING])
            row_sum = sbm("row_sum", [P, RING])
            row_inv = sbm("row_inv", [P, RING])
            cmp_m = sbm("cmp_m", [P, 16])
            cmp_r = sbm("cmp_r", [P, 16])
        feed = ExitStack()
        feed_ctx = ctx.enter_context(feed)
        acc = sb("acc", [P, TT, D_MODEL], F32, feed)
        ln_g = sb("ln_g", [P, D_MODEL], F32, feed)
        ln_b = sb("ln_b", [P, D_MODEL], F32, feed)
        h_hi = sb("h_hi", [P, 4, SEQ], F32R, feed)
        h_lo = sb("h_lo", [P, 4, SEQ], F32R, feed)
        silu_g = sb("silu_g", [P, 2, SEQ], F32, feed)
        hid = sb("hid", [P, 2, SEQ], F32, feed)

        x_nat = proj[:, 0:16, :].rearrange("p (i k) s -> p i (k s)", i=TT)
        vec_nat = sel[0:VEC_ROWS, 0:SEQ]
        pos_nat = sel[0:2 * CMP_BLOCK, SEQ:SEQ + P]
        later = cmp_p[:, 0:P]
        ones = cmp_p[:, P:2 * P]
        ik_high = blk[64:128, 0, 0:SEQ]
        relu_ring = pt[:, :, :].rearrange("p a b -> p (a b)")[:, 0:6 * SEQ].rearrange("p (r s) -> p r s", r=6)
        squares = relu_ring
        rstd_conv = proj[:, S_CONV + 3, :]
        tmp_a, tmp_b = blk[:, 0, 0:SEQ], blk[:, 0, SEQ:2 * SEQ]
        cmp_pT = blk[0:N_CMP, :, :].rearrange("c a b -> c (a b)").rearrange("c (h s) -> c h s", h=HEADS)

        spare_slot = (h_hi[:, :, :].rearrange("p k n -> p (k n)"), h_lo[:, :, :].rearrange("p k n -> p (k n)"))
        late_hi = [act_hi[:, 4 * c:4 * c + 4, :].rearrange("p k n -> p (k n)") for c in range(2)]
        late_lo = [act_lo[:, 4 * c:4 * c + 4, :].rearrange("p k n -> p (k n)") for c in range(2)]

        raw_loaded = [sem(f"raw_loaded{i}") for i in range(2)]
        aux_used = sem("aux_used")
        split_begun = sem("split_begun")
        hi_done = sem("hi_done")
        split_done = sem("split_done")
        slab_done = sem("slab_done")
        x_loaded = [sem(f"x_loaded{i}") for i in range(TT)]
        small_loaded = sem("small_loaded")
        const_ready = sem("const_ready")
        ident_ready = sem("ident_ready")
        xt_done = sem("xt_done")
        xt_hi = sem("xt_hi")
        xt_lo = sem("xt_lo")
        bank_free = [sem(f"bank_free{i}") for i in range(2)]
        vec_t = sem("vec_t")
        vec_ready = sem("vec_ready")
        iwg_t = sem("iwg_t")
        iwg_ready = sem("iwg_ready")
        gates_ready = sem("gates_ready")
        ik_dup = sem("ik_dup")
        logit_done = sem("logit_done")
        relu_done = sem("relu_done")
        relu_used = sem("relu_used")
        sig_ready = sem("sig_ready")
        dve = sem("dve")
        conv_out = sem("conv_out")
        channel_sum = sem("channel_sum")
        mean_done = sem("mean_done")
        centred = sem("centred")
        squared = sem("squared")
        var_done = sem("var_done")
        std_ready = sem("std_ready")
        normed = sem("normed")
        silu_ready = sem("silu_ready")
        pw_done = sem("pw_done")
        pool_in = sem("pool_in")
        pool_done = sem("pool_done")
        v_t = sem("v_t")
        v_nat = sem("v_nat")
        blk_ready = sem("blk_ready")
        cmp1_done = sem("cmp1_done")
        gelu_ready = sem("gelu_ready")
        cmp2_done = sem("cmp2_done")
        cmp_kv = sem("cmp_kv")
        cmp_logit = sem("cmp_logit")
        cmp_shift = sem("cmp_shift")
        cmp_exp = sem("cmp_exp")
        cmp_prob = sem("cmp_prob")
        cmp_t = sem("cmp_t")
        cmp_t_ready = sem("cmp_t_ready")
        qk_done = sem("qk_done")
        scored = sem("scored")
        max_ready = sem("max_ready")
        exp_done = sem("exp_done")
        inv_ready = sem("inv_ready")
        prob_ready = sem("prob_ready")
        tr_done = sem("tr_done")
        pt_ready = sem("pt_ready")
        pv_done = sem("pv_done")
        mix_hi = sem("mix_hi")
        mix_split = sem("mix_split")
        piece_hi = sem("piece_hi")
        piece_lo = sem("piece_lo")
        resid_loaded = sem("resid_loaded")
        ln_loaded = sem("ln_loaded")
        tile_done = sem("tile_done")
        tile_added = sem("tile_added")
        var_ready = sem("var_ready")
        std_done = sem("std_done")
        rstd_ready = sem("rstd_ready")
        xn_ready = sem("xn_ready")
        gained = sem("gained")
        gained_pool = sem("gained_pool")
        x1_ready = [sem(f"x1_ready{i}") for i in range(TT)]
        x1_t = sem("x1_t")
        x1_hi = sem("x1_hi")
        x1_lo = sem("x1_lo")
        scaled = sem("scaled")
        silu_done = sem("silu_done")
        hid_ready = sem("hid_ready")
        hid_hi = sem("hid_hi")
        hid_lo = sem("hid_lo")
        y_ready = [sem(f"y_ready{i}") for i in range(TT)]
        stored = sem("stored")

        win = w_in[0].rearrange("(k p) n -> p k n", p=P)
        wout = w_out[0].rearrange("(k p) n -> p k n", p=P)
        wgu = w_gate_up[0].rearrange("(k p) n -> p k n", p=P)
        wdown = w_down[0].rearrange("(k p) n -> p k n", p=P)
        x_dram = x[0].rearrange("(i p) d -> p i d", p=P)
        out_dram = out[0].rearrange("(i p) d -> p i d", p=P)

        N_AUX = 6
        FF0 = N_IN + N_OUT
        TILES0 = 8

        def copied(eng, n):
            eng.wait_ge(bank_free[n % 2], n // 2 + 1)

        def tile_ready(eng, group, slab, i):
            if i < TT - 1:
                eng.wait_ge(tile_done, group * (TT - 1) + (i + 1))
            else:
                eng.wait_ge(slab_done, slab + 1)

        def affine_count(i, half):
            return 1 if half == 0 else i + 2

        def aux_slot(a):
            return (N_IN + a) % 2

        block = ctx.enter_context(nc.Block())

        @block.sync
        def _(sp):
            def load(slot, src, shape_k):
                dst = raw[:, slot, 0:shape_k * (SLAB // shape_k)].rearrange("p (k n) -> p k n", k=shape_k)
                nc.sync.dma_start(dst, src).then_inc(raw_loaded[slot], 16)

            def x_tile(i):
                nc.sync.dma_start(x_nat[:, i, :], x_dram[:, i, :]).then_inc(x_loaded[i], 16)

            load(0, win[:, :, C_IQ:C_IQ + P], KT)
            x_tile(0)
            x_tile(1)
            x_tile(2)
            x_tile(3)
            load(1, win[:, :, C_IQ + P:C_IQ + 2 * P], KT)
            rows = ((conv_w[0], 0, CONV_WIDTH), (conv_b, V_CB, 1), (conv_ln_g, V_LG, 1),
                    (conv_ln_b, V_LB, 1), (conv_pw_b, V_PB, 1), (pool_scale, V_PS, 1))
            for src, at, n in rows:
                nc.sync.dma_start(sel[at:at + n, 0:SEQ], src).then_inc(small_loaded, 16)
            nc.sync.dma_start(sel[0:CMP_BLOCK, SEQ:SEQ + P], cmp_pos_k[0]).then_inc(small_loaded, 16)
            nc.sync.dma_start(sel[CMP_BLOCK:2 * CMP_BLOCK, SEQ:SEQ + P], cmp_pos_v[0]).then_inc(small_loaded, 16)
            nc.sync.dma_start(w2[:, 0, :], cmp_k_w2[0]).then_inc(small_loaded, 16)
            nc.sync.dma_start(w2[:, 1, :], cmp_v_w2[0]).then_inc(small_loaded, 16)

            for n in (2, 3):
                sp.wait_ge(split_done, n - 1)
                load(n % 2, win[:, :, C_IQ + n * P:C_IQ + (n + 1) * P], KT)
            sp.wait_ge(split_done, N_IKWG - 1)
            ikwg = raw[:, 0, 0:KT * (W_IKW + W_NG)].rearrange("p (k n) -> p k n", k=KT)
            nc.sync.dma_start(ikwg[:, :, 0:W_IKW], win[:, :, C_IK:C_IK + W_IKW]).then_inc(raw_loaded[0], 16)
            nc.sync.dma_start(ikwg[:, :, W_IKW:], win[:, :, C_NG:C_NG + W_NG]).then_inc(raw_loaded[0], 16)

            with sp.Fori(0, 4) as c:
                sp.wait_ge(split_done, 2 * c + (N_CONV - 1))
                load(1, win[:, :, bass.ds(c * P + C_G, P)], KT)
                sp.wait_ge(split_done, 2 * c + N_CONV)
                load(0, win[:, :, bass.ds(c * P + C_A, P)], KT)

            def pairs(count, first, column):
                with sp.Fori(0, count) as c:
                    sp.wait_ge(split_done, 2 * c + (first - 1))
                    load(1, win[:, :, bass.ds(c * (2 * P) + column, P)], KT)
                    sp.wait_ge(split_done, 2 * c + first)
                    load(0, win[:, :, bass.ds(c * (2 * P) + (column + P), P)], KT)

            pairs(2, N_POOL, C_POOL)
            pairs(3, N_QKV, C_DQ)
            pairs(5, N_QKV + 6, C_NQ)

            for a in range(N_AUX):
                if a < 2:
                    sp.wait_ge(split_done, N_IN - 1 + a)
                else:
                    sp.wait_ge(aux_used, a - 1)
                slot = (N_IN + a) % 2
                if a < 4:
                    w1 = (cmp_k_w1, cmp_v_w1)[a // 2][0].rearrange("(l d) h -> d l h", d=P)
                    load(slot, w1[:, 16 * (a % 2):16 * (a % 2) + 16, :], 16)
                elif a == 4:
                    load(slot, conv_pw_w[0].rearrange("(k p) n -> p k n", p=P), 4)
                else:
                    nc.sync.dma_start(raw[:, slot, 0:4 * P].rearrange("p (g d) -> p g d", g=4),
                                      pool_w[0].rearrange("g c d -> c g d")).then_inc(raw_loaded[slot], 16)

            for m in range(2):
                sp.wait_ge((pw_done, pool_done)[m], 4)
                load((m + 1) % 2, wout[:, 4 * m:4 * m + 4, 0:SEQ], 4)
            for m in range(2, 4):
                sp.wait_ge(split_done, N_IN + m - 1)
                load((m + 1) % 2, wout[:, 4 * m:4 * m + 4, 0:SEQ], 4)
            sp.wait_ge(mix_split, 16)
            nc.sync.dma_start(acc[:, :, :], x_dram).then_inc(resid_loaded, 16)
            nc.sync.dma_start(ln_g[:, :], ln1_g.to_broadcast([P, D_MODEL])).then_inc(ln_loaded, 16)
            nc.sync.dma_start(ln_b[:, :], ln1_b.to_broadcast([P, D_MODEL])).then_inc(ln_loaded, 16)
            with sp.Fori(1, 4) as n:
                for kq in range(4):
                    sp.wait_ge(split_done, 4 * n + (N_IN + kq - 1))
                    load((kq + 1) % 2, wout[:, 4 * kq:4 * kq + 4, bass.ds(n * SEQ, SEQ)], 4)

            def gate_up(first, chunk):
                for u in range(2):
                    sp.wait_ge(split_done, first + (u - 1))
                    load((u + 1) % 2, wgu[:, :, bass.ds(chunk * P + u * D_FF, P)], KT)

            def down(first, group):
                for n in range(4):
                    sp.wait_ge(split_done, first + (n - 1))
                    load((n + 1) % 2, wdown[:, bass.ds(group * 4, 4), n * SEQ:(n + 1) * SEQ], 4)

            gate_up(FF0, 0)
            sp.wait_ge(split_done, FF0 + 2)
            gate_up(FF0 + 2, 1)
            for i in range(TT):
                sp.wait_ge(x1_ready[i], 1)
            nc.sync.dma_start(ln_g[:, :], ln2_g.to_broadcast([P, D_MODEL])).then_inc(ln_loaded, 16)
            nc.sync.dma_start(ln_b[:, :], ln2_b.to_broadcast([P, D_MODEL])).then_inc(ln_loaded, 16)
            with sp.Fori(0, FF_GROUPS - 1) as g:
                gate_up(g * 12 + (FF0 + 4), g * 4 + 2)
                gate_up(g * 12 + (FF0 + 6), g * 4 + 3)
                gate_up(g * 12 + (FF0 + 8), g * 4 + 4)
                down(g * 12 + (FF0 + 10), g)
                gate_up(g * 12 + (FF0 + 14), g * 4 + 5)
            last = FF0 + 12 * (FF_GROUPS - 1)
            gate_up(last + 4, FF_CHUNKS - 2)
            gate_up(last + 6, FF_CHUNKS - 1)
            down(last + 8, FF_GROUPS - 1)

            def store(i, ready, blocks):
                sp.wait_ge(y_ready[i], ready)
                cols = slice(blocks[0] * SEQ, (blocks[-1] + 1) * SEQ)
                nc.sync.dma_start(out_dram[:, i, cols], acc[:, i, cols]).then_inc(stored, 16)

            stores = ((0, 2, (0, 1, 2, 3)), (1, 2, (0, 1, 2, 3)), (2, 1, (0, 1)), (3, 1, (0,)), (3, 2, (1,)),
                      (2, 2, (2, 3)), (3, 3, (2,)), (3, 4, (3,)))
            for i, ready, blocks in stores:
                store(i, ready, blocks)
            sp.wait_ge(stored, 16 * len(stores))

        @block.gpsimd
        def _(pool):
            nc.gpsimd.memset(ident[:, :], 0.0).then_inc(const_ready, 1)
            pool.wait_ge(const_ready, 1)
            nc.gpsimd.affine_select(out=ident[:, :], in_=ident[:, :], compare_op=ALU.not_equal, fill=1.0,
                                    base=0, pattern=[[-1, P]], channel_multiplier=1).then_inc(ident_ready, 1)

            def split(slot, loads, n, words=SLAB, dst=None, used=-1):
                hi, lo = dst or (w_hi[:, slot, 0:words], w_lo[:, slot, 0:words])
                pool.wait_ge(raw_loaded[slot], loads)
                if used == -1 and not (isinstance(n, int) and n < 2):
                    used = n - 1
                if not (isinstance(used, int) and used <= 0):
                    pool.wait_ge(slab_done, used)
                nc.gpsimd.sem_inc(split_begun, 1)
                nc.gpsimd.tensor_scalar(hi, raw[:, slot, 0:words], 1.0, 1.0, ALU.mult, ALU.mult)\
                    .then_inc(hi_done, 1)
                pool.wait_ge(hi_done, n + 1)
                nc.gpsimd.tensor_tensor(lo, raw[:, slot, 0:words], hi.bitcast(F32), ALU.subtract)\
                    .then_inc(split_done, 1)

            split(0, 16, 0)
            nc.gpsimd.iota(dist[:, :], pattern=[[1, SEQ]], base=-(SEQ - P), channel_multiplier=-1,
                           allow_small_or_imprecise_dtypes=True).then_inc(const_ready, 1)
            pool.wait_ge(const_ready, 2)
            nc.gpsimd.affine_select(out=dist[:, :], in_=dist[:, :], compare_op=ALU.is_ge, fill=MASKED,
                                    base=SEQ - P, pattern=[[-1, SEQ]], channel_multiplier=1).then_inc(const_ready, 1)
            nc.gpsimd.iota(cmp_dist[:, :], pattern=[[-P, TT], [CMP_STRIDE, N_CMP]], base=CMP_BLOCK - 1,
                           channel_multiplier=-1, allow_small_or_imprecise_dtypes=True).then_inc(const_ready, 1)
            pool.wait_ge(const_ready, 4)
            nc.gpsimd.affine_select(out=cmp_dist[:, :], in_=cmp_dist[:, :], compare_op=ALU.is_ge, fill=MASKED,
                                    base=-(CMP_BLOCK - 1), pattern=[[P, TT], [-CMP_STRIDE, N_CMP]],
                                    channel_multiplier=1).then_inc(const_ready, 1)
            nc.gpsimd.memset(later[:, :], 0.0).then_inc(const_ready, 1)
            nc.gpsimd.memset(ones[:, :], 1.0 / SEQ).then_inc(const_ready, 1)
            nc.gpsimd.memset(eps[:, :], LN_EPS).then_inc(const_ready, 1)
            nc.gpsimd.iota(inv_count[:, :], pattern=[[1, 16]], base=1, channel_multiplier=0,
                           allow_small_or_imprecise_dtypes=True).then_inc(const_ready, 1)
            pool.wait_ge(const_ready, 6)
            nc.gpsimd.affine_select(out=later[:, :], in_=later[:, :], compare_op=ALU.is_ge, fill=MASKED,
                                    base=0, pattern=[[-1, P]], channel_multiplier=1).then_inc(const_ready, 1)

            split(1, 16, 1)
            split(0, 32, 2)
            split(1, 32, 3)
            split(0, 64, N_IKWG, KT * (W_IKW + W_NG))
            with pool.Fori(0, (N_IN - N_CONV) // 2) as c:
                split(1, c * 16 + 48, 2 * c + N_CONV)
                split(0, c * 16 + 80, 2 * c + (N_CONV + 1))

            odd = 16 * (N_IN // 2 + N_AUX // 2)
            even = 16 * (N_IN // 2 + 2 + N_AUX // 2)

            def normalise(g):
                u, i = g // TT, g % TT
                p = proj[:, T_SLOTS[g % RING], 0:(i + 1) * P]
                inv = row_inv[:, g % RING:g % RING + 1]
                pool.wait_ge(inv_ready, g + 1)
                if u < HEADS:
                    ins = nc.gpsimd.tensor_scalar(p, p, inv, 1.0, ALU.mult, ALU.mult)
                else:
                    col = W_IKW + 3 * ((u - HEADS) // 2) + 1 + (u - HEADS) % 2
                    ins = nc.gpsimd.tensor_scalar(p, p, inv, iwg[:, i, col:col + 1], ALU.mult, ALU.mult)
                ins.then_inc(prob_ready, 1)

            def split_piece(m, c):
                slot, cols = (m + 1) % 2, slice(c * SLAB // 4, (c + 1) * SLAB // 4)
                n_piece = 4 * m + c + 1
                if c == 0:
                    pool.wait_ge(raw_loaded[slot], (even, odd)[slot] + 16)
                    pool.wait_ge(slab_done, N_IN)
                nc.gpsimd.tensor_scalar(w_hi[:, slot, cols], raw[:, slot, cols], 1.0, 1.0,
                                        ALU.mult, ALU.mult).then_inc(piece_hi, 1)
                pool.wait_ge(piece_hi, n_piece)
                nc.gpsimd.tensor_tensor(w_lo[:, slot, cols], raw[:, slot, cols],
                                        w_hi[:, slot, cols].bitcast(F32), ALU.subtract).then_inc(piece_lo, 1)
                if c == 3:
                    pool.wait_ge(piece_lo, n_piece)
                    nc.gpsimd.sem_inc(hi_done, 1)
                    nc.gpsimd.sem_inc(split_done, 1)

            pool.wait_ge(gates_ready, 1)
            for g in range(N_TILES):
                normalise(g)
                if g >= TT and g % TT == 0 and g <= 8 * TT:
                    split_piece((g // TT - 1) // 4, (g // TT - 1) % 4)

            def split_pairs(first, end):
                with pool.Fori(first, end) as c:
                    split(1, c * 16 + (odd + 16), 2 * c + N_IN)
                    split(0, c * 16 + (even + 16), 2 * c + (N_IN + 1))

            def apply_gain(i, half):
                pool.wait_ge(xn_ready, affine_count(i, half))
                nc.gpsimd.tensor_tensor(acc[:, i, :], acc[:, i, :], ln_g[:, :], ALU.mult).then_inc(gained_pool, 1)

            def add_bias(i, done):
                if i == 0:
                    pool.wait_ge(gained_pool, 2)
                else:
                    pool.wait_ge(gained, i)
                for h in range(2):
                    cols = slice(h * D_MODEL // 2, (h + 1) * D_MODEL // 2)
                    nc.gpsimd.tensor_tensor(acc[:, i, cols], acc[:, i, cols], ln_b[:, cols], ALU.add)\
                        .then_inc(done[i], 1)

            ff_pair = N_OUT // 2
            split_pairs(1, ff_pair - 1)
            split(1, odd + 16 * ff_pair, FF0 - 2)
            split(0, even + 16 * ff_pair, FF0 - 1, dst=spare_slot, used=0)
            split(0, even + 16 * (ff_pair + 1), FF0, used=FF0 - 2)
            split(1, odd + 16 * (ff_pair + 1), FF0 + 1, used=FF0)
            apply_gain(TT - 1, 0)
            pairs = (N_OUT + 12 * FF_GROUPS) // 2
            split_pairs(ff_pair + 1, pairs - 1)
            n_late = N_IN + 2 * (pairs - 1)
            for c, loads in ((0, odd + 16 * pairs), (1, even + 16 * pairs)):
                split(1 - c, loads, n_late + c, dst=(late_hi[c], late_lo[c]), used=n_late - 2)
            apply_gain(0, 1)
            for i in range(TT - 1):
                add_bias(i, y_ready)

        @block.tensor
        def _(pe):
            def passes(out_ap, stat_hi, stat_lo, mov_hi, mov_lo, first, last):
                nc.tensor.matmul(out_ap, stat_hi, mov_hi, start=first, stop=False)
                nc.tensor.matmul(out_ap, stat_hi, mov_lo, start=False, stop=False)
                return nc.tensor.matmul(out_ap, stat_lo, mov_hi, start=False, stop=last)

            pe.wait_ge(ident_ready, 1)

            def turn_x(i):
                pe.wait_ge(x_loaded[i], 16)
                for q in range(4):
                    g = 4 * i + q
                    if g >= 6:
                        pe.wait_ge(xt_lo, g - 5)
                    for k in range(4):
                        mm = nc.tensor.transpose(psum[:, 2 + g % 6, k * P:(k + 1) * P],
                                                 x_nat[:, i, (4 * q + k) * P:(4 * q + k + 1) * P], ident[:, :])
                    mm.then_inc(xt_done, 1)

            def feature_slab(bank, slot, ready, m=P):
                pe.wait_ge(split_done, ready)
                for k in range(KT):
                    cols = slice(k * m, (k + 1) * m)
                    mm = passes(psum[0:m, bank, :], w_hi[:, slot, cols], w_lo[:, slot, cols],
                                act_hi[:, k, :], act_lo[:, k, :], k == 0, k == KT - 1)
                return mm

            def proj_slab(n, m=P, free=None):
                parity = n % 2 if isinstance(n, int) else None
                if free is not None:
                    pe.wait_ge(bank_free[parity], free)
                feature_slab(parity, parity, n + 1, m).then_inc(slab_done, 1)

            def proj_pairs(first, count):
                with pe.Fori(0, count) as c:
                    for b in (1, 0):
                        pe.wait_ge(bank_free[b], c + ((first - 1) // 2 + (1 - b)))
                        feature_slab(b, b, 2 * c + (first + 2 - b)).then_inc(slab_done, 1)

            half_toks = SEQ // 2
            turn_x(0)
            turn_x(1)
            for half in range(2):
                pe.wait_ge(xt_lo, 8 * half + 8)
                pe.wait_ge(split_done, 1)
                toks = slice(half * half_toks, (half + 1) * half_toks)
                for k in range(KT):
                    cols = slice(k * P, (k + 1) * P)
                    mm = passes(psum[:, 0, toks], w_hi[:, 0, cols], w_lo[:, 0, cols],
                                act_hi[:, k, toks], act_lo[:, k, toks], k == 0, k == KT - 1)
                    if half == 0 and k in (KT // 2 - 1, 3 * KT // 4 - 1):
                        turn_x(2 if k < KT // 2 else 3)
            mm.then_inc(slab_done, 1)
            proj_slab(1)
            proj_slab(2, free=1)
            proj_slab(3, free=1)
            proj_slab(N_IKWG, m=W_IKW + W_NG, free=2)

            pe.wait_ge(small_loaded, 16 * 10)
            for c in range(4):
                nc.tensor.transpose(psum[:, 7, c * VEC_ROWS:(c + 1) * VEC_ROWS],
                                    sel[0:VEC_ROWS, c * P:(c + 1) * P], ident[0:VEC_ROWS, 0:VEC_ROWS])
            nc.tensor.transpose(psum[:, 7, 4 * VEC_ROWS:4 * VEC_ROWS + 2 * CMP_BLOCK], pos_nat,
                                ident[0:2 * CMP_BLOCK, 0:2 * CMP_BLOCK]).then_inc(vec_t, 1)

            proj_pairs(N_CONV, 2)

            width = W_IKW + W_NG
            copied(pe, N_IKWG)
            for i in range(TT):
                mm = nc.tensor.transpose(psum[:, 6, i * width:(i + 1) * width],
                                         proj[0:width, S_IKWG, i * P:(i + 1) * P], ident[0:width, 0:width])
            mm.then_inc(iwg_t, 1)
            pe.wait_ge(ik_dup, 16)
            for e in range(3 * IDX_HEADS):
                i, h = e // IDX_HEADS + 1, e % IDX_HEADS
                if e >= 4:
                    pe.wait_ge(relu_done, e - 3)
                half = slice(64 * (h % 2), 64 * (h % 2) + 64)
                keys = proj[0:64, S_IKWG, 0:(i + 1) * P] if h % 2 == 0 else ik_high[:, 0:(i + 1) * P]
                nc.tensor.matmul(psum[:, 2 + e % 4, 0:(i + 1) * P], proj[half, S_IQ + h // 2, i * P:(i + 1) * P],
                                 keys, start=True, stop=True).then_inc(logit_done, 1)

            proj_pairs(N_CONV + 4, 11)
            pe.wait_ge(channel_sum, 1)
            nc.tensor.matmul(psum[:, 2, :], ones[:, :], tmp_a, start=True, stop=True).then_inc(mean_done, 1)
            proj_pairs(N_CONV + 26, 1)
            pe.wait_ge(channel_sum, 2)
            nc.tensor.matmul(psum[:, 3, :], ones[:, :], squares[:, 0, :], start=True, stop=True).then_inc(var_done, 1)

            for v, slot in enumerate((S_DV, S_SV, S_WV)):
                copied(pe, SLAB_OF[slot])
                for j in range(TT):
                    mm = nc.tensor.transpose(psum[:, 4 + v, j * P:(j + 1) * P], proj[:, slot, j * P:(j + 1) * P],
                                             ident[:, :])
                mm.then_inc(v_t, 1)

            def aux_wait(a):
                slot = aux_slot(a)
                pe.wait_ge(raw_loaded[slot], 16 * (N_IN // 2 + (2 if slot == 0 else 0) + a // 2 + 1))
                return slot

            copied(pe, N_IN - 1)
            copied(pe, N_IN - 2)
            for a in range(4):
                slot, kv = aux_wait(a), a // 2
                pe.wait_ge(blk_ready, 2 * kv + 2)
                for l in range(16):
                    row = 16 * (a % 2) + l
                    mm = nc.tensor.matmul(psum[:, kv, 0:N_CMP], raw[:, slot, l * P:(l + 1) * P],
                                          blk[:, kv, row * CMP_BLOCK:row * CMP_BLOCK + N_CMP],
                                          start=row == 0, stop=row == CMP_BLOCK - 1)
                mm.then_inc(aux_used, 1)
            slot = aux_wait(4)
            pe.wait_ge(silu_ready, 4)
            pe.wait_ge(v_nat, 3)
            for m in range(4):
                for c in range(4):
                    mm = nc.tensor.matmul(psum[:, PW_BANKS[m], :],
                                          raw[:, slot, c * SEQ + m * P:c * SEQ + (m + 1) * P],
                                          proj[:, CONV_OUT[c], :], start=c == 0, stop=c == 3)
                mm.then_inc(pw_done, 1)
            slot = aux_wait(5)
            for g in range(4):
                pe.wait_ge(pool_in, g + 1)
                if g >= 2:
                    pe.wait_ge(mix_split, 4 + g - 1)
                mm = nc.tensor.matmul(psum[:, 4 + g % 2, :], raw[:, slot, g * P:(g + 1) * P],
                                      proj[:, S_POOL + g, :], start=True, stop=True)
                mm.then_inc(pool_done, 1)
            pe.wait_ge(gelu_ready, 2)
            nc.tensor.matmul(psum[:, 0, 64:64 + N_CMP], w2[:, 0, :], cmp_h[:, 0, :], start=True, stop=True)
            nc.tensor.matmul(psum[0:N_CMP, 1, P:2 * P], cmp_h[:, 1, :], w2[:, 1, :],
                             start=True, stop=True).then_inc(cmp2_done, 1)
            pe.wait_ge(cmp_kv, 2)
            for e in range(HEADS * TT):
                h, i = e // TT, e % TT
                mm = nc.tensor.matmul(psum[:, 0, e * N_CMP:(e + 1) * N_CMP],
                                      proj[:, S_NQ + h, i * P:(i + 1) * P], cmp_kT[:, :], start=True, stop=True)
            mm.then_inc(cmp_logit, 1)

            def scores(g):
                q, k, _, _ = UNITS[g // TT]
                i = g % TT
                if g < 2:
                    pe.wait_ge(mix_split, 4)
                else:
                    pe.wait_ge(scored, g - 1)
                nc.tensor.matmul(psum[:, 2 + g % 2, 0:(i + 1) * P], proj[:, q, i * P:(i + 1) * P],
                                 proj[:, k, 0:(i + 1) * P], start=True, stop=True).then_inc(qk_done, 1)

            def turn(g):
                i = g % TT
                pe.wait_ge(prob_ready, g + 1)
                if g < 2:
                    pe.wait_ge(mix_split, 8)
                else:
                    pe.wait_ge(pt_ready, g - 1)
                for j in range(i + 1):
                    mm = nc.tensor.transpose(psum[:, 4 + g % 2, j * P:(j + 1) * P],
                                             proj[:, T_SLOTS[g % RING], j * P:(j + 1) * P], ident[:, :])
                mm.then_inc(tr_done, 1)

            def weigh(u):
                v = UNITS[u][2]
                o = head_of(u)
                opens = u < HEADS or (u - HEADS) % 2 == 0
                pe.wait_ge(pt_ready, TT * (u + 1))
                if opens and o >= 2:
                    pe.wait_ge(mix_split, 7 + o)
                for j in range(TT):
                    mm = nc.tensor.matmul(psum[:, 6 + o % 2, j * P:SEQ], proj[:, v, j * P:(j + 1) * P],
                                          pt[:, u % 2, 4 * j * P:4 * j * P + (TT - j) * P],
                                          start=opens and j == 0, stop=u < HEADS and j == TT - 1)
                if u >= HEADS and closes_head(u):
                    pe.wait_ge(cmp_t_ready, HEADS)
                    mm = nc.tensor.matmul(psum[:, 6 + o % 2, :], cmp_v[:, :], cmp_pT[:, o - HEADS, :],
                                          start=False, stop=True)
                mm.then_inc(pv_done, 1)

            for g in range(N_TILES + WEIGH_LAG):
                if g < N_TILES:
                    scores(g)
                if TURN_LAG <= g < N_TILES + TURN_LAG:
                    turn(g - TURN_LAG)
                if g >= WEIGH_LAG and (g - WEIGH_LAG) % TT == TT - 1:
                    weigh((g - WEIGH_LAG) // TT)
                if g == HEADS * TT:
                    pe.wait_ge(cmp_prob, 1)
                    for h in range(HEADS):
                        if h >= 2:
                            pe.wait_ge(cmp_t_ready, h - 1)
                        for i in range(TT):
                            e = h * TT + i
                            mm = nc.tensor.matmul(psum[0:N_CMP, h % 2, i * P:(i + 1) * P],
                                                  cmp_p[:, e * N_CMP:(e + 1) * N_CMP], ident[:, :],
                                                  start=True, stop=True)
                        mm.then_inc(cmp_t, 1)

            pe.wait_ge(mix_split, 16)
            nc.tensor.sem_inc(tile_added, TILES0)

            def token_slabs(bank0, slots, first, hi, lo, tiles, added, stops=True):
                for s, slot in enumerate(slots):
                    pe.wait_ge(split_done, first + (s + 1))
                    for i in range(TT):
                        if s == 0:
                            pe.wait_ge(tile_added, added + (i + 1))
                        for k in range(4):
                            t = tiles * s + k
                            toks, cols = slice(i * P, (i + 1) * P), slice(k * SEQ, (k + 1) * SEQ)
                            out_ap = psum[:, bank0 + i, :]
                            first_mm = s == 0 and k == 0
                            last_mm = stops and s == len(slots) - 1 and k == 3
                            nc.tensor.matmul(out_ap, hi[:, t, toks], w_hi[:, slot, cols], start=first_mm, stop=False)
                            nc.tensor.matmul(out_ap, lo[:, t, toks], w_hi[:, slot, cols], start=False, stop=False)
                            mm = nc.tensor.matmul(out_ap, hi[:, t, toks], w_lo[:, slot, cols],
                                                  start=False, stop=last_mm)
                        if i == TT - 1:
                            mm.then_inc(slab_done, 1)
                        elif stops and s == len(slots) - 1:
                            mm.then_inc(tile_done, 1)

            for n in range(3):
                token_slabs(4 * (n % 2), (1, 0, 1, 0), N_IN + 4 * n, act_hi, act_lo, 4, 4 * n)
            token_slabs(4, (1, 0), N_IN + 12, act_hi, act_lo, 4, 12, stops=False)

            def turn_x1(i):
                pe.wait_ge(x1_ready[i], 1)
                for q in range(4):
                    e = 4 * i + q
                    if e >= 6:
                        pe.wait_ge(x1_lo, e - 5)
                    elif e >= 4:
                        pe.wait_ge(tile_added, TILES0 + 12 + (e - 2) + 1)
                    for k in range(4):
                        mm = nc.tensor.transpose(psum[:, X1_BANKS[e % 6], k * P:(k + 1) * P],
                                                 acc[:, i, (4 * q + k) * P:(4 * q + k + 1) * P], ident[:, :])
                    mm.then_inc(x1_t, 1)

            last_slabs = ((8, w_hi[:, 1, :], w_lo[:, 1, :]), (12,) + spare_slot)
            pe.wait_ge(split_done, FF0 - 1)
            for i in range(TT):
                if i == TT - 1:
                    turn_x1(0)
                for s, (t, w_h, w_l) in enumerate(last_slabs):
                    if s == 1:
                        pe.wait_ge(split_done, FF0)
                    for k in range(4):
                        toks, cols = slice(i * P, (i + 1) * P), slice(k * SEQ, (k + 1) * SEQ)
                        out_ap = psum[:, 4 + i, :]
                        nc.tensor.matmul(out_ap, act_hi[:, t + k, toks], w_h[:, cols], start=False, stop=False)
                        nc.tensor.matmul(out_ap, act_lo[:, t + k, toks], w_h[:, cols], start=False, stop=False)
                        mm = nc.tensor.matmul(out_ap, act_hi[:, t + k, toks], w_l[:, cols],
                                              start=False, stop=s == 1 and k == 3)
                    if i == TT - 1:
                        mm.then_inc(slab_done, 1)
                    elif s == 1:
                        mm.then_inc(tile_done, 1)

            def hidden(j, first, free=None):
                if free is not None:
                    pe.wait_ge(hid_ready, free)
                for u in range(2):
                    feature_slab(4 + 2 * (j % 2) + u, (u + 1) % 2, first + (u + 1)).then_inc(slab_done, 1)

            def down(first, group):
                pe.wait_ge(hid_lo, group * 4 + 4)
                for n in range(4):
                    token_slabs(0, ((n + 1) % 2,), first + n, h_hi, h_lo, 0,
                                group * 16 + (4 * n + TILES0 + 4 * 4 - 4))

            turn_x1(1)
            for half in range(2):
                pe.wait_ge(x1_lo, 8 * half + 8)
                toks = slice(half * half_toks, (half + 1) * half_toks)
                for v in range(2):
                    u = 1 - v if half == 0 else v
                    pe.wait_ge(split_done, FF0 + 1 + v)
                    for k in range(KT):
                        cols = slice(k * P, (k + 1) * P)
                        mm = passes(psum[:, 4 + u, toks], w_hi[:, 1 - u, cols], w_lo[:, 1 - u, cols],
                                    act_hi[:, k, toks], act_lo[:, k, toks], k == 0, k == KT - 1)
                        if half == 0 and v == 1 and k in (KT // 2 - 1, 3 * KT // 4 - 1):
                            turn_x1(2 if k < KT // 2 else 3)
                    if half == 1:
                        mm.then_inc(slab_done, 1)
            hidden(1, FF0 + 2)
            with pe.Fori(0, FF_GROUPS - 1) as g:
                hidden(2, g * 12 + (FF0 + 4), g * 4 + 1)
                hidden(3, g * 12 + (FF0 + 6), g * 4 + 2)
                hidden(4, g * 12 + (FF0 + 8), g * 4 + 3)
                down(g * 12 + (FF0 + 10), g)
                hidden(5, g * 12 + (FF0 + 14), g * 4 + 4)
            last = FF_GROUPS - 1
            hidden(2, 12 * last + FF0 + 4, 4 * last + 1)
            hidden(3, 12 * last + FF0 + 6, 4 * last + 2)
            first = 12 * last + FF0 + 8
            added = 16 * last + TILES0 + 16

            def token_tile(bank, i, w_h, w_l, ks):
                toks = slice(i * P, (i + 1) * P)
                for k in ks:
                    cols = slice(k * SEQ, (k + 1) * SEQ)
                    out_ap = psum[:, bank, :]
                    nc.tensor.matmul(out_ap, h_hi[:, k, toks], w_h[:, cols], start=k == 0, stop=False)
                    nc.tensor.matmul(out_ap, h_lo[:, k, toks], w_h[:, cols], start=False, stop=False)
                    mm = nc.tensor.matmul(out_ap, h_hi[:, k, toks], w_l[:, cols], start=False, stop=k == 3)
                return mm

            for n in range(2):
                slot = (n + 1) % 2
                pe.wait_ge(split_done, first + n + 1)
                for ks in ((0, 1, 2), (3,)):
                    pe.wait_ge(hid_lo, 4 * last + ks[-1] + 1)
                    for i in range(TT):
                        if ks[0] == 0:
                            pe.wait_ge(tile_added, added + 4 * n - 4 + i + 1)
                        mm = token_tile(i, i, w_hi[:, slot, :], w_lo[:, slot, :], ks)
                        if ks[0] == 3:
                            mm.then_inc(tile_done if i < TT - 1 else slab_done, 1)
            for i in range(TT):
                for n in (2, 3):
                    pe.wait_ge(split_done, first + n + 1)
                    if n == 2:
                        pe.wait_ge(tile_added, added + 4 + i + 1)
                    token_tile(4 * (n - 2) + i, i, late_hi[n - 2], late_lo[n - 2], range(4))\
                        .then_inc(tile_done if i < TT - 1 else slab_done, 1)

        @block.scalar
        def _(act):
            for i in range(TT):
                for q in range(4):
                    g = 4 * i + q
                    act.wait_ge(xt_done, g + 1)
                    nc.scalar.copy(act_hi[:, 4 * q:4 * q + 4, i * P:(i + 1) * P],
                                   psum[:, 2 + g % 6, :].rearrange("p (k s) -> p k s", k=4)).then_inc(xt_hi, 1)

            def copy_out(n, slot, scale=1.0, rows=P):
                act.wait_ge(slab_done, n + 1)
                nc.scalar.activation(proj[0:rows, slot, :], psum[0:rows, n % 2, :], ACT.Copy,
                                     scale=scale).then_inc(bank_free[n % 2], 1)

            def conv_gate(c):
                n = N_CONV + 2 * c
                act.wait_ge(slab_done, n + 1)
                nc.scalar.activation(proj[:, S_CONV + c, :], psum[:, n % 2, :], ACT.Sigmoid)\
                    .then_inc(bank_free[n % 2], 1)

            for n in range(4):
                copy_out(n, S_IQ + n)
            copy_out(N_IKWG, S_IKWG, rows=W_IKW + W_NG)
            copied(act, N_IKWG)
            nc.scalar.dma_start(ik_high, proj[0:64, S_IKWG, :]).then_inc(ik_dup, 16)
            conv_gate(0)
            conv_gate(1)
            act.wait_ge(iwg_ready, 2)
            nc.scalar.activation(iwg[:, :, W_IKW:], iwg[:, :, W_IKW:], ACT.Sigmoid).then_inc(gates_ready, 1)
            for e in range(3 * IDX_HEADS):
                w = (e // IDX_HEADS + 2) * P
                act.wait_ge(logit_done, e + 1)
                if e >= 6:
                    act.wait_ge(relu_used, e - 5)
                nc.scalar.activation(relu_ring[:, e % 6, 0:w], psum[:, 2 + e % 4, 0:w], ACT.Relu)\
                    .then_inc(relu_done, 1)
            conv_gate(2)
            conv_gate(3)
            for g in range(4):
                copy_out(N_POOL + g, S_POOL + g)
            for s in range(14):
                scale = 1.0
                if s < 4:
                    scale = ATTN_SCALE / SLOPES_DSA[s]
                elif 6 <= s < 10:
                    scale = ATTN_SCALE / SLOPES_NSA[s - 6]
                copy_out(N_QKV + s, S_DQ + s, scale)
            for c in range(4):
                act.wait_ge(centred, c + 1)
                nc.scalar.activation(squares[:, c, :], proj[:, CONV_OUT[c], :], ACT.Square).then_inc(squared, 1)
            for s in range(14, 16):
                copy_out(N_QKV + s, S_DQ + s)
            act.wait_ge(var_done, 1)
            act.wait_ge(conv_out, 4)
            nc.scalar.activation(rstd_conv, psum[:, 3, :], ACT.Sqrt, bias=eps[:, :]).then_inc(std_ready, 1)
            for c in range(4):
                act.wait_ge(normed, c + 1)
                nc.scalar.activation(proj[:, CONV_OUT[c], :], proj[:, CONV_OUT[c], :], ACT.Silu,
                                     bias=vecs[:, c, V_LB:V_LB + 1],
                                     scale=vecs[:, c, V_LG:V_LG + 1]).then_inc(silu_ready, 1)
            for v, slot in enumerate((S_DV, S_SV, S_WV)):
                act.wait_ge(v_t, v + 1)
                nc.scalar.copy(proj[:, slot, :], psum[:, 4 + v, :]).then_inc(v_nat, 1)
            for kv in range(2):
                act.wait_ge(aux_used, 2 * kv + 2)
                nc.scalar.activation(cmp_h[:, kv, :], psum[:, kv, 0:N_CMP], ACT.Gelu_apprx_tanh)\
                    .then_inc(gelu_ready, 1)
            act.wait_ge(pw_done, 4)
            for m in range(4):
                nc.scalar.activation(act_hi[:, MIX_ORDER[m], :], psum[:, PW_BANKS[m], :], ACT.Identity,
                                     bias=vecs[:, m, V_PB:V_PB + 1]).then_inc(mix_hi, 1)
            for g in range(4):
                act.wait_ge(pool_done, g + 1)
                nc.scalar.activation(act_hi[:, MIX_ORDER[4 + g], :], psum[:, 4 + g % 2, :], ACT.Copy,
                                     scale=vecs[:, g, V_PS:V_PS + 1]).then_inc(mix_hi, 1)

            act.wait_ge(cmp_shift, 1)
            for h in range(HEADS):
                cols = slice(h * TT * N_CMP, (h + 1) * TT * N_CMP)
                nc.scalar.activation(cmp_p[:, cols], cmp_p[:, cols], ACT.Exp, scale=SLOPES_NSA[h])\
                    .then_inc(cmp_exp, 1)

            def exponentials(g):
                u, w = g // TT, (g % TT + 1) * P
                act.wait_ge(max_ready, g + 1)
                nc.scalar.activation(proj[:, T_SLOTS[g % RING], 0:w], proj[:, T_SLOTS[g % RING], 0:w], ACT.Exp,
                                     bias=neg_max[:, g % RING:g % RING + 1], scale=UNITS[u][3],
                                     accum_out=row_sum[:, g % RING:g % RING + 1]).then_inc(exp_done, 1)

            def turned(g):
                u, i = g // TT, g % TT
                act.wait_ge(tr_done, g + 1)
                if i == 0 and u >= 2:
                    act.wait_ge(pv_done, u - 1)
                dst = pt[:, u % 2, :].rearrange("p (b s) -> p b s", s=P)[:, i:i + 3 * i + 1:3, :]
                nc.scalar.copy(dst, psum[:, 4 + g % 2, 0:(i + 1) * P].rearrange("p (b s) -> p b s", s=P))\
                    .then_inc(pt_ready, 1)

            def head_out(u):
                if closes_head(u):
                    o = head_of(u)
                    act.wait_ge(pv_done, u + 1)
                    nc.scalar.copy(act_hi[:, MIX_ORDER[8 + o], :], psum[:, 6 + o % 2, :]).then_inc(mix_hi, 1)

            for g in range(N_TILES + OUT_LAG):
                if TURN_LAG <= g < N_TILES + TURN_LAG:
                    turned(g - TURN_LAG)
                if g < N_TILES:
                    exponentials(g)
                if g >= OUT_LAG and (g - OUT_LAG) % TT == TT - 1:
                    head_out((g - OUT_LAG) // TT)

            def deviation(i, half):
                act.wait_ge(var_ready, TT * half + i + 1)
                nc.scalar.activation(std[:, i:i + 1], moments[:, i, 1:2], ACT.Sqrt, bias=eps[:, :])\
                    .then_inc(std_done, 1)

            def normal(i, half):
                act.wait_ge(rstd_ready, TT * half + i + 1)
                nc.scalar.activation(acc[:, i, :], acc[:, i, :], ACT.Identity, bias=shift[:, i:i + 1],
                                     scale=rstd[:, i:i + 1]).then_inc(xn_ready, 1)

            def x1_high(i):
                for q in range(4):
                    e = 4 * i + q
                    act.wait_ge(x1_t, e + 1)
                    nc.scalar.copy(act_hi[:, 4 * q:4 * q + 4, i * P:(i + 1) * P],
                                   psum[:, X1_BANKS[e % 6], :].rearrange("p (k s) -> p k s", k=4)).then_inc(x1_hi, 1)

            deviation(0, 0)
            deviation(1, 0)
            x1_high(0)
            deviation(2, 0)
            x1_high(1)
            deviation(3, 0)
            normal(3, 0)
            x1_high(2)
            x1_high(3)
            for i in range(TT):
                nc.scalar.mul(acc[:, i, :], acc[:, i, :], ALPHA).then_inc(scaled, 1)

            def gate(j, q, slab):
                act.wait_ge(slab_done, slab + 1)
                if not isinstance(q, int) or q >= 2:
                    act.wait_ge(hid_ready, q - 1)
                nc.scalar.activation(silu_g[:, j % 2, :], psum[:, 4 + 2 * (j % 2), :], ACT.Silu).then_inc(silu_done, 1)

            def hidden_hi(j, q):
                act.wait_ge(hid_ready, q + 1)
                nc.scalar.copy(h_hi[:, j % 4, :], hid[:, j % 2, :]).then_inc(hid_hi, 1)

            gate(0, 0, FF0)
            hidden_hi(0, 0)
            gate(1, 1, FF0 + 2)
            hidden_hi(1, 1)
            with act.Fori(0, FF_GROUPS - 1) as g:
                for j in (2, 3):
                    gate(j, g * 4 + j, g * 12 + (FF0 + 2 * j))
                    hidden_hi(j, g * 4 + j)
                gate(4, g * 4 + 4, g * 12 + (FF0 + 8))
                act.wait_ge(slab_done, g * 12 + (FF0 + 14))
                hidden_hi(4, g * 4 + 4)
                gate(5, g * 4 + 5, g * 12 + (FF0 + 14))
                hidden_hi(5, g * 4 + 5)
            last = FF_GROUPS - 1
            for j in (2, 3):
                gate(j, 4 * last + j, 12 * last + FF0 + 2 * j)
                hidden_hi(j, 4 * last + j)
            for i in range(TT):
                deviation(i, 1)
                if i < TT - 1:
                    normal(i, 1)

        @block.vector
        def _(ve):
            chain = [0]

            def link(ins):
                chain[0] += 1
                ins.then_inc(dve, 1)
                ve.wait_ge(dve, chain[0])

            for i in range(TT):
                for q in range(4):
                    g = 4 * i + q
                    here = (slice(None), slice(4 * q, 4 * q + 4), slice(i * P, (i + 1) * P))
                    ve.wait_ge(xt_hi, g + 1)
                    nc.vector.tensor_tensor(act_lo[here], psum[:, 2 + g % 6, :].rearrange("p (k s) -> p k s", k=4),
                                            act_hi[here].bitcast(F32), ALU.subtract).then_inc(xt_lo, 1)
            ve.wait_ge(const_ready, 10)
            link(nc.vector.reciprocal(inv_count[:, :], inv_count[:, :]))
            ve.wait_ge(vec_t, 1)
            nc.vector.tensor_copy(vecs[:, :, :].rearrange("p c v -> p (c v)"), psum[:, 7, 0:4 * VEC_ROWS])\
                .then_inc(vec_ready, 1)
            nc.vector.tensor_copy(pos[:, :], psum[:, 7, 4 * VEC_ROWS:4 * VEC_ROWS + 2 * CMP_BLOCK])\
                .then_inc(vec_ready, 1)

            def conv_value(c):
                n = N_CONV + 2 * c + 1
                copied(ve, n - 1)
                ve.wait_ge(slab_done, n + 1)
                nc.vector.tensor_tensor(proj[:, S_CONV + c, :], psum[:, n % 2, :], proj[:, S_CONV + c, :],
                                        ALU.mult).then_inc(bank_free[n % 2], 1)

            conv_value(0)
            conv_value(1)
            ve.wait_ge(iwg_t, 1)
            nc.vector.tensor_copy(iwg[:, :, :].rearrange("p i w -> p (i w)"), psum[:, 6, 0:TT * (W_IKW + W_NG)])\
                .then_inc(iwg_ready, 1)
            ve.wait_ge(iwg_ready, 1)
            nc.vector.tensor_scalar(iwg[:, :, IDX_DIM:W_IKW], iwg[:, :, IDX_DIM:W_IKW], IDX_SCALE, None, ALU.mult)\
                .then_inc(iwg_ready, 1)
            ve.wait_ge(iwg_ready, 2)
            for e in range(3 * IDX_HEADS):
                i, h = e // IDX_HEADS + 1, e % IDX_HEADS
                w = (i + 1) * P
                score = sel[:, SEL_OFF[i]:SEL_OFF[i] + w]
                weight = iwg[:, i, IDX_DIM + h:IDX_DIM + h + 1]
                ve.wait_ge(relu_done, e + 1)
                if h > 0:
                    ve.wait_ge(relu_used, e)
                    nc.vector.scalar_tensor_tensor(out=score, in0=relu_ring[:, e % 6, 0:w], scalar=weight,
                                                   in1=score, op0=ALU.mult, op1=ALU.add).then_inc(relu_used, 1)
                else:
                    nc.vector.tensor_scalar(score, relu_ring[:, e % 6, 0:w], weight, None, ALU.mult)\
                        .then_inc(relu_used, 1)
            conv_value(2)
            conv_value(3)
            ve.wait_ge(relu_used, 3 * IDX_HEADS)
            for i in range(1, TT):
                w = (i + 1) * P
                score = sel[:, SEL_OFF[i]:SEL_OFF[i] + w]
                diagonal = sel[:, SEL_OFF[i] + i * P:SEL_OFF[i] + w]
                link(nc.vector.tensor_tensor(diagonal, diagonal, later[:, :], ALU.add))
                for _ in range(TOPK // 8):
                    link(nc.vector.max(out=top8[:, :], in_=score))
                    link(nc.vector.match_replace(out=score, in_to_replace=top8[:, :], in_values=score,
                                                 imm_value=PICKED))
                link(nc.vector.tensor_scalar(score, score, 0.5 * PICKED, MASKED, ALU.is_gt, ALU.mult))
                link(nc.vector.tensor_tensor(score, score, dist[:, SEQ - w:SEQ], ALU.add))

            for c in range(4):
                h_in, y = proj[:, S_CONV + c, :], proj[:, CONV_OUT[c], :]
                copied(ve, N_CONV + 2 * c + 1)
                if c > 0:
                    ve.wait_ge(conv_out, c)
                tap = CONV_WIDTH - 1
                link(nc.vector.tensor_scalar(y, h_in, vecs[:, c, tap:tap + 1], vecs[:, c, V_CB:V_CB + 1],
                                             ALU.mult, ALU.add))
                for tap in range(CONV_WIDTH - 1):
                    s = CONV_WIDTH - 1 - tap
                    ins = nc.vector.scalar_tensor_tensor(out=y[:, s:], in0=h_in[:, 0:SEQ - s],
                                                         scalar=vecs[:, c, tap:tap + 1], in1=y[:, s:],
                                                         op0=ALU.mult, op1=ALU.add)
                    if tap < CONV_WIDTH - 2:
                        link(ins)
                ins.then_inc(conv_out, 1)

            for g in range(4):
                u = proj[:, S_POOL + g, :]
                copied(ve, N_POOL + g)
                if g > 0:
                    ve.wait_ge(pool_in, g)
                src, bufs = u, [tmp_a, tmp_b]
                for s in range(g + 1):
                    step, dst = 2 ** s, bufs[s % 2]
                    nc.vector.tensor_copy(dst[:, 0:step], src[:, 0:step])
                    link(nc.vector.tensor_tensor(dst[:, step:], src[:, step:], src[:, 0:SEQ - step], ALU.add))
                    src = dst
                win = 2 ** (g + 1)
                head = bufs[(g + 1) % 2][:, 0:win - 1]
                link(nc.vector.tensor_tensor(head, src[:, 0:win - 1], inv_count[:, 0:win - 1], ALU.mult))
                link(nc.vector.tensor_tensor(u[:, 0:win - 1], head, u[:, 0:win - 1], ALU.subtract))
                nc.vector.scalar_tensor_tensor(out=u[:, win - 1:], in0=src[:, win - 1:], scalar=1.0 / win,
                                               in1=u[:, win - 1:], op0=ALU.mult, op1=ALU.subtract)\
                    .then_inc(pool_in, 1)

            ve.wait_ge(pool_in, 4)
            ve.wait_ge(conv_out, 4)
            link(nc.vector.tensor_tensor(tmp_a, proj[:, CONV_OUT[0], :], proj[:, CONV_OUT[1], :], ALU.add))
            link(nc.vector.tensor_tensor(tmp_a, tmp_a, proj[:, CONV_OUT[2], :], ALU.add))
            nc.vector.tensor_tensor(tmp_a, tmp_a, proj[:, CONV_OUT[3], :], ALU.add).then_inc(channel_sum, 1)
            ve.wait_ge(mean_done, 1)
            for c in range(4):
                y = proj[:, CONV_OUT[c], :]
                nc.vector.tensor_tensor(y, y, psum[:, 2, :], ALU.subtract).then_inc(centred, 1)
            for c in range(1, 4):
                ve.wait_ge(squared, c + 1)
                ins = nc.vector.tensor_tensor(squares[:, 0, :], squares[:, 0, :], squares[:, c, :], ALU.add)
                if c < 3:
                    link(ins)
            ins.then_inc(channel_sum, 1)
            ve.wait_ge(pool_in, 4)
            ve.wait_ge(vec_ready, 2)
            for kv, slot in enumerate((S_CK, S_CV)):
                copied(ve, SLAB_OF[slot])
                src = proj[:, slot, :].rearrange("p (c b) -> p b c", b=CMP_STRIDE)
                dst = blk[:, kv, :].rearrange("p (l c) -> p l c", c=CMP_BLOCK)
                for a in range(2):
                    rows = slice(CMP_STRIDE * a, CMP_STRIDE * (a + 1))
                    at = pos[:, kv * CMP_BLOCK + CMP_STRIDE * a:kv * CMP_BLOCK + CMP_STRIDE * (a + 1)]
                    nc.vector.tensor_tensor(dst[:, rows, 0:N_CMP], src[:, :, a:a + N_CMP],
                                            at.unsqueeze(2).to_broadcast([P, CMP_STRIDE, N_CMP]),
                                            ALU.add).then_inc(blk_ready, 1)

            ve.wait_ge(std_ready, 1)
            link(nc.vector.reciprocal(rstd_conv, rstd_conv))
            ve.wait_ge(squared, 4)
            ve.wait_ge(centred, 4)
            for c in range(4):
                y = proj[:, CONV_OUT[c], :]
                nc.vector.tensor_tensor(y, y, rstd_conv, ALU.mult).then_inc(normed, 1)

            def mix_lo(m, bank, **affine):
                lo, hi = act_lo[:, MIX_ORDER[m], :], act_hi[:, MIX_ORDER[m], :].bitcast(F32)
                ve.wait_ge(mix_hi, m + 1)
                if affine:
                    ins = nc.vector.scalar_tensor_tensor(out=lo, in0=psum[:, bank, :], in1=hi, op1=ALU.subtract,
                                                         **affine)
                else:
                    ins = nc.vector.tensor_tensor(lo, psum[:, bank, :], hi, ALU.subtract)
                ins.then_inc(mix_split, 1)

            for m in range(4):
                mix_lo(m, PW_BANKS[m], scalar=vecs[:, m, V_PB:V_PB + 1], op0=ALU.add)
            for g in range(4):
                mix_lo(4 + g, 4 + g % 2, scalar=vecs[:, g, V_PS:V_PS + 1], op0=ALU.mult)

            ve.wait_ge(cmp2_done, 1)
            nc.vector.tensor_copy(cmp_kT[:, :], psum[:, 0, 64:64 + N_CMP]).then_inc(cmp_kv, 1)
            nc.vector.tensor_copy(cmp_v[:, :], psum[0:N_CMP, 1, P:2 * P]).then_inc(cmp_kv, 1)

            flat = cmp_p[:, :].rearrange("p (h e) -> p h e", h=HEADS)
            rows = cmp_p[:, :].rearrange("p (e c) -> p e c", c=N_CMP)
            ve.wait_ge(cmp_logit, 1)
            link(nc.vector.tensor_tensor(flat, psum[:, 0, 0:16 * N_CMP].rearrange("p (h e) -> p h e", h=HEADS),
                                         cmp_dist[:, :].unsqueeze(1).to_broadcast([P, HEADS, TT * N_CMP]), ALU.add))
            link(nc.vector.tensor_reduce(cmp_m[:, :], rows, AX.X, ALU.max))
            link(nc.vector.tensor_scalar(cmp_m[:, :], cmp_m[:, :], 0.1 * MASKED, None, ALU.max))
            nc.vector.tensor_tensor(rows, rows, cmp_m[:, :].unsqueeze(2).to_broadcast([P, 16, N_CMP]), ALU.subtract)\
                .then_inc(cmp_shift, 1)

            def add_distance(g):
                u, i = g // TT, g % TT
                w = (i + 1) * P
                if u < HEADS and i > 0:
                    d = sel[:, SEL_OFF[i]:SEL_OFF[i] + w]
                else:
                    d = dist[:, SEQ - w:SEQ]
                ve.wait_ge(qk_done, g + 1)
                if g >= RING:
                    ve.wait_ge(tr_done, g - RING + 1)
                nc.vector.tensor_tensor_reduce(out=proj[:, T_SLOTS[g % RING], 0:w], in0=psum[:, 2 + g % 2, 0:w], in1=d,
                                               scale=1.0, scalar=PICKED, op0=ALU.add, op1=ALU.max,
                                               accum_out=row_max[:, g % RING:g % RING + 1]).then_inc(scored, 1)
                ve.wait_ge(scored, g + 1)
                nc.vector.tensor_scalar(neg_max[:, g % RING:g % RING + 1], row_max[:, g % RING:g % RING + 1], 0.1 * MASKED,
                                        -UNITS[u][3], ALU.max, ALU.mult).then_inc(max_ready, 1)

            def inverse(g):
                inv = row_inv[:, g % RING:g % RING + 1]
                ve.wait_ge(exp_done, g + 1)
                link(nc.vector.tensor_scalar(inv, row_sum[:, g % RING:g % RING + 1], 1e-30, None, ALU.max))
                nc.vector.reciprocal(inv, inv).then_inc(inv_ready, 1)

            def compressed_probs():
                ve.wait_ge(cmp_exp, HEADS)
                link(nc.vector.tensor_reduce(cmp_r[:, :], rows, AX.X, ALU.add))
                link(nc.vector.tensor_scalar(cmp_r[:, :], cmp_r[:, :], 1e-30, None, ALU.max))
                link(nc.vector.reciprocal(cmp_r[:, :], cmp_r[:, :]))
                gates = iwg[:, :, W_IKW:].rearrange("p i (h b) -> p h i b", b=3)[:, :, :, 0]
                r = cmp_r[:, :].rearrange("p (h i) -> p h i", h=HEADS)
                link(nc.vector.tensor_tensor(r, r, gates, ALU.mult))
                nc.vector.tensor_tensor(rows, rows, cmp_r[:, :].unsqueeze(2).to_broadcast([P, 16, N_CMP]),
                                        ALU.mult).then_inc(cmp_prob, 1)

            ve.wait_ge(gates_ready, 1)
            for g in range(N_TILES + LO_LAG):
                if g < N_TILES:
                    add_distance(g)
                if 1 <= g <= N_TILES:
                    inverse(g - 1)
                if g >= LO_LAG and (g - LO_LAG) % TT == TT - 1:
                    u = (g - LO_LAG) // TT
                    if closes_head(u):
                        mix_lo(8 + head_of(u), 6 + head_of(u) % 2)
                if g == 4:
                    compressed_probs()
                if g == HEADS * TT:
                    for h in range(HEADS):
                        ve.wait_ge(cmp_t, h + 1)
                        nc.vector.tensor_copy(cmp_pT[:, h, :], psum[0:N_CMP, h % 2, :]).then_inc(cmp_t_ready, 1)

            def add_out(n, i):
                cols = acc[:, i, n * SEQ:(n + 1) * SEQ]
                tile_ready(ve, n, N_IN + 4 * n + 3, i)
                nc.vector.scalar_tensor_tensor(out=cols, in0=cols, scalar=ALPHA, in1=psum[:, 4 * (n % 2) + i, :],
                                               op0=ALU.mult, op1=ALU.add).then_inc(tile_added, 1)
                ve.wait_ge(tile_added, TILES0 + 4 * n + i + 1)
                link(nc.vector.bn_stats(stats[:, i, n, :], cols))

            def add_down(group, slab, n, i, with_stats=False):
                cols = acc[:, i, n * SEQ:(n + 1) * SEQ]
                tile_ready(ve, group * 4 + (4 + n), slab + n, i)
                nc.vector.tensor_tensor(cols, cols, psum[:, i, :], ALU.add).then_inc(tile_added, 1)
                if with_stats:
                    ve.wait_ge(tile_added, group * 16 + (TILES0 + 16 + 4 * n + i + 1))
                    link(nc.vector.bn_stats(stats[:, i, n, :], cols))

            def moments_of(i):
                nc.vector.bn_aggr(moments[:, i, :], stats[:, i, :, :].rearrange("p n s -> p (n s)"))\
                    .then_inc(var_ready, 1)

            def rstd_of(i, half):
                ve.wait_ge(std_done, TT * half + i + 1)
                link(nc.vector.reciprocal(rstd[:, i:i + 1], std[:, i:i + 1]))
                nc.vector.scalar_tensor_tensor(out=shift[:, i:i + 1], in0=moments[:, i, 0:1], scalar=-1.0,
                                               in1=rstd[:, i:i + 1], op0=ALU.mult, op1=ALU.mult)\
                    .then_inc(rstd_ready, 1)

            def gain(i, half):
                ve.wait_ge(xn_ready, affine_count(i, half))
                nc.vector.tensor_tensor(acc[:, i, :], acc[:, i, :], ln_g[:, :], ALU.mult).then_inc(gained, 1)

            def bias(i, done):
                ve.wait_ge(gained_pool, 1)
                nc.vector.tensor_tensor(acc[:, i, :], acc[:, i, :], ln_b[:, :], ALU.add).then_inc(done[i], 1)

            def centre(i, cols, count):
                ve.wait_ge(var_ready, count)
                y = acc[:, i, cols]
                link(nc.vector.scalar_tensor_tensor(out=y, in0=y, scalar=moments[:, i, 0:1], in1=ln_g[:, cols],
                                                    op0=ALU.subtract, op1=ALU.mult))

            def scale_and_shift(i, cols, count, done):
                ve.wait_ge(rstd_ready, count)
                y = acc[:, i, cols]
                nc.vector.scalar_tensor_tensor(out=y, in0=y, scalar=rstd[:, i:i + 1], in1=ln_b[:, cols],
                                               op0=ALU.mult, op1=ALU.add).then_inc(done[i], 1)

            def x1_split(i):
                for q in range(4):
                    e = 4 * i + q
                    here = (slice(None), slice(4 * q, 4 * q + 4), slice(i * P, (i + 1) * P))
                    ve.wait_ge(x1_hi, e + 1)
                    nc.vector.tensor_tensor(act_lo[here],
                                            psum[:, X1_BANKS[e % 6], :].rearrange("p (k s) -> p k s", k=4),
                                            act_hi[here].bitcast(F32), ALU.subtract).then_inc(x1_lo, 1)

            ve.wait_ge(resid_loaded, 16)
            for n in range(3):
                for i in range(TT):
                    add_out(n, i)
            ve.wait_ge(ln_loaded, 32)
            for i in range(2):
                add_out(3, i)
                moments_of(i)
                centre(i, slice(0, D_MODEL), i + 1)
                rstd_of(i, 0)
                scale_and_shift(i, slice(0, D_MODEL), i + 1, x1_ready)
            x1_split(0)
            add_out(3, 2)
            moments_of(2)
            add_out(3, 3)
            moments_of(3)
            x1_split(1)
            rstd_of(2, 0)
            rstd_of(3, 0)
            centre(2, slice(0, D_MODEL), 3)
            scale_and_shift(2, slice(0, D_MODEL), 3, x1_ready)
            bias(3, x1_ready)
            x1_split(2)
            x1_split(3)

            def hidden(j, q, slab):
                ve.wait_ge(slab_done, slab + 1)
                ve.wait_ge(silu_done, q + 1)
                if not isinstance(q, int) or q >= 2:
                    ve.wait_ge(hid_lo, q - 1)
                nc.vector.tensor_tensor(hid[:, j % 2, :], psum[:, 5 + 2 * (j % 2), :], silu_g[:, j % 2, :],
                                        ALU.mult).then_inc(hid_ready, 1)

            def hidden_lo(j, q):
                ve.wait_ge(hid_hi, q + 1)
                nc.vector.tensor_tensor(h_lo[:, j % 4, :], hid[:, j % 2, :], h_hi[:, j % 4, :].bitcast(F32),
                                        ALU.subtract).then_inc(hid_lo, 1)

            hidden(0, 0, FF0 + 1)
            hidden_lo(0, 0)
            hidden(1, 1, FF0 + 3)
            hidden_lo(1, 1)
            ve.wait_ge(scaled, TT)
            with ve.Fori(0, FF_GROUPS - 1) as g:
                for j in (2, 3):
                    hidden(j, g * 4 + j, g * 12 + (FF0 + 2 * j + 1))
                    hidden_lo(j, g * 4 + j)
                hidden(4, g * 4 + 4, g * 12 + (FF0 + 9))
                for n in range(4):
                    for i in range(TT):
                        add_down(g, g * 12 + (FF0 + 10), n, i)
                hidden_lo(4, g * 4 + 4)
                hidden(5, g * 4 + 5, g * 12 + (FF0 + 15))
                hidden_lo(5, g * 4 + 5)
            last = FF_GROUPS - 1
            for j in (2, 3):
                hidden(j, 4 * last + j, 12 * last + FF0 + 2 * j + 1)
                hidden_lo(j, 4 * last + j)
            slab = 12 * last + FF0 + 8
            for n in range(2):
                for i in range(TT):
                    add_down(last, slab, n, i, with_stats=True)
            ve.wait_ge(ln_loaded, 64)
            finished = (4 + 4 * last + 2) * (TT - 1)
            added = 16 * last + TILES0 + 16 + 8

            def add_late(i, n):
                if i < TT - 1:
                    ve.wait_ge(tile_done, finished + 2 * i + (n - 2) + 1)
                else:
                    ve.wait_ge(slab_done, slab + n + 1)
                cols = acc[:, i, n * SEQ:(n + 1) * SEQ]
                nc.vector.tensor_tensor(cols, cols, psum[:, 4 * (n - 2) + i, :], ALU.add).then_inc(tile_added, 1)
                ve.wait_ge(tile_added, added + 2 * i + (n - 2) + 1)
                link(nc.vector.bn_stats(stats[:, i, n, :], cols))

            add_late(0, 2)
            for i in range(TT):
                add_late(i, 3)
                moments_of(i)
                if i == TT - 1:
                    gain(i - 1, 1)
                rstd_of(i, 1)
                if i < TT - 1:
                    add_late(i + 1, 2)
                if i == 1:
                    gain(i, 1)
            for n in range(4):
                cols = slice(n * SEQ, (n + 1) * SEQ)
                centre(TT - 1, cols, 2 * TT)
                scale_and_shift(TT - 1, cols, 2 * TT, y_ready)


_INS = ["x", "w_in", "w_out", "pool_w", "pool_scale", "conv_w", "conv_b", "conv_ln_g", "conv_ln_b",
        "conv_pw_w", "conv_pw_b", "cmp_pos_k", "cmp_pos_v", "cmp_k_w1", "cmp_k_w2", "cmp_v_w1",
        "cmp_v_w2", "ln1_g", "ln1_b", "ln2_g", "ln2_b", "w_gate_up", "w_down"]


def kernel(**inputs):
    import concourse.bacc as bacc
    from concourse.bass_utils import run_bass_kernel_spmd

    nc = bacc.Bacc("TRN2", target_bir_lowering=False, num_devices=1)
    arrays, args = {}, []
    for name in _INS:
        a = np.ascontiguousarray(inputs[name])
        arrays[f"in_{name}"] = a
        args.append(nc.dram_tensor(f"in_{name}", a.shape, mybir.dt.from_np(a.dtype), kind="ExternalInput").ap())
    out = nc.dram_tensor("out", (1, SEQ, D_MODEL), F32, kind="ExternalOutput").ap()
    build(nc, *args, out)
    result = run_bass_kernel_spmd(nc, [arrays], core_ids=[0])
    return result.results[0]["out"]
```

```python
from contextlib import ExitStack

import numpy as np

import concourse.bass as bass
from concourse import mybir

F32 = mybir.dt.float32
F32R = mybir.dt.float32r
ALU = mybir.AluOpType
ACT = mybir.ActivationFunctionType
AX = mybir.AxisListType

P = 128
SEQ = 512
D_MODEL = 2048
KT = D_MODEL // P
TT = SEQ // P
D_FF = 5632
HEADS = 4
IDX_HEADS, IDX_DIM = 8, 64
TOPK = min(256, SEQ // 4)
CONV_WIDTH = 31
CMP_BLOCK, CMP_STRIDE = 32, 16
N_CMP = (SEQ - CMP_BLOCK) // CMP_STRIDE + 1
ALPHA = 2.0 ** 0.25
LN_EPS = 1e-5
ATTN_SCALE = float(P) ** -0.5
IDX_SCALE = float(IDX_HEADS * IDX_DIM) ** -0.5
SLOPES_DSA = [2.0 ** -(2 * h + 1) for h in range(HEADS)]
SLOPES_NSA = [2.0 ** -(2 * h + 2) for h in range(HEADS)]
MASKED = -1e30
PICKED = -3e38

SLAB = 2048
C_POOL, C_A, C_G, C_DQ, C_IQ, C_IK, C_NQ, C_NG = 0, 512, 1024, 1536, 2304, 2816, 2888, 4168
W_IKW, W_NG = IDX_DIM + IDX_HEADS, 3 * HEADS

N_IDX, N_IKWG, N_CONV, N_POOL, N_QKV = 0, 4, 5, 13, 17
N_IN = 33
N_OUT = 16
FF_CHUNKS = D_FF // P
FF_GROUPS = FF_CHUNKS // 4

S_IQ, S_IKWG, S_CONV, S_SPARE, S_POOL, S_DQ, S_DK, S_DV, S_NQ = 0, 4, 5, 9, 10, 14, 18, 19, 20
S_CK, S_CV, S_SK, S_SV, S_WK, S_WV = 24, 25, 26, 27, 28, 29
N_SLOTS = 30
CONV_OUT = [S_SPARE, S_CONV, S_CONV + 1, S_CONV + 2]
VEC_ROWS = CONV_WIDTH + 5
V_CB, V_LG, V_LB, V_PB, V_PS = range(CONV_WIDTH, VEC_ROWS)

UNITS = [(S_DQ + h, S_DK, S_DV, SLOPES_DSA[h]) for h in range(HEADS)]
for _h in range(HEADS):
    UNITS += [(S_NQ + _h, S_SK, S_SV, SLOPES_NSA[_h]), (S_NQ + _h, S_WK, S_WV, SLOPES_NSA[_h])]
N_UNITS = len(UNITS)
N_TILES = N_UNITS * TT
SLAB_OF = {S_POOL + g: N_POOL + g for g in range(4)}
SLAB_OF.update({S_DQ + s: N_QKV + s for s in range(16)})
T_SLOTS = [S_IQ, S_IQ + 1, S_IQ + 2, S_IQ + 3, S_IKWG, S_CONV + 3, S_CONV, S_CONV + 1]
RING = len(T_SLOTS)
EARLY = 6
TURN_LAG = EARLY
WEIGH_LAG = TURN_LAG + 2
OUT_LAG = WEIGH_LAG + 1
LO_LAG = OUT_LAG + 1
X1_BANKS = [0, 1, 2, 3, 4, 5, 0, 1, 2, 3, 6, 7, 0, 1, 2, 3]
SEL_OFF = [None, 0, 2 * P, 5 * P]
MIX_ORDER = [0, 1, 4, 5, 6, 7, 2, 3] + list(range(8, 16))
MIX_BANKS = [4, 5, 6, 7, 4, 5, 6, 7]


def head_of(u):
    return u if u < HEADS else HEADS + (u - HEADS) // 2


def closes_head(u):
    return u < HEADS or (u - HEADS) % 2 == 1


def build(nc, x, w_in, w_out, pool_w, pool_scale, conv_w, conv_b, conv_ln_g, conv_ln_b, conv_pw_w,
          conv_pw_b, cmp_pos_k, cmp_pos_v, cmp_k_w1, cmp_k_w2, cmp_v_w1, cmp_v_w2, ln1_g, ln1_b,
          ln2_g, ln2_b, w_gate_up, w_down, out):
    with ExitStack() as ctx:
        def sb(name, shape, dt=F32, where=ctx):
            return where.enter_context(nc.sbuf_tensor(name, shape, dt))

        def sem(name):
            return ctx.enter_context(nc.semaphore(name))

        psum = ctx.enter_context(nc.psum_tensor("psum", [P, 8, SEQ], F32))

        act_hi = sb("act_hi", [P, KT, SEQ], F32R)
        act_lo = sb("act_lo", [P, KT, SEQ], F32R)
        w_hi = sb("w_hi", [P, 2, SLAB], F32R)
        w_lo = sb("w_lo", [P, 2, SLAB], F32R)
        raw = sb("raw", [P, 2, SLAB])
        stats = sb("stats", [P, TT, 4, 6])
        moments = sb("moments", [P, TT, 2])
        rstd = sb("rstd", [P, TT])
        shift = sb("shift", [P, TT])
        std = sb("std", [P, TT])
        ident = sb("ident", [P, P])
        eps = sb("eps", [P, 1])

        mixing = ExitStack()
        with mixing:
            def sbm(name, shape):
                return sb(name, shape, F32, mixing)

            proj = sbm("proj", [P, N_SLOTS, SEQ])
            dist = sbm("dist", [P, SEQ])
            sel = sbm("sel", [P, 9 * P])
            pt = sbm("pt", [P, 2, 13 * P])
            blk = sbm("blk", [P, 2, CMP_BLOCK * CMP_BLOCK])
            cmp_p = sbm("cmp_p", [P, 16 * N_CMP])
            vecs = sbm("vecs", [P, 4, VEC_ROWS])
            pos = sbm("pos", [P, 2 * CMP_BLOCK])
            iwg = sbm("iwg", [P, TT, W_IKW + W_NG])
            cmp_dist = sbm("cmp_dist", [P, TT * N_CMP])
            cmp_kT = sbm("cmp_kT", [P, N_CMP])
            cmp_h = sbm("cmp_h", [P, 2, N_CMP])
            cmp_v = sbm("cmp_v", [N_CMP, P])
            w2 = sbm("w2", [P, 2, P])
            inv_count = sbm("inv_count", [P, 16])
            top8 = sbm("top8", [P, 8])
            row_max = sbm("row_max", [P, RING])
            neg_max = sbm("neg_max", [P, RING])
            row_sum = sbm("row_sum", [P, RING])
            row_inv = sbm("row_inv", [P, RING])
            cmp_m = sbm("cmp_m", [P, 16])
            cmp_r = sbm("cmp_r", [P, 16])
        feed = ExitStack()
        feed_ctx = ctx.enter_context(feed)
        acc = sb("acc", [P, TT, D_MODEL], F32, feed)
        ln_g = sb("ln_g", [P, D_MODEL], F32, feed)
        ln_b = sb("ln_b", [P, D_MODEL], F32, feed)
        h_hi = sb("h_hi", [P, 4, SEQ], F32R, feed)
        h_lo = sb("h_lo", [P, 4, SEQ], F32R, feed)
        silu_g = sb("silu_g", [P, 2, SEQ], F32, feed)
        hid = sb("hid", [P, 2, SEQ], F32, feed)

        x_nat = proj[:, 0:16, :].rearrange("p (i k) s -> p i (k s)", i=TT)
        vec_nat = sel[0:VEC_ROWS, 0:SEQ]
        pos_nat = sel[0:2 * CMP_BLOCK, SEQ:SEQ + P]
        later = cmp_p[:, 0:P]
        ones = cmp_p[:, P:2 * P]
        ik_high = blk[64:128, 0, 0:SEQ]
        relu_ring = pt[:, :, :].rearrange("p a b -> p (a b)")[:, 0:6 * SEQ].rearrange("p (r s) -> p r s", r=6)
        squares = relu_ring
        rstd_conv = proj[:, S_CONV + 3, :]
        tmp_a, tmp_b = blk[:, 0, 0:SEQ], blk[:, 0, SEQ:2 * SEQ]
        cmp_pre = proj[0:N_CMP, S_IKWG, 0:2 * P]
        cmp_pT = blk[0:N_CMP, :, :].rearrange("c a b -> c (a b)").rearrange("c (h s) -> c h s", h=HEADS)

        spare_slot = (h_hi[:, :, :].rearrange("p k n -> p (k n)"), h_lo[:, :, :].rearrange("p k n -> p (k n)"))
        late_hi = [act_hi[:, 4 * c:4 * c + 4, :].rearrange("p k n -> p (k n)") for c in range(2)]
        late_lo = [act_lo[:, 4 * c:4 * c + 4, :].rearrange("p k n -> p (k n)") for c in range(2)]

        pt_flat = pt[:, :, :].rearrange("p a b -> p (a b)")
        aux_weights = {"v0": proj[:, S_IQ:S_IQ + 4, :].rearrange("p k s -> p (k s)"), "v1": raw[:, 1, :],
                       "pool": pt_flat[:, 0:SEQ], "pw": pt_flat[:, SEQ:SEQ + SLAB]}

        raw_loaded = [sem(f"raw_loaded{i}") for i in range(2)]
        aux_loaded = {name: sem(f"aux_loaded_{name}") for name in aux_weights}
        aux_used = sem("aux_used")
        split_begun = sem("split_begun")
        hi_done = sem("hi_done")
        split_done = sem("split_done")
        slab_done = sem("slab_done")
        x_loaded = [sem(f"x_loaded{i}") for i in range(TT)]
        small_loaded = sem("small_loaded")
        const_ready = sem("const_ready")
        ident_ready = sem("ident_ready")
        xt_done = sem("xt_done")
        xt_hi = sem("xt_hi")
        xt_lo = sem("xt_lo")
        bank_free = [sem(f"bank_free{i}") for i in range(2)]
        vec_t = sem("vec_t")
        vec_ready = sem("vec_ready")
        iwg_t = sem("iwg_t")
        iwg_ready = sem("iwg_ready")
        gates_ready = sem("gates_ready")
        ik_dup = sem("ik_dup")
        logit_done = sem("logit_done")
        relu_done = sem("relu_done")
        relu_used = sem("relu_used")
        dve = sem("dve")
        conv_out = sem("conv_out")
        channel_sum = sem("channel_sum")
        mean_done = sem("mean_done")
        centred = sem("centred")
        squared = sem("squared")
        var_done = sem("var_done")
        std_ready = sem("std_ready")
        normed = sem("normed")
        silu_ready = sem("silu_ready")
        pw_done = sem("pw_done")
        pool_in = sem("pool_in")
        pool_done = sem("pool_done")
        v_t = sem("v_t")
        v_nat = sem("v_nat")
        blk_ready = sem("blk_ready")
        cmp_pre_ready = sem("cmp_pre_ready")
        cmp_pre_t = sem("cmp_pre_t")
        gelu_ready = sem("gelu_ready")
        cmp2_done = sem("cmp2_done")
        cmp_kv = sem("cmp_kv")
        cmp_logit = sem("cmp_logit")
        cmp_shift = sem("cmp_shift")
        cmp_exp = sem("cmp_exp")
        cmp_prob = sem("cmp_prob")
        cmp_t = sem("cmp_t")
        cmp_t_ready = sem("cmp_t_ready")
        qk_done = sem("qk_done")
        scored = sem("scored")
        max_ready = sem("max_ready")
        exp_done = sem("exp_done")
        inv_ready = sem("inv_ready")
        prob_ready = sem("prob_ready")
        tr_done = sem("tr_done")
        pt_ready = sem("pt_ready")
        pv_done = sem("pv_done")
        mix_hi = sem("mix_hi")
        mix_split = sem("mix_split")
        half_loaded = [sem(f"half_loaded{i}") for i in range(2)]
        half_hi = sem("half_hi")
        half_lo = sem("half_lo")
        piece_hi = sem("piece_hi")
        piece_lo = sem("piece_lo")
        resid_loaded = sem("resid_loaded")
        ln_loaded = sem("ln_loaded")
        tile_done = sem("tile_done")
        tile_added = sem("tile_added")
        var_ready = sem("var_ready")
        std_done = sem("std_done")
        rstd_ready = sem("rstd_ready")
        xn_ready = sem("xn_ready")
        gained = sem("gained")
        gained_pool = sem("gained_pool")
        x1_ready = [sem(f"x1_ready{i}") for i in range(TT)]
        x1_t = sem("x1_t")
        x1_hi = sem("x1_hi")
        x1_lo = sem("x1_lo")
        scaled = sem("scaled")
        silu_done = sem("silu_done")
        hid_ready = sem("hid_ready")
        hid_hi = sem("hid_hi")
        hid_lo = sem("hid_lo")
        y_ready = [sem(f"y_ready{i}") for i in range(TT)]
        stored = sem("stored")

        win = w_in[0].rearrange("(k p) n -> p k n", p=P)
        wout = w_out[0].rearrange("(k p) n -> p k n", p=P)
        wgu = w_gate_up[0].rearrange("(k p) n -> p k n", p=P)
        wdown = w_down[0].rearrange("(k p) n -> p k n", p=P)
        x_dram = x[0].rearrange("(i p) d -> p i d", p=P)
        out_dram = out[0].rearrange("(i p) d -> p i d", p=P)

        N_AUX = 2
        FF0 = N_IN + N_OUT
        TILES0 = 8

        def copied(eng, n):
            eng.wait_ge(bank_free[n % 2], n // 2 + 1)

        def tile_ready(eng, group, slab, i):
            if i < TT - 1:
                eng.wait_ge(tile_done, group * (TT - 1) + (i + 1))
            else:
                eng.wait_ge(slab_done, slab + 1)

        def affine_count(i, half):
            return 1 if half == 0 else i + 2

        block = ctx.enter_context(nc.Block())

        @block.sync
        def _(sp):
            def load(slot, src, shape_k):
                dst = raw[:, slot, 0:shape_k * (SLAB // shape_k)].rearrange("p (k n) -> p k n", k=shape_k)
                nc.sync.dma_start(dst, src).then_inc(raw_loaded[slot], 16)

            def x_tile(i):
                nc.sync.dma_start(x_nat[:, i, :], x_dram[:, i, :]).then_inc(x_loaded[i], 16)

            x_tile(0)
            x_tile(1)
            for h in range(2):
                dst = raw[:, 0, h * (SLAB // 2):(h + 1) * (SLAB // 2)].rearrange("p (k n) -> p k n", n=P)
                nc.sync.dma_start(dst, win[:, h * (KT // 2):(h + 1) * (KT // 2), C_IQ:C_IQ + P])\
                    .then_inc(half_loaded[h], 16)
            x_tile(2)
            x_tile(3)
            load(1, win[:, :, C_IQ + P:C_IQ + 2 * P], KT)
            rows = ((conv_w[0], 0, CONV_WIDTH), (conv_b, V_CB, 1), (conv_ln_g, V_LG, 1),
                    (conv_ln_b, V_LB, 1), (conv_pw_b, V_PB, 1), (pool_scale, V_PS, 1))
            for src, at, n in rows:
                nc.sync.dma_start(sel[at:at + n, 0:SEQ], src).then_inc(small_loaded, 16)
            nc.sync.dma_start(sel[0:CMP_BLOCK, SEQ:SEQ + P], cmp_pos_k[0]).then_inc(small_loaded, 16)
            nc.sync.dma_start(sel[CMP_BLOCK:2 * CMP_BLOCK, SEQ:SEQ + P], cmp_pos_v[0]).then_inc(small_loaded, 16)
            nc.sync.dma_start(w2[:, 0, :], cmp_k_w2[0]).then_inc(small_loaded, 16)
            nc.sync.dma_start(w2[:, 1, :], cmp_v_w2[0]).then_inc(small_loaded, 16)

            for n in (2, 3):
                sp.wait_ge(split_done, n - 1)
                load(n % 2, win[:, :, C_IQ + n * P:C_IQ + (n + 1) * P], KT)
            sp.wait_ge(split_done, N_IKWG - 1)
            ikwg = raw[:, 0, 0:KT * (W_IKW + W_NG)].rearrange("p (k n) -> p k n", k=KT)
            nc.sync.dma_start(ikwg[:, :, 0:W_IKW], win[:, :, C_IK:C_IK + W_IKW]).then_inc(raw_loaded[0], 16)
            nc.sync.dma_start(ikwg[:, :, W_IKW:], win[:, :, C_NG:C_NG + W_NG]).then_inc(raw_loaded[0], 16)

            with sp.Fori(0, 4) as c:
                sp.wait_ge(split_done, 2 * c + (N_CONV - 1))
                load(1, win[:, :, bass.ds(c * P + C_G, P)], KT)
                sp.wait_ge(split_done, 2 * c + N_CONV)
                load(0, win[:, :, bass.ds(c * P + C_A, P)], KT)

            def pairs(count, first, column):
                with sp.Fori(0, count) as c:
                    sp.wait_ge(split_done, 2 * c + (first - 1))
                    load(1, win[:, :, bass.ds(c * (2 * P) + column, P)], KT)
                    sp.wait_ge(split_done, 2 * c + first)
                    load(0, win[:, :, bass.ds(c * (2 * P) + (column + P), P)], KT)

            pairs(2, N_POOL, C_POOL)
            pairs(3, N_QKV, C_DQ)
            pairs(5, N_QKV + 6, C_NQ)

            wk1, wv1 = (w[0].rearrange("(l d) h -> d l h", d=P) for w in (cmp_k_w1, cmp_v_w1))
            def aux_load(name, src, k):
                dst = aux_weights[name].rearrange("p (k n) -> p k n", k=k)
                nc.sync.dma_start(dst, src).then_inc(aux_loaded[name], 16)

            sp.wait_ge(logit_done, 3 * IDX_HEADS)
            aux_load("v0", wv1[:, 0:16, :], 16)
            for a in range(N_AUX):
                sp.wait_ge(split_done, N_IN - 1 + a)
                load((N_IN + a) % 2, wk1[:, 16 * a:16 * a + 16, :], 16)

            sp.wait_ge(var_done, 1)
            aux_load("pw", conv_pw_w[0].rearrange("(k p) n -> p k n", p=P), 4)
            aux_load("pool", pool_w[0].rearrange("g c d -> c g d"), 4)
            sp.wait_ge(aux_used, 1)
            aux_load("v1", wv1[:, 16:32, :], 16)

            for m in range(2):
                sp.wait_ge(aux_used, (4, 2)[m])
                load((m + 1) % 2, wout[:, 4 * m:4 * m + 4, 0:SEQ], 4)
            for m in range(2, 4):
                sp.wait_ge(split_done, N_IN + m - 1)
                load((m + 1) % 2, wout[:, 4 * m:4 * m + 4, 0:SEQ], 4)
            sp.wait_ge(mix_split, 16)
            nc.sync.dma_start(acc[:, :, :], x_dram).then_inc(resid_loaded, 16)
            nc.sync.dma_start(ln_g[:, :], ln1_g.to_broadcast([P, D_MODEL])).then_inc(ln_loaded, 16)
            nc.sync.dma_start(ln_b[:, :], ln1_b.to_broadcast([P, D_MODEL])).then_inc(ln_loaded, 16)
            with sp.Fori(1, 4) as n:
                for kq in range(4):
                    sp.wait_ge(split_done, 4 * n + (N_IN + kq - 1))
                    load((kq + 1) % 2, wout[:, 4 * kq:4 * kq + 4, bass.ds(n * SEQ, SEQ)], 4)

            def gate_up(first, chunk):
                for u in range(2):
                    sp.wait_ge(split_done, first + (u - 1))
                    load((u + 1) % 2, wgu[:, :, bass.ds(chunk * P + u * D_FF, P)], KT)

            def down(first, group):
                for n in range(4):
                    sp.wait_ge(split_done, first + (n - 1))
                    load((n + 1) % 2, wdown[:, bass.ds(group * 4, 4), n * SEQ:(n + 1) * SEQ], 4)

            gate_up(FF0, 0)
            sp.wait_ge(split_done, FF0 + 2)
            gate_up(FF0 + 2, 1)
            for i in range(TT):
                sp.wait_ge(x1_ready[i], 1)
            nc.sync.dma_start(ln_g[:, :], ln2_g.to_broadcast([P, D_MODEL])).then_inc(ln_loaded, 16)
            nc.sync.dma_start(ln_b[:, :], ln2_b.to_broadcast([P, D_MODEL])).then_inc(ln_loaded, 16)
            with sp.Fori(0, FF_GROUPS - 1) as g:
                gate_up(g * 12 + (FF0 + 4), g * 4 + 2)
                gate_up(g * 12 + (FF0 + 6), g * 4 + 3)
                gate_up(g * 12 + (FF0 + 8), g * 4 + 4)
                down(g * 12 + (FF0 + 10), g)
                gate_up(g * 12 + (FF0 + 14), g * 4 + 5)
            last = FF0 + 12 * (FF_GROUPS - 1)
            gate_up(last + 4, FF_CHUNKS - 2)
            gate_up(last + 6, FF_CHUNKS - 1)
            down(last + 8, FF_GROUPS - 1)

            def store(i, ready, blocks):
                sp.wait_ge(y_ready[i], ready)
                cols = slice(blocks[0] * SEQ, (blocks[-1] + 1) * SEQ)
                nc.sync.dma_start(out_dram[:, i, cols], acc[:, i, cols]).then_inc(stored, 16)

            stores = ((0, 2, (0, 1, 2, 3)), (1, 2, (0, 1, 2, 3)), (2, 1, (0, 1)), (3, 1, (0,)), (3, 2, (1,)),
                      (2, 2, (2, 3)), (3, 3, (2,)), (3, 4, (3,)))
            for i, ready, blocks in stores:
                store(i, ready, blocks)
            sp.wait_ge(stored, 16 * len(stores))

        @block.gpsimd
        def _(pool):
            nc.gpsimd.memset(ident[:, :], 0.0).then_inc(const_ready, 1)
            pool.wait_ge(const_ready, 1)
            nc.gpsimd.affine_select(out=ident[:, :], in_=ident[:, :], compare_op=ALU.not_equal, fill=1.0,
                                    base=0, pattern=[[-1, P]], channel_multiplier=1).then_inc(ident_ready, 1)

            def split(slot, loads, n, words=SLAB, dst=None, used=-1):
                hi, lo = dst or (w_hi[:, slot, 0:words], w_lo[:, slot, 0:words])
                pool.wait_ge(raw_loaded[slot], loads)
                if used == -1 and not (isinstance(n, int) and n < 2):
                    used = n - 1
                if not (isinstance(used, int) and used <= 0):
                    pool.wait_ge(slab_done, used)
                nc.gpsimd.sem_inc(split_begun, 1)
                nc.gpsimd.tensor_scalar(hi, raw[:, slot, 0:words], 1.0, 1.0, ALU.mult, ALU.mult)\
                    .then_inc(hi_done, 1)
                pool.wait_ge(hi_done, n + 1)
                nc.gpsimd.tensor_tensor(lo, raw[:, slot, 0:words], hi.bitcast(F32), ALU.subtract)\
                    .then_inc(split_done, 1)

            for h in range(2):
                cols = slice(h * (SLAB // 2), (h + 1) * (SLAB // 2))
                pool.wait_ge(half_loaded[h], 16)
                nc.gpsimd.tensor_scalar(w_hi[:, 0, cols], raw[:, 0, cols], 1.0, 1.0, ALU.mult, ALU.mult)\
                    .then_inc(half_hi, 1)
                pool.wait_ge(half_hi, h + 1)
                nc.gpsimd.tensor_tensor(w_lo[:, 0, cols], raw[:, 0, cols], w_hi[:, 0, cols].bitcast(F32),
                                        ALU.subtract).then_inc(half_lo, 1)
            pool.wait_ge(half_lo, 2)
            nc.gpsimd.sem_inc(hi_done, 1)
            nc.gpsimd.sem_inc(split_done, 1)
            nc.gpsimd.iota(dist[:, :], pattern=[[1, SEQ]], base=-(SEQ - P), channel_multiplier=-1,
                           allow_small_or_imprecise_dtypes=True).then_inc(const_ready, 1)
            pool.wait_ge(const_ready, 2)
            nc.gpsimd.affine_select(out=dist[:, :], in_=dist[:, :], compare_op=ALU.is_ge, fill=MASKED,
                                    base=SEQ - P, pattern=[[-1, SEQ]], channel_multiplier=1).then_inc(const_ready, 1)
            nc.gpsimd.iota(cmp_dist[:, :], pattern=[[-P, TT], [CMP_STRIDE, N_CMP]], base=CMP_BLOCK - 1,
                           channel_multiplier=-1, allow_small_or_imprecise_dtypes=True).then_inc(const_ready, 1)
            pool.wait_ge(const_ready, 4)
            nc.gpsimd.affine_select(out=cmp_dist[:, :], in_=cmp_dist[:, :], compare_op=ALU.is_ge, fill=MASKED,
                                    base=-(CMP_BLOCK - 1), pattern=[[P, TT], [-CMP_STRIDE, N_CMP]],
                                    channel_multiplier=1).then_inc(const_ready, 1)
            nc.gpsimd.memset(later[:, :], 0.0).then_inc(const_ready, 1)
            nc.gpsimd.memset(ones[:, :], 1.0 / SEQ).then_inc(const_ready, 1)
            nc.gpsimd.memset(eps[:, :], LN_EPS).then_inc(const_ready, 1)
            nc.gpsimd.iota(inv_count[:, :], pattern=[[1, 16]], base=1, channel_multiplier=0,
                           allow_small_or_imprecise_dtypes=True).then_inc(const_ready, 1)
            pool.wait_ge(const_ready, 6)
            nc.gpsimd.affine_select(out=later[:, :], in_=later[:, :], compare_op=ALU.is_ge, fill=MASKED,
                                    base=0, pattern=[[-1, P]], channel_multiplier=1).then_inc(const_ready, 1)

            split(1, 16, 1)
            split(0, 16, 2)
            split(1, 32, 3)
            split(0, 48, N_IKWG, KT * (W_IKW + W_NG))
            with pool.Fori(0, (N_IN - N_CONV) // 2) as c:
                split(1, c * 16 + 48, 2 * c + N_CONV)
                split(0, c * 16 + 64, 2 * c + (N_CONV + 1))

            odd = 16 * (N_IN // 2 + N_AUX // 2)
            even = 16 * (N_IN // 2 + 1 + N_AUX // 2)

            def normalise(g):
                u, i = g // TT, g % TT
                p = proj[:, T_SLOTS[g % RING], 0:(i + 1) * P]
                inv = row_inv[:, g % RING:g % RING + 1]
                pool.wait_ge(inv_ready, g + 1)
                if u < HEADS:
                    ins = nc.gpsimd.tensor_scalar(p, p, inv, 1.0, ALU.mult, ALU.mult)
                else:
                    col = W_IKW + 3 * ((u - HEADS) // 2) + 1 + (u - HEADS) % 2
                    ins = nc.gpsimd.tensor_scalar(p, p, inv, iwg[:, i, col:col + 1], ALU.mult, ALU.mult)
                ins.then_inc(prob_ready, 1)

            def split_piece(m, c):
                slot, cols = (m + 1) % 2, slice(c * SLAB // 4, (c + 1) * SLAB // 4)
                n_piece = 4 * m + c + 1
                if c == 0:
                    pool.wait_ge(raw_loaded[slot], (even, odd)[slot] + 16)
                    pool.wait_ge(slab_done, N_IN)
                nc.gpsimd.tensor_scalar(w_hi[:, slot, cols], raw[:, slot, cols], 1.0, 1.0,
                                        ALU.mult, ALU.mult).then_inc(piece_hi, 1)
                pool.wait_ge(piece_hi, n_piece)
                nc.gpsimd.tensor_tensor(w_lo[:, slot, cols], raw[:, slot, cols],
                                        w_hi[:, slot, cols].bitcast(F32), ALU.subtract).then_inc(piece_lo, 1)
                if c == 3:
                    pool.wait_ge(piece_lo, n_piece)
                    nc.gpsimd.sem_inc(hi_done, 1)
                    nc.gpsimd.sem_inc(split_done, 1)

            pool.wait_ge(gates_ready, 1)
            for g in range(N_TILES):
                normalise(g)
                piece = g // TT - 2
                if g % TT == 0 and 0 <= piece < 8:
                    split_piece(piece // 4, piece % 4)

            def split_pairs(first, end):
                with pool.Fori(first, end) as c:
                    split(1, c * 16 + (odd + 16), 2 * c + N_IN)
                    split(0, c * 16 + (even + 16), 2 * c + (N_IN + 1))

            def apply_gain(i, half):
                pool.wait_ge(xn_ready, affine_count(i, half))
                nc.gpsimd.tensor_tensor(acc[:, i, :], acc[:, i, :], ln_g[:, :], ALU.mult).then_inc(gained_pool, 1)

            def add_bias(i, done):
                if i == 0:
                    pool.wait_ge(gained_pool, 2)
                else:
                    pool.wait_ge(gained, i)
                for h in range(2):
                    cols = slice(h * D_MODEL // 2, (h + 1) * D_MODEL // 2)
                    nc.gpsimd.tensor_tensor(acc[:, i, cols], acc[:, i, cols], ln_b[:, cols], ALU.add)\
                        .then_inc(done[i], 1)

            ff_pair = N_OUT // 2
            split_pairs(1, ff_pair - 1)
            split(1, odd + 16 * ff_pair, FF0 - 2)
            split(0, even + 16 * ff_pair, FF0 - 1, dst=spare_slot, used=0)
            split(0, even + 16 * (ff_pair + 1), FF0, used=FF0 - 2)
            split(1, odd + 16 * (ff_pair + 1), FF0 + 1, used=FF0)
            apply_gain(TT - 1, 0)
            pairs = (N_OUT + 12 * FF_GROUPS) // 2
            split_pairs(ff_pair + 1, pairs - 1)
            n_late = N_IN + 2 * (pairs - 1)
            for c, loads in ((0, odd + 16 * pairs), (1, even + 16 * pairs)):
                split(1 - c, loads, n_late + c, dst=(late_hi[c], late_lo[c]), used=n_late - 2)
            apply_gain(0, 1)
            for i in range(TT - 1):
                add_bias(i, y_ready)

        @block.tensor
        def _(pe):
            def passes(out_ap, stat_hi, stat_lo, mov_hi, mov_lo, first, last):
                nc.tensor.matmul(out_ap, stat_hi, mov_hi, start=first, stop=False)
                nc.tensor.matmul(out_ap, stat_hi, mov_lo, start=False, stop=False)
                return nc.tensor.matmul(out_ap, stat_lo, mov_hi, start=False, stop=last)

            pe.wait_ge(ident_ready, 1)

            def turn_x(i):
                pe.wait_ge(x_loaded[i], 16)
                for q in range(4):
                    g = 4 * i + q
                    if g >= 6:
                        pe.wait_ge(xt_lo, g - 5)
                    for k in range(4):
                        mm = nc.tensor.transpose(psum[:, 2 + g % 6, k * P:(k + 1) * P],
                                                 x_nat[:, i, (4 * q + k) * P:(4 * q + k + 1) * P], ident[:, :])
                    mm.then_inc(xt_done, 1)

            def feature_slab(bank, slot, ready, m=P):
                pe.wait_ge(split_done, ready)
                for k in range(KT):
                    cols = slice(k * m, (k + 1) * m)
                    mm = passes(psum[0:m, bank, :], w_hi[:, slot, cols], w_lo[:, slot, cols],
                                act_hi[:, k, :], act_lo[:, k, :], k == 0, k == KT - 1)
                return mm

            def proj_slab(n, m=P, free=None):
                parity = n % 2 if isinstance(n, int) else None
                if free is not None:
                    pe.wait_ge(bank_free[parity], free)
                feature_slab(parity, parity, n + 1, m).then_inc(slab_done, 1)

            def proj_pairs(first, count):
                with pe.Fori(0, count) as c:
                    for b in (1, 0):
                        pe.wait_ge(bank_free[b], c + ((first - 1) // 2 + (1 - b)))
                        feature_slab(b, b, 2 * c + (first + 2 - b)).then_inc(slab_done, 1)

            half_toks = SEQ // 2
            turn_x(0)
            turn_x(1)
            for half in range(2):
                pe.wait_ge(xt_lo, 8 * half + 8)
                toks = slice(half * half_toks, (half + 1) * half_toks)
                for k in range(KT):
                    if half == 0 and k % (KT // 2) == 0:
                        pe.wait_ge(half_lo, k // (KT // 2) + 1)
                    cols = slice(k * P, (k + 1) * P)
                    mm = passes(psum[:, 0, toks], w_hi[:, 0, cols], w_lo[:, 0, cols],
                                act_hi[:, k, toks], act_lo[:, k, toks], k == 0, k == KT - 1)
                    if half == 0 and k in (KT // 2 - 1, 3 * KT // 4 - 1):
                        turn_x(2 if k < KT // 2 else 3)
            mm.then_inc(slab_done, 1)
            proj_slab(1)
            proj_slab(2, free=1)
            proj_slab(3, free=1)
            proj_slab(N_IKWG, m=W_IKW + W_NG, free=2)

            pe.wait_ge(small_loaded, 16 * 10)
            for c in range(4):
                nc.tensor.transpose(psum[:, 7, c * VEC_ROWS:(c + 1) * VEC_ROWS],
                                    sel[0:VEC_ROWS, c * P:(c + 1) * P], ident[0:VEC_ROWS, 0:VEC_ROWS])
            nc.tensor.transpose(psum[:, 7, 4 * VEC_ROWS:4 * VEC_ROWS + 2 * CMP_BLOCK], pos_nat,
                                ident[0:2 * CMP_BLOCK, 0:2 * CMP_BLOCK]).then_inc(vec_t, 1)

            proj_pairs(N_CONV, 2)

            width = W_IKW + W_NG
            copied(pe, N_IKWG)
            for i in range(TT):
                mm = nc.tensor.transpose(psum[:, 6, i * width:(i + 1) * width],
                                         proj[0:width, S_IKWG, i * P:(i + 1) * P], ident[0:width, 0:width])
            mm.then_inc(iwg_t, 1)
            pe.wait_ge(ik_dup, 16)
            for e in range(3 * IDX_HEADS):
                i, h = e // IDX_HEADS + 1, e % IDX_HEADS
                if e >= 4:
                    pe.wait_ge(relu_done, e - 3)
                half = slice(64 * (h % 2), 64 * (h % 2) + 64)
                keys = proj[0:64, S_IKWG, 0:(i + 1) * P] if h % 2 == 0 else ik_high[:, 0:(i + 1) * P]
                nc.tensor.matmul(psum[:, 2 + e % 4, 0:(i + 1) * P], proj[half, S_IQ + h // 2, i * P:(i + 1) * P],
                                 keys, start=True, stop=True).then_inc(logit_done, 1)

            proj_pairs(N_CONV + 4, 11)
            pe.wait_ge(channel_sum, 1)
            nc.tensor.matmul(psum[:, 2, :], ones[:, :], tmp_a, start=True, stop=True).then_inc(mean_done, 1)
            proj_pairs(N_CONV + 26, 1)
            pe.wait_ge(channel_sum, 2)
            nc.tensor.matmul(psum[:, 3, :], ones[:, :], squares[:, 0, :], start=True, stop=True).then_inc(var_done, 1)

            for v, slot in enumerate((S_DV, S_SV, S_WV)):
                copied(pe, SLAB_OF[slot])
                for j in range(TT):
                    mm = nc.tensor.transpose(psum[:, 4 + v, j * P:(j + 1) * P], proj[:, slot, j * P:(j + 1) * P],
                                             ident[:, :])
                mm.then_inc(v_t, 1)

            copied(pe, N_IN - 1)
            copied(pe, N_IN - 2)
            for a in range(4):
                kv = a // 2
                if a < N_AUX:
                    slot = (N_IN + a) % 2
                    pe.wait_ge(raw_loaded[slot], 16 * (N_IN // 2 + (1 if slot == 0 else 0) + 1))
                    weights = raw[:, slot, :]
                else:
                    name = ("v0", "v1")[a - N_AUX]
                    pe.wait_ge(aux_loaded[name], 16)
                    weights = aux_weights[name]
                pe.wait_ge(blk_ready, 2 * kv + 2)
                for l in range(16):
                    row = 16 * (a % 2) + l
                    mm = nc.tensor.matmul(psum[0:N_CMP, kv, 0:P],
                                          blk[:, kv, row * CMP_BLOCK:row * CMP_BLOCK + N_CMP],
                                          weights[:, l * P:(l + 1) * P],
                                          start=row == 0, stop=row == CMP_BLOCK - 1)
                mm.then_inc(aux_used, 1)
            def mix_product(m):
                bank, chunk = MIX_BANKS[m], MIX_ORDER[m]
                if m >= 4:
                    pe.wait_ge(mix_split, m - 3)
                if chunk < 4:
                    pe.wait_ge(pool_in, chunk + 1)
                    nc.tensor.matmul(psum[:, bank, :], aux_weights["pool"][:, chunk * P:(chunk + 1) * P],
                                     proj[:, S_POOL + chunk, :], start=True, stop=True).then_inc(pool_done, 1)
                    return
                for c in range(4):
                    at = c * SEQ + (chunk - 4) * P
                    mm = nc.tensor.matmul(psum[:, bank, :], aux_weights["pw"][:, at:at + P], proj[:, CONV_OUT[c], :],
                                          start=c == 0, stop=c == 3)
                mm.then_inc(pw_done, 1)

            def scores(g):
                q, k, _, _ = UNITS[g // TT]
                i = g % TT
                if g >= 2:
                    pe.wait_ge(scored, g - 1)
                nc.tensor.matmul(psum[:, 2 + g % 2, 0:(i + 1) * P], proj[:, q, i * P:(i + 1) * P],
                                 proj[:, k, 0:(i + 1) * P], start=True, stop=True).then_inc(qk_done, 1)

            pe.wait_ge(aux_loaded["pool"], 16)
            pe.wait_ge(v_nat, 3)
            mix_product(0)
            mix_product(1)
            pe.wait_ge(centred, 4)
            pe.wait_ge(std_ready, 1)
            scores(0)
            scores(1)
            for kv in range(2):
                pe.wait_ge(cmp_pre_ready, kv + 1)
                mm = nc.tensor.matmul(psum[:, 0, P + kv * CMP_BLOCK:P + kv * CMP_BLOCK + N_CMP],
                                      cmp_pre[:, kv * P:(kv + 1) * P], ident[0:N_CMP, 0:N_CMP],
                                      start=True, stop=True)
            mm.then_inc(cmp_pre_t, 1)
            pe.wait_ge(aux_loaded["pw"], 16)
            pe.wait_ge(silu_ready, 4)
            mix_product(2)
            pe.wait_ge(gelu_ready, 2)
            nc.tensor.matmul(psum[:, 0, 64:64 + N_CMP], w2[:, 0, :], cmp_h[:, 0, :], start=True, stop=True)
            nc.tensor.matmul(psum[0:N_CMP, 1, P:2 * P], cmp_h[:, 1, :], w2[:, 1, :],
                             start=True, stop=True).then_inc(cmp2_done, 1)
            scores(2)
            scores(3)
            mix_product(3)
            scores(4)
            scores(5)
            mix_product(4)
            pe.wait_ge(cmp_kv, 2)
            for e in range(HEADS * TT):
                h, i = e // TT, e % TT
                mm = nc.tensor.matmul(psum[:, 0, e * N_CMP:(e + 1) * N_CMP],
                                      proj[:, S_NQ + h, i * P:(i + 1) * P], cmp_kT[:, :], start=True, stop=True)
            mm.then_inc(cmp_logit, 1)
            mix_product(5)
            mix_product(6)
            mix_product(7)

            def turn(g):
                i = g % TT
                pe.wait_ge(prob_ready, g + 1)
                if g < 2:
                    pe.wait_ge(mix_split, 6)
                else:
                    pe.wait_ge(pt_ready, g - 1)
                for j in range(i + 1):
                    mm = nc.tensor.transpose(psum[:, 4 + g % 2, j * P:(j + 1) * P],
                                             proj[:, T_SLOTS[g % RING], j * P:(j + 1) * P], ident[:, :])
                mm.then_inc(tr_done, 1)

            def weigh(u):
                v = UNITS[u][2]
                o = head_of(u)
                opens = u < HEADS or (u - HEADS) % 2 == 0
                pe.wait_ge(pt_ready, TT * (u + 1))
                if opens:
                    pe.wait_ge(mix_split, max(7 + o, 8))
                for j in range(TT):
                    mm = nc.tensor.matmul(psum[:, 6 + o % 2, j * P:SEQ], proj[:, v, j * P:(j + 1) * P],
                                          pt[:, u % 2, 4 * j * P:4 * j * P + (TT - j) * P],
                                          start=opens and j == 0, stop=u < HEADS and j == TT - 1)
                if u >= HEADS and closes_head(u):
                    pe.wait_ge(cmp_t_ready, HEADS)
                    mm = nc.tensor.matmul(psum[:, 6 + o % 2, :], cmp_v[:, :], cmp_pT[:, o - HEADS, :],
                                          start=False, stop=True)
                mm.then_inc(pv_done, 1)

            def ring(slab):
                return w_hi[:, slab % 2, :], w_lo[:, slab % 2, :]

            def out_tile(n, part, i, slab):
                toks, out_ap = slice(i * P, (i + 1) * P), psum[:, 4 * (n % 2) + i, :]
                w_h, w_l = slab
                for k in range(4):
                    t, cols = 4 * part + k, slice(k * SEQ, (k + 1) * SEQ)
                    first_mm, last_mm = t == 0, t == KT - 1
                    nc.tensor.matmul(out_ap, act_hi[:, t, toks], w_h[:, cols], start=first_mm, stop=False)
                    nc.tensor.matmul(out_ap, act_lo[:, t, toks], w_h[:, cols], start=False, stop=False)
                    mm = nc.tensor.matmul(out_ap, act_hi[:, t, toks], w_l[:, cols], start=False, stop=last_mm)
                return mm

            for g in range(TURN_LAG, N_TILES + WEIGH_LAG):
                i = g - (N_TILES + WEIGH_LAG - TT)
                if i >= 0:
                    if i == 0:
                        nc.tensor.sem_inc(tile_added, TILES0)
                        pe.wait_ge(cmp_t_ready, HEADS)
                        pe.wait_ge(scored, N_TILES)
                        pe.wait_ge(split_done, N_IN + 1)
                    mm = out_tile(0, 0, i, ring(N_IN))
                    if i == TT - 1:
                        mm.then_inc(slab_done, 1)
                if EARLY <= g < N_TILES:
                    scores(g)
                if TURN_LAG <= g < N_TILES + TURN_LAG:
                    turn(g - TURN_LAG)
                if g >= WEIGH_LAG and (g - WEIGH_LAG) % TT == TT - 1:
                    weigh((g - WEIGH_LAG) // TT)
                if g == HEADS * TT:
                    pe.wait_ge(cmp_prob, 1)
                    for h in range(HEADS):
                        if h >= 2:
                            pe.wait_ge(cmp_t_ready, h - 1)
                        for i in range(TT):
                            e = h * TT + i
                            mm = nc.tensor.matmul(psum[0:N_CMP, h % 2, i * P:(i + 1) * P],
                                                  cmp_p[:, e * N_CMP:(e + 1) * N_CMP], ident[:, :],
                                                  start=True, stop=True)
                        mm.then_inc(cmp_t, 1)

            for n in range(3):
                for part in range(1 if n == 0 else 0, 4):
                    slab = N_IN + 4 * n + part
                    pe.wait_ge(split_done, slab + 1)
                    if n == 0:
                        pe.wait_ge(mix_split, (8, 8, 12, 16)[part])
                    for i in range(TT):
                        if part == 0 and n >= 2:
                            pe.wait_ge(tile_added, TILES0 + 4 * (n - 2) + i + 1)
                        mm = out_tile(n, part, i, ring(slab))
                        if i == TT - 1:
                            mm.then_inc(slab_done, 1)
                        elif part == 3:
                            mm.then_inc(tile_done, 1)
            for part in range(2):
                slab = N_IN + 12 + part
                pe.wait_ge(split_done, slab + 1)
                for i in range(TT):
                    if part == 0:
                        pe.wait_ge(tile_added, TILES0 + 4 + i + 1)
                    mm = out_tile(3, part, i, ring(slab))
                mm.then_inc(slab_done, 1)

            def turn_x1(i):
                pe.wait_ge(x1_ready[i], 1)
                for q in range(4):
                    e = 4 * i + q
                    if e >= 6:
                        pe.wait_ge(x1_lo, e - 5)
                    elif e >= 4:
                        pe.wait_ge(tile_added, TILES0 + 12 + (e - 4) + 1)
                    for k in range(4):
                        mm = nc.tensor.transpose(psum[:, X1_BANKS[e], k * P:(k + 1) * P],
                                                 acc[:, i, (4 * q + k) * P:(4 * q + k + 1) * P], ident[:, :])
                    mm.then_inc(x1_t, 1)

            pe.wait_ge(split_done, FF0 - 1)
            for i in range(TT):
                if i == TT - 1:
                    turn_x1(0)
                for part, slab in ((2, ring(FF0 - 2)), (3, spare_slot)):
                    if part == 3:
                        pe.wait_ge(split_done, FF0)
                        if i == TT - 1:
                            turn_x1(1)
                    mm = out_tile(3, part, i, slab)
                    if i == TT - 1:
                        mm.then_inc(slab_done, 1)
                    elif part == 3:
                        mm.then_inc(tile_done, 1)

            def hidden(j, first, free=None):
                if free is not None:
                    pe.wait_ge(hid_ready, free)
                for u in range(2):
                    feature_slab(4 + 2 * (j % 2) + u, (u + 1) % 2, first + (u + 1)).then_inc(slab_done, 1)

            def down(first, group):
                pe.wait_ge(hid_lo, group * 4 + 4)
                for n in range(4):
                    slot = (n + 1) % 2
                    pe.wait_ge(split_done, first + (n + 1))
                    for i in range(TT):
                        pe.wait_ge(tile_added, group * 16 + (4 * n + TILES0 + 4 * 4 - 4 + i + 1))
                        for k in range(4):
                            toks, cols = slice(i * P, (i + 1) * P), slice(k * SEQ, (k + 1) * SEQ)
                            out_ap = psum[:, i, :]
                            nc.tensor.matmul(out_ap, h_hi[:, k, toks], w_hi[:, slot, cols], start=k == 0, stop=False)
                            nc.tensor.matmul(out_ap, h_lo[:, k, toks], w_hi[:, slot, cols], start=False, stop=False)
                            mm = nc.tensor.matmul(out_ap, h_hi[:, k, toks], w_lo[:, slot, cols],
                                                  start=False, stop=k == 3)
                        mm.then_inc(tile_done if i < TT - 1 else slab_done, 1)

            for half in range(2):
                pe.wait_ge(x1_lo, 8 * half + 8)
                toks = slice(half * half_toks, (half + 1) * half_toks)
                for v in range(2):
                    u = 1 - v if half == 0 else v
                    pe.wait_ge(split_done, FF0 + 1 + v)
                    for k in range(KT):
                        cols = slice(k * P, (k + 1) * P)
                        mm = passes(psum[:, 4 + u, toks], w_hi[:, 1 - u, cols], w_lo[:, 1 - u, cols],
                                    act_hi[:, k, toks], act_lo[:, k, toks], k == 0, k == KT - 1)
                        if half == 0 and v == 1 and k in (KT // 2 - 1, 3 * KT // 4 - 1):
                            turn_x1(2 if k < KT // 2 else 3)
                    if half == 1:
                        mm.then_inc(slab_done, 1)
            hidden(1, FF0 + 2)
            with pe.Fori(0, FF_GROUPS - 1) as g:
                hidden(2, g * 12 + (FF0 + 4), g * 4 + 1)
                hidden(3, g * 12 + (FF0 + 6), g * 4 + 2)
                hidden(4, g * 12 + (FF0 + 8), g * 4 + 3)
                down(g * 12 + (FF0 + 10), g)
                hidden(5, g * 12 + (FF0 + 14), g * 4 + 4)
            last = FF_GROUPS - 1
            hidden(2, 12 * last + FF0 + 4, 4 * last + 1)
            hidden(3, 12 * last + FF0 + 6, 4 * last + 2)
            first = 12 * last + FF0 + 8
            added = 16 * last + TILES0 + 16

            def token_tile(bank, i, w_h, w_l, ks):
                toks = slice(i * P, (i + 1) * P)
                for k in ks:
                    cols = slice(k * SEQ, (k + 1) * SEQ)
                    out_ap = psum[:, bank, :]
                    nc.tensor.matmul(out_ap, h_hi[:, k, toks], w_h[:, cols], start=k == 0, stop=False)
                    nc.tensor.matmul(out_ap, h_lo[:, k, toks], w_h[:, cols], start=False, stop=False)
                    mm = nc.tensor.matmul(out_ap, h_hi[:, k, toks], w_l[:, cols], start=False, stop=k == 3)
                return mm

            for n in range(2):
                slot = (n + 1) % 2
                pe.wait_ge(split_done, first + n + 1)
                for ks in ((0, 1, 2), (3,)):
                    pe.wait_ge(hid_lo, 4 * last + ks[-1] + 1)
                    for i in range(TT):
                        if ks[0] == 0:
                            pe.wait_ge(tile_added, added + 4 * n - 4 + i + 1)
                        mm = token_tile(i, i, w_hi[:, slot, :], w_lo[:, slot, :], ks)
                        if ks[0] == 3:
                            mm.then_inc(tile_done if i < TT - 1 else slab_done, 1)
            for i in range(TT):
                for n in (2, 3):
                    pe.wait_ge(split_done, first + n + 1)
                    if n == 2:
                        pe.wait_ge(tile_added, added + 4 + i + 1)
                    token_tile(4 * (n - 2) + i, i, late_hi[n - 2], late_lo[n - 2], range(4))\
                        .then_inc(tile_done if i < TT - 1 else slab_done, 1)

        @block.scalar
        def _(act):
            for i in range(TT):
                for q in range(4):
                    g = 4 * i + q
                    act.wait_ge(xt_done, g + 1)
                    nc.scalar.copy(act_hi[:, 4 * q:4 * q + 4, i * P:(i + 1) * P],
                                   psum[:, 2 + g % 6, :].rearrange("p (k s) -> p k s", k=4)).then_inc(xt_hi, 1)

            def copy_out(n, slot, scale=1.0, rows=P):
                act.wait_ge(slab_done, n + 1)
                nc.scalar.activation(proj[0:rows, slot, :], psum[0:rows, n % 2, :], ACT.Copy,
                                     scale=scale).then_inc(bank_free[n % 2], 1)

            def conv_gate(c):
                n = N_CONV + 2 * c
                act.wait_ge(slab_done, n + 1)
                nc.scalar.activation(proj[:, S_CONV + c, :], psum[:, n % 2, :], ACT.Sigmoid)\
                    .then_inc(bank_free[n % 2], 1)

            for n in range(4):
                copy_out(n, S_IQ + n)
            copy_out(N_IKWG, S_IKWG, rows=W_IKW + W_NG)
            copied(act, N_IKWG)
            nc.scalar.dma_start(ik_high, proj[0:64, S_IKWG, :]).then_inc(ik_dup, 16)
            conv_gate(0)
            conv_gate(1)
            act.wait_ge(iwg_ready, 2)
            nc.scalar.activation(iwg[:, :, W_IKW:], iwg[:, :, W_IKW:], ACT.Sigmoid).then_inc(gates_ready, 1)
            for e in range(3 * IDX_HEADS):
                w = (e // IDX_HEADS + 2) * P
                act.wait_ge(logit_done, e + 1)
                if e >= 6:
                    act.wait_ge(relu_used, e - 5)
                nc.scalar.activation(relu_ring[:, e % 6, 0:w], psum[:, 2 + e % 4, 0:w], ACT.Relu)\
                    .then_inc(relu_done, 1)
            conv_gate(2)
            conv_gate(3)
            for g in range(4):
                copy_out(N_POOL + g, S_POOL + g)
            for s in range(14):
                scale = 1.0
                if s < 4:
                    scale = ATTN_SCALE / SLOPES_DSA[s]
                elif 6 <= s < 10:
                    scale = ATTN_SCALE / SLOPES_NSA[s - 6]
                copy_out(N_QKV + s, S_DQ + s, scale)
            for c in range(4):
                act.wait_ge(centred, c + 1)
                nc.scalar.activation(squares[:, c, :], proj[:, CONV_OUT[c], :], ACT.Square).then_inc(squared, 1)
            for s in range(14, 16):
                copy_out(N_QKV + s, S_DQ + s)
            act.wait_ge(var_done, 1)
            act.wait_ge(conv_out, 4)
            nc.scalar.activation(rstd_conv, psum[:, 3, :], ACT.Sqrt, bias=eps[:, :]).then_inc(std_ready, 1)
            for c in range(4):
                act.wait_ge(normed, c + 1)
                nc.scalar.activation(proj[:, CONV_OUT[c], :], proj[:, CONV_OUT[c], :], ACT.Silu,
                                     bias=vecs[:, c, V_LB:V_LB + 1],
                                     scale=vecs[:, c, V_LG:V_LG + 1]).then_inc(silu_ready, 1)
            for v, slot in enumerate((S_DV, S_SV, S_WV)):
                act.wait_ge(v_t, v + 1)
                nc.scalar.copy(proj[:, slot, :], psum[:, 4 + v, :]).then_inc(v_nat, 1)
            for kv in range(2):
                act.wait_ge(aux_used, 2 * kv + 2)
                nc.scalar.copy(cmp_pre[:, kv * P:(kv + 1) * P], psum[0:N_CMP, kv, 0:P]).then_inc(cmp_pre_ready, 1)
            def mix_high(m):
                chunk, product = MIX_ORDER[m], psum[:, MIX_BANKS[m], :]
                if chunk < 4:
                    act.wait_ge(pool_done, chunk + 1)
                    nc.scalar.activation(act_hi[:, chunk, :], product, ACT.Copy,
                                         scale=vecs[:, chunk, V_PS:V_PS + 1]).then_inc(mix_hi, 1)
                else:
                    act.wait_ge(pw_done, chunk - 3)
                    nc.scalar.activation(act_hi[:, chunk, :], product, ACT.Identity,
                                         bias=vecs[:, chunk - 4, V_PB:V_PB + 1]).then_inc(mix_hi, 1)

            def exponentials(g):
                u, w = g // TT, (g % TT + 1) * P
                act.wait_ge(max_ready, g + 1)
                nc.scalar.activation(proj[:, T_SLOTS[g % RING], 0:w], proj[:, T_SLOTS[g % RING], 0:w], ACT.Exp,
                                     bias=neg_max[:, g % RING:g % RING + 1], scale=UNITS[u][3],
                                     accum_out=row_sum[:, g % RING:g % RING + 1]).then_inc(exp_done, 1)

            mix_high(0)
            mix_high(1)
            exponentials(0)
            exponentials(1)
            for kv in range(2):
                act.wait_ge(cmp_pre_t, 1)
                nc.scalar.activation(cmp_h[:, kv, :], psum[:, 0, P + kv * CMP_BLOCK:P + kv * CMP_BLOCK + N_CMP],
                                     ACT.Gelu_apprx_tanh).then_inc(gelu_ready, 1)
            mix_high(2)
            exponentials(2)
            exponentials(3)
            mix_high(3)
            exponentials(4)
            exponentials(5)
            mix_high(4)
            mix_high(5)
            mix_high(6)
            mix_high(7)
            act.wait_ge(cmp_shift, 1)
            for h in range(HEADS):
                cols = slice(h * TT * N_CMP, (h + 1) * TT * N_CMP)
                nc.scalar.activation(cmp_p[:, cols], cmp_p[:, cols], ACT.Exp, scale=SLOPES_NSA[h])\
                    .then_inc(cmp_exp, 1)

            def turned(g):
                u, i = g // TT, g % TT
                act.wait_ge(tr_done, g + 1)
                if i == 0 and u >= 2:
                    act.wait_ge(pv_done, u - 1)
                dst = pt[:, u % 2, :].rearrange("p (b s) -> p b s", s=P)[:, i:i + 3 * i + 1:3, :]
                nc.scalar.copy(dst, psum[:, 4 + g % 2, 0:(i + 1) * P].rearrange("p (b s) -> p b s", s=P))\
                    .then_inc(pt_ready, 1)

            def head_out(u):
                if closes_head(u):
                    o = head_of(u)
                    act.wait_ge(pv_done, u + 1)
                    nc.scalar.copy(act_hi[:, MIX_ORDER[8 + o], :], psum[:, 6 + o % 2, :]).then_inc(mix_hi, 1)

            for g in range(TURN_LAG, N_TILES + OUT_LAG):
                if TURN_LAG <= g < N_TILES + TURN_LAG:
                    turned(g - TURN_LAG)
                if EARLY <= g < N_TILES:
                    exponentials(g)
                if g >= OUT_LAG and (g - OUT_LAG) % TT == TT - 1:
                    head_out((g - OUT_LAG) // TT)

            def deviation(i, half):
                act.wait_ge(var_ready, TT * half + i + 1)
                nc.scalar.activation(std[:, i:i + 1], moments[:, i, 1:2], ACT.Sqrt, bias=eps[:, :])\
                    .then_inc(std_done, 1)

            def normal(i, half):
                act.wait_ge(rstd_ready, TT * half + i + 1)
                nc.scalar.activation(acc[:, i, :], acc[:, i, :], ACT.Identity, bias=shift[:, i:i + 1],
                                     scale=rstd[:, i:i + 1]).then_inc(xn_ready, 1)

            def x1_high(i):
                for q in range(4):
                    e = 4 * i + q
                    act.wait_ge(x1_t, e + 1)
                    nc.scalar.copy(act_hi[:, 4 * q:4 * q + 4, i * P:(i + 1) * P],
                                   psum[:, X1_BANKS[e], :].rearrange("p (k s) -> p k s", k=4)).then_inc(x1_hi, 1)

            deviation(0, 0)
            deviation(1, 0)
            x1_high(0)
            x1_high(1)
            deviation(2, 0)
            deviation(3, 0)
            normal(3, 0)
            x1_high(2)
            x1_high(3)
            for i in range(TT):
                nc.scalar.mul(acc[:, i, :], acc[:, i, :], ALPHA).then_inc(scaled, 1)

            def gate(j, q, slab):
                act.wait_ge(slab_done, slab + 1)
                if not isinstance(q, int) or q >= 2:
                    act.wait_ge(hid_ready, q - 1)
                nc.scalar.activation(silu_g[:, j % 2, :], psum[:, 4 + 2 * (j % 2), :], ACT.Silu).then_inc(silu_done, 1)

            def hidden_hi(j, q):
                act.wait_ge(hid_ready, q + 1)
                nc.scalar.copy(h_hi[:, j % 4, :], hid[:, j % 2, :]).then_inc(hid_hi, 1)

            gate(0, 0, FF0)
            hidden_hi(0, 0)
            gate(1, 1, FF0 + 2)
            hidden_hi(1, 1)
            with act.Fori(0, FF_GROUPS - 1) as g:
                for j in (2, 3):
                    gate(j, g * 4 + j, g * 12 + (FF0 + 2 * j))
                    hidden_hi(j, g * 4 + j)
                gate(4, g * 4 + 4, g * 12 + (FF0 + 8))
                act.wait_ge(slab_done, g * 12 + (FF0 + 14))
                hidden_hi(4, g * 4 + 4)
                gate(5, g * 4 + 5, g * 12 + (FF0 + 14))
                hidden_hi(5, g * 4 + 5)
            last = FF_GROUPS - 1
            for j in (2, 3):
                gate(j, 4 * last + j, 12 * last + FF0 + 2 * j)
                hidden_hi(j, 4 * last + j)
            for i in range(TT):
                deviation(i, 1)
                if i < TT - 1:
                    normal(i, 1)

        @block.vector
        def _(ve):
            chain = [0]

            def link(ins):
                chain[0] += 1
                ins.then_inc(dve, 1)
                ve.wait_ge(dve, chain[0])

            for i in range(TT):
                for q in range(4):
                    g = 4 * i + q
                    here = (slice(None), slice(4 * q, 4 * q + 4), slice(i * P, (i + 1) * P))
                    ve.wait_ge(xt_hi, g + 1)
                    nc.vector.tensor_tensor(act_lo[here], psum[:, 2 + g % 6, :].rearrange("p (k s) -> p k s", k=4),
                                            act_hi[here].bitcast(F32), ALU.subtract).then_inc(xt_lo, 1)
            ve.wait_ge(const_ready, 10)
            link(nc.vector.reciprocal(inv_count[:, :], inv_count[:, :]))
            ve.wait_ge(vec_t, 1)
            nc.vector.tensor_copy(vecs[:, :, :].rearrange("p c v -> p (c v)"), psum[:, 7, 0:4 * VEC_ROWS])\
                .then_inc(vec_ready, 1)
            nc.vector.tensor_copy(pos[:, :], psum[:, 7, 4 * VEC_ROWS:4 * VEC_ROWS + 2 * CMP_BLOCK])\
                .then_inc(vec_ready, 1)

            def conv_value(c):
                n = N_CONV + 2 * c + 1
                copied(ve, n - 1)
                ve.wait_ge(slab_done, n + 1)
                nc.vector.tensor_tensor(proj[:, S_CONV + c, :], psum[:, n % 2, :], proj[:, S_CONV + c, :],
                                        ALU.mult).then_inc(bank_free[n % 2], 1)

            conv_value(0)
            conv_value(1)
            ve.wait_ge(iwg_t, 1)
            nc.vector.tensor_copy(iwg[:, :, :].rearrange("p i w -> p (i w)"), psum[:, 6, 0:TT * (W_IKW + W_NG)])\
                .then_inc(iwg_ready, 1)
            ve.wait_ge(iwg_ready, 1)
            nc.vector.tensor_scalar(iwg[:, :, IDX_DIM:W_IKW], iwg[:, :, IDX_DIM:W_IKW], IDX_SCALE, None, ALU.mult)\
                .then_inc(iwg_ready, 1)
            ve.wait_ge(iwg_ready, 2)
            for e in range(3 * IDX_HEADS):
                i, h = e // IDX_HEADS + 1, e % IDX_HEADS
                w = (i + 1) * P
                score = sel[:, SEL_OFF[i]:SEL_OFF[i] + w]
                weight = iwg[:, i, IDX_DIM + h:IDX_DIM + h + 1]
                ve.wait_ge(relu_done, e + 1)
                if h > 0:
                    ve.wait_ge(relu_used, e)
                    nc.vector.scalar_tensor_tensor(out=score, in0=relu_ring[:, e % 6, 0:w], scalar=weight,
                                                   in1=score, op0=ALU.mult, op1=ALU.add).then_inc(relu_used, 1)
                else:
                    nc.vector.tensor_scalar(score, relu_ring[:, e % 6, 0:w], weight, None, ALU.mult)\
                        .then_inc(relu_used, 1)
            conv_value(2)
            conv_value(3)
            ve.wait_ge(relu_used, 3 * IDX_HEADS)
            for i in range(1, TT):
                w = (i + 1) * P
                score = sel[:, SEL_OFF[i]:SEL_OFF[i] + w]
                diagonal = sel[:, SEL_OFF[i] + i * P:SEL_OFF[i] + w]
                link(nc.vector.tensor_tensor(diagonal, diagonal, later[:, :], ALU.add))
                for _ in range(TOPK // 8):
                    link(nc.vector.max(out=top8[:, :], in_=score))
                    link(nc.vector.match_replace(out=score, in_to_replace=top8[:, :], in_values=score,
                                                 imm_value=PICKED))
                link(nc.vector.tensor_scalar(score, score, 0.5 * PICKED, MASKED, ALU.is_gt, ALU.mult))
                link(nc.vector.tensor_tensor(score, score, dist[:, SEQ - w:SEQ], ALU.add))

            for c in range(4):
                h_in, y = proj[:, S_CONV + c, :], proj[:, CONV_OUT[c], :]
                copied(ve, N_CONV + 2 * c + 1)
                if c > 0:
                    ve.wait_ge(conv_out, c)
                tap = CONV_WIDTH - 1
                link(nc.vector.tensor_scalar(y, h_in, vecs[:, c, tap:tap + 1], vecs[:, c, V_CB:V_CB + 1],
                                             ALU.mult, ALU.add))
                for tap in range(CONV_WIDTH - 1):
                    s = CONV_WIDTH - 1 - tap
                    ins = nc.vector.scalar_tensor_tensor(out=y[:, s:], in0=h_in[:, 0:SEQ - s],
                                                         scalar=vecs[:, c, tap:tap + 1], in1=y[:, s:],
                                                         op0=ALU.mult, op1=ALU.add)
                    if tap < CONV_WIDTH - 2:
                        link(ins)
                ins.then_inc(conv_out, 1)

            for g in range(4):
                u = proj[:, S_POOL + g, :]
                copied(ve, N_POOL + g)
                if g > 0:
                    ve.wait_ge(pool_in, g)
                src, bufs = u, [tmp_a, tmp_b]
                for s in range(g + 1):
                    step, dst = 2 ** s, bufs[s % 2]
                    nc.vector.tensor_copy(dst[:, 0:step], src[:, 0:step])
                    link(nc.vector.tensor_tensor(dst[:, step:], src[:, step:], src[:, 0:SEQ - step], ALU.add))
                    src = dst
                win = 2 ** (g + 1)
                head = bufs[(g + 1) % 2][:, 0:win - 1]
                link(nc.vector.tensor_tensor(head, src[:, 0:win - 1], inv_count[:, 0:win - 1], ALU.mult))
                link(nc.vector.tensor_tensor(u[:, 0:win - 1], head, u[:, 0:win - 1], ALU.subtract))
                nc.vector.scalar_tensor_tensor(out=u[:, win - 1:], in0=src[:, win - 1:], scalar=1.0 / win,
                                               in1=u[:, win - 1:], op0=ALU.mult, op1=ALU.subtract)\
                    .then_inc(pool_in, 1)

            ve.wait_ge(pool_in, 4)
            ve.wait_ge(conv_out, 4)
            link(nc.vector.tensor_tensor(tmp_a, proj[:, CONV_OUT[0], :], proj[:, CONV_OUT[1], :], ALU.add))
            link(nc.vector.tensor_tensor(tmp_a, tmp_a, proj[:, CONV_OUT[2], :], ALU.add))
            nc.vector.tensor_tensor(tmp_a, tmp_a, proj[:, CONV_OUT[3], :], ALU.add).then_inc(channel_sum, 1)
            ve.wait_ge(mean_done, 1)
            for c in range(4):
                y = proj[:, CONV_OUT[c], :]
                nc.vector.tensor_tensor(y, y, psum[:, 2, :], ALU.subtract).then_inc(centred, 1)
            for c in range(1, 4):
                ve.wait_ge(squared, c + 1)
                ins = nc.vector.tensor_tensor(squares[:, 0, :], squares[:, 0, :], squares[:, c, :], ALU.add)
                if c < 3:
                    link(ins)
            ins.then_inc(channel_sum, 1)
            ve.wait_ge(pool_in, 4)
            ve.wait_ge(vec_ready, 2)
            for kv, slot in enumerate((S_CK, S_CV)):
                copied(ve, SLAB_OF[slot])
                src = proj[:, slot, :].rearrange("p (c b) -> p b c", b=CMP_STRIDE)
                dst = blk[:, kv, :].rearrange("p (l c) -> p l c", c=CMP_BLOCK)
                for a in range(2):
                    rows = slice(CMP_STRIDE * a, CMP_STRIDE * (a + 1))
                    at = pos[:, kv * CMP_BLOCK + CMP_STRIDE * a:kv * CMP_BLOCK + CMP_STRIDE * (a + 1)]
                    nc.vector.tensor_tensor(dst[:, rows, 0:N_CMP], src[:, :, a:a + N_CMP],
                                            at.unsqueeze(2).to_broadcast([P, CMP_STRIDE, N_CMP]),
                                            ALU.add).then_inc(blk_ready, 1)

            ve.wait_ge(std_ready, 1)
            link(nc.vector.reciprocal(rstd_conv, rstd_conv))
            ve.wait_ge(squared, 4)
            ve.wait_ge(centred, 4)
            for c in range(4):
                y = proj[:, CONV_OUT[c], :]
                nc.vector.tensor_tensor(y, y, rstd_conv, ALU.mult).then_inc(normed, 1)

            def mix_lo(m, bank, **affine):
                lo, hi = act_lo[:, MIX_ORDER[m], :], act_hi[:, MIX_ORDER[m], :].bitcast(F32)
                ve.wait_ge(mix_hi, m + 1)
                if affine:
                    ins = nc.vector.scalar_tensor_tensor(out=lo, in0=psum[:, bank, :], in1=hi, op1=ALU.subtract,
                                                         **affine)
                else:
                    ins = nc.vector.tensor_tensor(lo, psum[:, bank, :], hi, ALU.subtract)
                ins.then_inc(mix_split, 1)

            def branch_lo(m):
                chunk = MIX_ORDER[m]
                if chunk < 4:
                    mix_lo(m, MIX_BANKS[m], scalar=vecs[:, chunk, V_PS:V_PS + 1], op0=ALU.mult)
                else:
                    mix_lo(m, MIX_BANKS[m], scalar=vecs[:, chunk - 4, V_PB:V_PB + 1], op0=ALU.add)

            def add_distance(g):
                u, i = g // TT, g % TT
                w = (i + 1) * P
                if u < HEADS and i > 0:
                    d = sel[:, SEL_OFF[i]:SEL_OFF[i] + w]
                else:
                    d = dist[:, SEQ - w:SEQ]
                ve.wait_ge(qk_done, g + 1)
                if g >= RING:
                    ve.wait_ge(tr_done, g - RING + 1)
                nc.vector.tensor_tensor_reduce(out=proj[:, T_SLOTS[g % RING], 0:w], in0=psum[:, 2 + g % 2, 0:w], in1=d,
                                               scale=1.0, scalar=PICKED, op0=ALU.add, op1=ALU.max,
                                               accum_out=row_max[:, g % RING:g % RING + 1]).then_inc(scored, 1)
                ve.wait_ge(scored, g + 1)
                nc.vector.tensor_scalar(neg_max[:, g % RING:g % RING + 1], row_max[:, g % RING:g % RING + 1], 0.1 * MASKED,
                                        -UNITS[u][3], ALU.max, ALU.mult).then_inc(max_ready, 1)

            def inverse(g):
                inv = row_inv[:, g % RING:g % RING + 1]
                ve.wait_ge(exp_done, g + 1)
                link(nc.vector.tensor_scalar(inv, row_sum[:, g % RING:g % RING + 1], 1e-30, None, ALU.max))
                nc.vector.reciprocal(inv, inv).then_inc(inv_ready, 1)

            branch_lo(0)
            branch_lo(1)
            add_distance(0)
            add_distance(1)
            inverse(0)
            inverse(1)
            branch_lo(2)
            ve.wait_ge(cmp2_done, 1)
            nc.vector.tensor_copy(cmp_kT[:, :], psum[:, 0, 64:64 + N_CMP]).then_inc(cmp_kv, 1)
            nc.vector.tensor_copy(cmp_v[:, :], psum[0:N_CMP, 1, P:2 * P]).then_inc(cmp_kv, 1)
            add_distance(2)
            add_distance(3)
            inverse(2)
            inverse(3)
            branch_lo(3)
            add_distance(4)
            add_distance(5)
            inverse(4)
            branch_lo(4)

            flat = cmp_p[:, :].rearrange("p (h e) -> p h e", h=HEADS)
            rows = cmp_p[:, :].rearrange("p (e c) -> p e c", c=N_CMP)
            ve.wait_ge(cmp_logit, 1)
            link(nc.vector.tensor_tensor(flat, psum[:, 0, 0:16 * N_CMP].rearrange("p (h e) -> p h e", h=HEADS),
                                         cmp_dist[:, :].unsqueeze(1).to_broadcast([P, HEADS, TT * N_CMP]), ALU.add))
            link(nc.vector.tensor_reduce(cmp_m[:, :], rows, AX.X, ALU.max))
            link(nc.vector.tensor_scalar(cmp_m[:, :], cmp_m[:, :], 0.1 * MASKED, None, ALU.max))
            nc.vector.tensor_tensor(rows, rows, cmp_m[:, :].unsqueeze(2).to_broadcast([P, 16, N_CMP]), ALU.subtract)\
                .then_inc(cmp_shift, 1)
            for m in range(5, 8):
                branch_lo(m)

            def compressed_probs():
                ve.wait_ge(cmp_exp, HEADS)
                link(nc.vector.tensor_reduce(cmp_r[:, :], rows, AX.X, ALU.add))
                link(nc.vector.tensor_scalar(cmp_r[:, :], cmp_r[:, :], 1e-30, None, ALU.max))
                link(nc.vector.reciprocal(cmp_r[:, :], cmp_r[:, :]))
                gates = iwg[:, :, W_IKW:].rearrange("p i (h b) -> p h i b", b=3)[:, :, :, 0]
                r = cmp_r[:, :].rearrange("p (h i) -> p h i", h=HEADS)
                link(nc.vector.tensor_tensor(r, r, gates, ALU.mult))
                nc.vector.tensor_tensor(rows, rows, cmp_r[:, :].unsqueeze(2).to_broadcast([P, 16, N_CMP]),
                                        ALU.mult).then_inc(cmp_prob, 1)

            ve.wait_ge(gates_ready, 1)
            for g in range(EARLY, N_TILES + LO_LAG):
                if g < N_TILES:
                    add_distance(g)
                if 1 <= g <= N_TILES:
                    inverse(g - 1)
                if g >= LO_LAG and (g - LO_LAG) % TT == TT - 1:
                    u = (g - LO_LAG) // TT
                    if closes_head(u):
                        mix_lo(8 + head_of(u), 6 + head_of(u) % 2)
                if g == WEIGH_LAG + TT - 1:
                    compressed_probs()
                if g == HEADS * TT:
                    for h in range(HEADS):
                        ve.wait_ge(cmp_t, h + 1)
                        nc.vector.tensor_copy(cmp_pT[:, h, :], psum[0:N_CMP, h % 2, :]).then_inc(cmp_t_ready, 1)

            def add_out(n, i):
                cols = acc[:, i, n * SEQ:(n + 1) * SEQ]
                tile_ready(ve, n, N_IN + 4 * n + 3, i)
                nc.vector.scalar_tensor_tensor(out=cols, in0=cols, scalar=ALPHA, in1=psum[:, 4 * (n % 2) + i, :],
                                               op0=ALU.mult, op1=ALU.add).then_inc(tile_added, 1)
                ve.wait_ge(tile_added, TILES0 + 4 * n + i + 1)
                link(nc.vector.bn_stats(stats[:, i, n, :], cols))

            def add_down(group, slab, n, i, with_stats=False):
                cols = acc[:, i, n * SEQ:(n + 1) * SEQ]
                tile_ready(ve, group * 4 + (4 + n), slab + n, i)
                nc.vector.tensor_tensor(cols, cols, psum[:, i, :], ALU.add).then_inc(tile_added, 1)
                if with_stats:
                    ve.wait_ge(tile_added, group * 16 + (TILES0 + 16 + 4 * n + i + 1))
                    link(nc.vector.bn_stats(stats[:, i, n, :], cols))

            def moments_of(i):
                nc.vector.bn_aggr(moments[:, i, :], stats[:, i, :, :].rearrange("p n s -> p (n s)"))\
                    .then_inc(var_ready, 1)

            def rstd_of(i, half):
                ve.wait_ge(std_done, TT * half + i + 1)
                link(nc.vector.reciprocal(rstd[:, i:i + 1], std[:, i:i + 1]))
                nc.vector.scalar_tensor_tensor(out=shift[:, i:i + 1], in0=moments[:, i, 0:1], scalar=-1.0,
                                               in1=rstd[:, i:i + 1], op0=ALU.mult, op1=ALU.mult)\
                    .then_inc(rstd_ready, 1)

            def gain(i, half):
                ve.wait_ge(xn_ready, affine_count(i, half))
                nc.vector.tensor_tensor(acc[:, i, :], acc[:, i, :], ln_g[:, :], ALU.mult).then_inc(gained, 1)

            def bias(i, done):
                ve.wait_ge(gained_pool, 1)
                nc.vector.tensor_tensor(acc[:, i, :], acc[:, i, :], ln_b[:, :], ALU.add).then_inc(done[i], 1)

            def centre(i, cols, count):
                ve.wait_ge(var_ready, count)
                y = acc[:, i, cols]
                link(nc.vector.scalar_tensor_tensor(out=y, in0=y, scalar=moments[:, i, 0:1], in1=ln_g[:, cols],
                                                    op0=ALU.subtract, op1=ALU.mult))

            def scale_and_shift(i, cols, count, done):
                ve.wait_ge(rstd_ready, count)
                y = acc[:, i, cols]
                nc.vector.scalar_tensor_tensor(out=y, in0=y, scalar=rstd[:, i:i + 1], in1=ln_b[:, cols],
                                               op0=ALU.mult, op1=ALU.add).then_inc(done[i], 1)

            def x1_split(i):
                for q in range(4):
                    e = 4 * i + q
                    here = (slice(None), slice(4 * q, 4 * q + 4), slice(i * P, (i + 1) * P))
                    ve.wait_ge(x1_hi, e + 1)
                    nc.vector.tensor_tensor(act_lo[here],
                                            psum[:, X1_BANKS[e], :].rearrange("p (k s) -> p k s", k=4),
                                            act_hi[here].bitcast(F32), ALU.subtract).then_inc(x1_lo, 1)

            ve.wait_ge(resid_loaded, 16)
            for n in range(3):
                for i in range(TT):
                    add_out(n, i)
            ve.wait_ge(ln_loaded, 32)
            for i in range(2):
                add_out(3, i)
                moments_of(i)
                centre(i, slice(0, D_MODEL), i + 1)
                rstd_of(i, 0)
                scale_and_shift(i, slice(0, D_MODEL), i + 1, x1_ready)
            x1_split(0)
            add_out(3, 2)
            moments_of(2)
            x1_split(1)
            add_out(3, 3)
            moments_of(3)
            rstd_of(2, 0)
            rstd_of(3, 0)
            centre(2, slice(0, D_MODEL), 3)
            scale_and_shift(2, slice(0, D_MODEL), 3, x1_ready)
            bias(3, x1_ready)
            x1_split(2)
            x1_split(3)

            def hidden(j, q, slab):
                ve.wait_ge(slab_done, slab + 1)
                ve.wait_ge(silu_done, q + 1)
                if not isinstance(q, int) or q >= 2:
                    ve.wait_ge(hid_lo, q - 1)
                nc.vector.tensor_tensor(hid[:, j % 2, :], psum[:, 5 + 2 * (j % 2), :], silu_g[:, j % 2, :],
                                        ALU.mult).then_inc(hid_ready, 1)

            def hidden_lo(j, q):
                ve.wait_ge(hid_hi, q + 1)
                nc.vector.tensor_tensor(h_lo[:, j % 4, :], hid[:, j % 2, :], h_hi[:, j % 4, :].bitcast(F32),
                                        ALU.subtract).then_inc(hid_lo, 1)

            hidden(0, 0, FF0 + 1)
            hidden_lo(0, 0)
            hidden(1, 1, FF0 + 3)
            hidden_lo(1, 1)
            ve.wait_ge(scaled, TT)
            with ve.Fori(0, FF_GROUPS - 1) as g:
                for j in (2, 3):
                    hidden(j, g * 4 + j, g * 12 + (FF0 + 2 * j + 1))
                    hidden_lo(j, g * 4 + j)
                hidden(4, g * 4 + 4, g * 12 + (FF0 + 9))
                for n in range(4):
                    for i in range(TT):
                        add_down(g, g * 12 + (FF0 + 10), n, i)
                hidden_lo(4, g * 4 + 4)
                hidden(5, g * 4 + 5, g * 12 + (FF0 + 15))
                hidden_lo(5, g * 4 + 5)
            last = FF_GROUPS - 1
            for j in (2, 3):
                hidden(j, 4 * last + j, 12 * last + FF0 + 2 * j + 1)
                hidden_lo(j, 4 * last + j)
            slab = 12 * last + FF0 + 8
            for n in range(2):
                for i in range(TT):
                    add_down(last, slab, n, i, with_stats=True)
            ve.wait_ge(ln_loaded, 64)
            finished = (4 + 4 * last + 2) * (TT - 1)
            added = 16 * last + TILES0 + 16 + 8

            def add_late(i, n):
                if i < TT - 1:
                    ve.wait_ge(tile_done, finished + 2 * i + (n - 2) + 1)
                else:
                    ve.wait_ge(slab_done, slab + n + 1)
                cols = acc[:, i, n * SEQ:(n + 1) * SEQ]
                nc.vector.tensor_tensor(cols, cols, psum[:, 4 * (n - 2) + i, :], ALU.add).then_inc(tile_added, 1)
                ve.wait_ge(tile_added, added + 2 * i + (n - 2) + 1)
                link(nc.vector.bn_stats(stats[:, i, n, :], cols))

            add_late(0, 2)
            for i in range(TT):
                add_late(i, 3)
                moments_of(i)
                if i == TT - 1:
                    gain(i - 1, 1)
                rstd_of(i, 1)
                if i < TT - 1:
                    add_late(i + 1, 2)
                if i == 1:
                    gain(i, 1)
            for n in range(4):
                cols = slice(n * SEQ, (n + 1) * SEQ)
                centre(TT - 1, cols, 2 * TT)
                scale_and_shift(TT - 1, cols, 2 * TT, y_ready)


_INS = ["x", "w_in", "w_out", "pool_w", "pool_scale", "conv_w", "conv_b", "conv_ln_g", "conv_ln_b",
        "conv_pw_w", "conv_pw_b", "cmp_pos_k", "cmp_pos_v", "cmp_k_w1", "cmp_k_w2", "cmp_v_w1",
        "cmp_v_w2", "ln1_g", "ln1_b", "ln2_g", "ln2_b", "w_gate_up", "w_down"]


def kernel(**inputs):
    import concourse.bacc as bacc
    from concourse.bass_utils import run_bass_kernel_spmd

    nc = bacc.Bacc("TRN2", target_bir_lowering=False, num_devices=1)
    arrays, args = {}, []
    for name in _INS:
        a = np.ascontiguousarray(inputs[name])
        arrays[f"in_{name}"] = a
        args.append(nc.dram_tensor(f"in_{name}", a.shape, mybir.dt.from_np(a.dtype), kind="ExternalInput").ap())
    out = nc.dram_tensor("out", (1, SEQ, D_MODEL), F32, kind="ExternalOutput").ap()
    build(nc, *args, out)
    result = run_bass_kernel_spmd(nc, [arrays], core_ids=[0])
    return result.results[0]["out"]
```
